# Optimizing a Trainium2 kernel written in Bass

```python
import jax, jax.numpy as jnp
from jax import lax
import numpy as np

D_MODEL = 1024
BATCH = 1
SEQ = 512
DEPTH = 1
DEC_BATCH = 1
DEC_SEQ = 64
PAST_LEN = 256

CHUNK = 64
Q_BLOCK = 128
EPS = 1e-6
M_HEADS = 4
M_HEAD_DIM = 128
M_WIDTH = M_HEADS * M_HEAD_DIM
A_HEADS = 8
A_NOPE = 64
A_ROPE = 32
A_V = 64
A_WIDTH = A_HEADS * A_V
Q_LORA = 384
KV_LORA = 256
ROPE_THETA = 10000.0
A_SCALE = (A_NOPE + A_ROPE) ** -0.5
MIX_WIDTH = M_WIDTH + A_WIDTH
IN_WIDTH = 4 * M_WIDTH + 2 * M_HEADS + Q_LORA + KV_LORA + A_ROPE
D_FF = 2816

kernel_name = 'hybrid_mlstm_mla_stream_step'

def rms_norm(x, g):
    x32 = x.astype(jnp.float32)
    y = x32 * lax.rsqrt(jnp.mean(x32 * x32, axis=-1, keepdims=True) + EPS)
    return (y * g.astype(jnp.float32)).astype(x.dtype)

def swiglu_half(x, pre_g, w_gate, w_up, w_down, post_g):
    h = rms_norm(x, pre_g)
    u = jax.nn.silu(h @ w_gate) * (h @ w_up)
    return x + 0.5 * rms_norm(u @ w_down, post_g)

def rope(x, pos):
    half = A_ROPE // 2
    freq = ROPE_THETA ** (-jnp.arange(half, dtype=jnp.float32) / half)
    ang = pos.astype(jnp.float32)[:, None] * freq[None, :]
    shape = (ang.shape[0],) + (1,) * (x.ndim - 3) + (half,)
    cos = jnp.cos(ang).reshape(shape)
    sin = jnp.sin(ang).reshape(shape)
    x32 = x.astype(jnp.float32)
    x1, x2 = x32[..., :half], x32[..., half:]
    return jnp.concatenate([x1 * cos - x2 * sin, x2 * cos + x1 * sin], axis=-1).astype(x.dtype)

def mixer_projections(h, pos, w_in, b_igate, b_fgate, q_a_g, w_uq, kv_a_g):
    B, S = h.shape[:2]
    sizes = (M_WIDTH, M_WIDTH, M_WIDTH, M_WIDTH, M_HEADS, M_HEADS, Q_LORA, KV_LORA, A_ROPE)
    idx = [int(i) for i in np.cumsum(sizes)[:-1]]
    mq, mk, mv, mo, mi, mf, aq, akv, ar = jnp.split(h @ w_in, idx, axis=-1)
    heads = lambda a: a.reshape(B, S, M_HEADS, M_HEAD_DIM)
    mq, mv, mo = heads(mq), heads(mv), heads(mo)
    mk = heads(mk) * (M_HEAD_DIM ** -0.5)
    ig = (mi + b_igate).astype(jnp.float32)
    lf = jax.nn.log_sigmoid((mf + b_fgate).astype(jnp.float32))
    q = (rms_norm(aq, q_a_g) @ w_uq).reshape(B, S, A_HEADS, A_NOPE + A_ROPE)
    q_nope, q_rope = q[..., :A_NOPE], rope(q[..., A_NOPE:], pos)
    c_kv = rms_norm(akv, kv_a_g)
    k_rope = rope(ar, pos)
    return mo, (mq, mk, mv, ig, lf, q_nope, q_rope, c_kv, k_rope)

def mlstm_chunk(carry, inp):
    C, n, m = carry
    q, k, v, ig, lf = inp
    q, k, v = q.astype(jnp.float32), k.astype(jnp.float32), v.astype(jnp.float32)
    ig = jnp.moveaxis(ig.astype(jnp.float32), 1, 2)
    lf = jnp.moveaxis(lf.astype(jnp.float32), 1, 2)
    L = q.shape[1]
    b = jnp.cumsum(lf, axis=-1)
    causal = jnp.tril(jnp.ones((L, L), dtype=bool))
    log_d = jnp.where(causal, b[..., :, None] - b[..., None, :] + ig[..., None, :], -jnp.inf)
    log_carry = b + m[..., None]
    m_t = jnp.maximum(log_carry, jnp.max(log_d, axis=-1))
    d = jnp.exp(log_d - m_t[..., None])
    w_carry = jnp.exp(log_carry - m_t)
    s = jnp.einsum('bthd,bshd->bhts', q, k) * d
    num = jnp.einsum('bhts,bshd->bhtd', s, v) + w_carry[..., None] * jnp.einsum('bhvk,bthk->bhtv', C, q)
    den = jnp.sum(s, axis=-1) + w_carry * jnp.einsum('bhk,bthk->bht', n, q)
    den = jnp.maximum(jnp.abs(den), jnp.exp(-m_t))
    h = jnp.moveaxis(num / den[..., None], 1, 2)
    m_new = m_t[..., -1]
    w_state = jnp.exp(b[..., -1] + m - m_new)
    w_row = jnp.exp(b[..., -1:] - b + ig - m_new[..., None])
    C_new = w_state[..., None, None] * C + jnp.einsum('bhs,bshv,bshk->bhvk', w_row, v, k)
    n_new = w_state[..., None] * n + jnp.einsum('bhs,bshk->bhk', w_row, k)
    return (C_new, n_new, m_new), h

def mla_expand(c_kv, w_ukv):
    B, T = c_kv.shape[:2]
    kv = (c_kv @ w_ukv).reshape(B, T, A_HEADS, A_NOPE + A_V)
    return kv[..., :A_NOPE], kv[..., A_NOPE:]

def mla_attend(q_nope, q_rope, k_nope, k_rope, v, q_pos, k_pos):
    s = jnp.einsum('bqhd,bkhd->bhqk', q_nope, k_nope) + jnp.einsum('bqhr,bkr->bhqk', q_rope, k_rope)
    s = s.astype(jnp.float32) * A_SCALE
    visible = (q_pos[:, None] // CHUNK) >= (k_pos[None, :] // CHUNK)
    s = jnp.where(visible, s, -jnp.inf)
    p = jax.nn.softmax(s, axis=-1).astype(v.dtype)
    return jnp.einsum('bhqk,bkhd->bqhd', p, v)

def prompt_token_mix(proj, pos, w_ukv):
    mq, mk, mv, ig, lf, q_nope, q_rope, c_kv, k_rope = proj
    B, S = mq.shape[:2]
    nc = S // CHUNK
    to_chunks = lambda a: jnp.moveaxis(a.reshape((B, nc, CHUNK) + a.shape[2:]), 1, 0)
    init = (jnp.zeros((B, M_HEADS, M_HEAD_DIM, M_HEAD_DIM), jnp.float32),
            jnp.zeros((B, M_HEADS, M_HEAD_DIM), jnp.float32),
            jnp.zeros((B, M_HEADS), jnp.float32))
    (C, n, m), hs = lax.scan(mlstm_chunk, init, (to_chunks(mq), to_chunks(mk), to_chunks(mv), to_chunks(ig), to_chunks(lf)))
    h_m = jnp.moveaxis(hs, 0, 1).reshape(B, S, M_HEADS, M_HEAD_DIM)
    k_nope, v = mla_expand(c_kv, w_ukv)
    nb = S // Q_BLOCK
    to_qblocks = lambda a: jnp.moveaxis(a.reshape((B, nb, Q_BLOCK) + a.shape[2:]), 1, 0)
    attn_blocks = lax.map(lambda blk: mla_attend(blk[0], blk[1], k_nope, k_rope, v, blk[2], pos),
                          (to_qblocks(q_nope), to_qblocks(q_rope), pos.reshape(nb, Q_BLOCK)))
    attn = jnp.moveaxis(attn_blocks, 0, 1).reshape(B, S, A_HEADS, A_V)
    return h_m, attn, (c_kv, k_rope, C, n, m)

def sample_token_mix(proj, pos, w_ukv, cache_kv_latent, cache_k_rope, state_C, state_n, state_m):
    mq, mk, mv, ig, lf, q_nope, q_rope, c_kv, k_rope = proj
    carry = (state_C.astype(jnp.float32), state_n.astype(jnp.float32), state_m.astype(jnp.float32))
    (C, n, m), h_m = mlstm_chunk(carry, (mq, mk, mv, ig, lf))
    c_all = jnp.concatenate([cache_kv_latent.astype(c_kv.dtype), c_kv], axis=1)
    kr_all = jnp.concatenate([cache_k_rope.astype(k_rope.dtype), k_rope], axis=1)
    k_nope, v = mla_expand(c_all, w_ukv)
    k_pos = jnp.arange(c_all.shape[1])
    attn = mla_attend(q_nope, q_rope, k_nope, kr_all, v, pos, k_pos)
    return h_m, attn, (c_kv, k_rope, C, n, m)

def run_layer(x, pos, token_mix, ff1, mix, ff2):
    x = swiglu_half(x, *ff1)
    mix_pre_g, w_in, b_igate, b_fgate, q_a_g, w_uq, kv_a_g, m_head_g, w_out, mix_post_g = mix
    mo, proj = mixer_projections(rms_norm(x, mix_pre_g), pos, w_in, b_igate, b_fgate, q_a_g, w_uq, kv_a_g)
    h_m, attn, new_state = token_mix(proj)
    B, S = x.shape[:2]
    h_m = rms_norm(h_m.astype(x.dtype), m_head_g) * jax.nn.sigmoid(mo)
    merged = jnp.concatenate([h_m.reshape(B, S, M_WIDTH), attn.reshape(B, S, A_WIDTH)], axis=-1)
    x = x + rms_norm(merged @ w_out, mix_post_g)
    x = swiglu_half(x, *ff2)
    return x, new_state

def setup_inputs(seed: int = 0) -> dict:
    key = jax.random.key(seed)
    ks = iter(jax.random.split(key, 40))
    f32 = jnp.float32
    nrm = lambda shape, scale: scale * jax.random.normal(next(ks), shape, f32)
    gain = lambda shape: 1.0 + 0.05 * jax.random.normal(next(ks), shape, f32)
    L = DEPTH
    return {
        'x_prompt': nrm((BATCH, SEQ, D_MODEL), 1.0),
        'x_sample': nrm((DEC_BATCH, DEC_SEQ, D_MODEL), 1.0),
        'cache_kv_latent': nrm((L, DEC_BATCH, PAST_LEN, KV_LORA), 1.0),
        'cache_k_rope': nrm((L, DEC_BATCH, PAST_LEN, A_ROPE), 1.0),
        'state_C': nrm((L, DEC_BATCH, M_HEADS, M_HEAD_DIM, M_HEAD_DIM), M_HEAD_DIM ** -0.5),
        'state_n': nrm((L, DEC_BATCH, M_HEADS, M_HEAD_DIM), 0.5),
        'state_m': nrm((L, DEC_BATCH, M_HEADS), 1.0),
        'ff1_pre_g': gain((L, D_MODEL)),
        'ff1_w_gate': nrm((L, D_MODEL, D_FF), D_MODEL ** -0.5),
        'ff1_w_up': nrm((L, D_MODEL, D_FF), D_MODEL ** -0.5),
        'ff1_w_down': nrm((L, D_FF, D_MODEL), D_FF ** -0.5),
        'ff1_post_g': gain((L, D_MODEL)),
        'mix_pre_g': gain((L, D_MODEL)),
        'w_in': nrm((L, D_MODEL, IN_WIDTH), D_MODEL ** -0.5),
        'b_igate': nrm((L, M_HEADS), 0.1),
        'b_fgate': 3.0 + nrm((L, M_HEADS), 0.5),
        'q_a_g': gain((L, Q_LORA)),
        'w_uq': nrm((L, Q_LORA, A_HEADS * (A_NOPE + A_ROPE)), Q_LORA ** -0.5),
        'kv_a_g': gain((L, KV_LORA)),
        'w_ukv': nrm((L, KV_LORA, A_HEADS * (A_NOPE + A_V)), KV_LORA ** -0.5),
        'm_head_g': gain((L, M_HEADS, M_HEAD_DIM)),
        'w_out': nrm((L, MIX_WIDTH, D_MODEL), MIX_WIDTH ** -0.5),
        'mix_post_g': gain((L, D_MODEL)),
        'ff2_pre_g': gain((L, D_MODEL)),
        'ff2_w_gate': nrm((L, D_MODEL, D_FF), D_MODEL ** -0.5),
        'ff2_w_up': nrm((L, D_MODEL, D_FF), D_MODEL ** -0.5),
        'ff2_w_down': nrm((L, D_FF, D_MODEL), D_FF ** -0.5),
        'ff2_post_g': gain((L, D_MODEL)),
    }

def reference(x_prompt, x_sample, cache_kv_latent, cache_k_rope, state_C, state_n, state_m,
              ff1_pre_g, ff1_w_gate, ff1_w_up, ff1_w_down, ff1_post_g,
              mix_pre_g, w_in, b_igate, b_fgate, q_a_g, w_uq, kv_a_g, w_ukv, m_head_g, w_out, mix_post_g,
              ff2_pre_g, ff2_w_gate, ff2_w_up, ff2_w_down, ff2_post_g):
    y_prompt, y_sample = x_prompt, x_sample
    pos_p = jnp.arange(x_prompt.shape[1])
    pos_s = cache_kv_latent.shape[2] + jnp.arange(x_sample.shape[1])
    new_p, new_s = [], []
    for l in range(DEPTH):
        ff1 = (ff1_pre_g[l], ff1_w_gate[l], ff1_w_up[l], ff1_w_down[l], ff1_post_g[l])
        mix = (mix_pre_g[l], w_in[l], b_igate[l], b_fgate[l], q_a_g[l], w_uq[l], kv_a_g[l],
               m_head_g[l], w_out[l], mix_post_g[l])
        ff2 = (ff2_pre_g[l], ff2_w_gate[l], ff2_w_up[l], ff2_w_down[l], ff2_post_g[l])
        wkv = w_ukv[l]
        y_prompt, st_p = run_layer(y_prompt, pos_p, lambda proj: prompt_token_mix(proj, pos_p, wkv), ff1, mix, ff2)
        cache_l = (cache_kv_latent[l], cache_k_rope[l], state_C[l], state_n[l], state_m[l])
        y_sample, st_s = run_layer(y_sample, pos_s, lambda proj: sample_token_mix(proj, pos_s, wkv, *cache_l), ff1, mix, ff2)
        new_p.append(st_p)
        new_s.append(st_s)
    p_kv_latent, p_k_rope, p_C, p_n, p_m = [jnp.stack(a) for a in zip(*new_p)]
    s_kv_latent, s_k_rope, s_C, s_n, s_m = [jnp.stack(a) for a in zip(*new_s)]
    return (y_prompt, y_sample, p_kv_latent, p_k_rope, p_C, p_n, p_m, s_kv_latent, s_k_rope, s_C, s_n, s_m)


_drawn_inputs = setup_inputs


def setup_inputs(seed=0):
    import zlib

    import numpy as np

    out = dict(_drawn_inputs(seed))
    spreads = {}
    factors = {'b_fgate': 22.192, 'q_a_g': 7.157, 'ff2_post_g': 3.928}
    for name, (base, spread) in spreads.items():
        noise = np.random.default_rng([zlib.crc32(name.encode()), seed]).standard_normal(out[name].shape)
        drawn = base * np.exp(spread * noise) if base else spread * noise
        out[name] = __import__('jax').numpy.asarray(drawn.astype(out[name].dtype))
    for name, factor in factors.items():
        out[name] = (out[name] * factor).astype(out[name].dtype)
    return out
```

```python
from contextlib import ExitStack

import concourse.bass as bass
from concourse import mybir

P = 128
D = 1024
KD = D // P
SEQ = 512
DEC = 64
T = SEQ + DEC
HT = T // 2
PAST = 256
TT = 5
FF = 2816
JF = FF // P
EPS = 1e-6
MH = 4
AH = 8
NOPE = 64
ROPE = 32
QK = NOPE + ROPE
AV = 64
QL = 384
KQ = QL // P
KVL = 256
KC = KVL // P
TK = T + PAST
MW = MH * P
A_SCALE = QK ** -0.5
MASKED = -3.0e38
NRAW = 4
NW = 2
DOWN_PARTS = (6, 6, 5, 5)
VP = 130
VAW = AH * AV + 32

F32 = mybir.dt.float32
F32R = mybir.dt.float32r
ACT = mybir.ActivationFunctionType
ALU = mybir.AluOpType
AX = mybir.AxisListType.X

GAINS = (("ff1_pre_g", KD), ("ff1_post_g", KD), ("mix_pre_g", KD), ("mix_post_g", KD), ("ff2_pre_g", KD),
         ("ff2_post_g", KD), ("q_a_g", KQ), ("kv_a_g", KC), ("m_head_g", MH))
GROW = {}
_n = 0
for _name, _k in GAINS:
    GROW[_name] = _n
    _n += _k
NG = _n

NB_GU = 2 * JF
NB_DOWN = KD * len(DOWN_PARTS)
NB_FF = NB_GU + NB_DOWN
MIX0 = NB_FF
B_AQ = MIX0
B_CKV = B_AQ + KQ
B_SMALL = B_CKV + KC
B_QK = B_SMALL + 1
B_UKV = B_QK + 2 * MH
B_UQ = B_UKV + 2
B_VO = B_UQ + 3
B_OUT = B_VO + 2 * MH
FF2_0 = B_OUT + KD
NB = FF2_0 + NB_FF
LOADS = [1] * NB
LOADS[B_SMALL] = 3
LOADS[B_UKV] = LOADS[B_UKV + 1] = KC
for _b in range(3):
    LOADS[B_UQ + _b] = KQ


def arrived(b):
    return 16 * sum(LOADS[c] for c in range(b % NRAW, b + 1, NRAW))


def build(nc, a, rope_table, outs):
    (y_prompt, y_sample, p_kv, p_kr, p_C, p_n, p_m, s_kv, s_kr, s_C, s_n, s_m) = outs
    ctx = ExitStack()
    with ctx:
        def sem(name):
            return ctx.enter_context(nc.semaphore(name))

        top = [(nc.sbuf_base + 31) // 32 * 32]

        def place(name, shape, dt=F32, offset=None):
            n = 4
            for s in shape[1:]:
                n *= s
            if offset is None:
                offset = top[0]
                top[0] += (n + 31) // 32 * 32
            return nc.alloc_sbuf_tensor_at(name, shape, dt, offset=offset)

        ROW = T * 4
        X = place("X", [P, KD, T])
        h_at = top[0]
        H_HI = place("H_HI", [P, KD, T], F32R)
        H_LO = place("H_LO", [P, KD, T], F32R)
        u_at = top[0]
        U_HI = place("U_HI", [P, JF, T], F32R)
        U_LO = place("U_LO", [P, JF, T], F32R)
        RAW = place("RAW", [P, NRAW, 8, P])
        W_HI = place("W_HI", [P, NW, 8, P], F32R)
        W_LO = place("W_LO", [P, NW, 8, P], F32R)
        RB = place("RB", [P, T])
        PAIR = place("PAIR", [P, 2, T])
        TF = place("TF", [P, 2, T])
        acc_at = top[0]
        ACC = place("ACC", [P, T])
        IDENT = place("IDENT", [P, P])
        ONES = place("ONES", [P, P])
        PERM = place("PERM", [P, P])
        trig_at = top[0]
        TRIG = place("TRIG", [P, 2, T])
        GCOLS = place("GCOLS", [P, NG])
        SEL = place("SEL", [MH, MH, P])
        GC = place("GC", [P, TT, MH])
        EMC = place("EMC", [P, TT, MH])
        BIAS = place("BIAS", [MH, 4])
        MEND = place("MEND", [MH, 2])
        M0B = place("M0B", [P, MH])
        WE = place("WE", [P, TT])
        S5 = place("S5", [P, 8, TT])
        EPSC = place("EPSC", [P, 1])
        assert top[0] <= nc.sbuf_usable_end, (top[0], nc.sbuf_usable_end)
        XIN = place("XIN", [P, TT, D], offset=u_at)
        GROWS = place("GROWS", [NG, P], offset=u_at + TT * D * 4)
        Y = place("Y", [P, KD, T], offset=h_at)
        PJ1 = place("PJ1", [P, 2 * MH, T], offset=u_at)
        PJ2 = place("PJ2", [P, 2 * MH, T], offset=u_at + 8 * ROW)
        CQ_HI = place("CQ_HI", [P, KQ, T], F32R, offset=u_at + 8 * ROW)
        CQ_LO = place("CQ_LO", [P, KQ, T], F32R, offset=u_at + 11 * ROW)
        qh_at = u_at + 16 * ROW
        QH = place("QH", [QK, AH, T], offset=qh_at)
        C_HI = place("C_HI", [P, KC, TK], F32R, offset=qh_at)
        C_LO = place("C_LO", [P, KC, TK], F32R, offset=qh_at + KC * TK * 4)
        kh_at = u_at + 24 * ROW
        KH = place("KH", [QK, AH, TK], offset=kh_at)
        CRAW = place("CRAW", [P, KC, TK], offset=kh_at)
        AQRAW = place("AQRAW", [P, KQ, T], offset=kh_at + KC * TK * 4)
        CIN = place("CIN", [P, 2, KVL], offset=kh_at + KC * TK * 4 + 3 * ROW)
        KIN = place("KIN", [P, 2, ROPE], offset=kh_at + KC * TK * 4 + 3 * ROW + 2048)
        CSTAGE = place("CSTAGE", [P, TT, KVL], offset=kh_at + KC * TK * 4 + 3 * ROW + 2304)
        ARS = place("ARS", [ROPE, T], offset=kh_at + KC * TK * 4 + 3 * ROW + 2304 + 5120)
        ONES4 = place("ONES4", [MH, T], offset=kh_at + KC * TK * 4 + 4 * ROW + 2304 + 5120)
        assert KC * TK * 4 + 5 * ROW + 2304 + 5120 <= AH * TK * 4
        va_at = kh_at + AH * TK * 4
        VA = place("VA", [P, 7, VAW], offset=va_at)
        IG, LF, BC, GR, MX, EM = (place(n, [MH, T], offset=va_at + i * ROW) for i, n in
                                  enumerate(("IG", "LF", "BC", "GR", "MX", "EM")))
        assert 6 * ROW <= 7 * VAW * 4
        rest_at = va_at + 7 * VAW * 4
        KR = place("KR", [ROPE, TK], offset=rest_at)
        assert rest_at + TK * 4 <= u_at + 2 * JF * ROW
        NM = place("NM", [MH, T], offset=acc_at)
        C0T = place("C0T", [P, MH, VP], offset=rest_at)
        N0 = place("N0", [1, MH, P], offset=rest_at + MH * VP * 4)
        assert rest_at + MH * VP * 4 + 2048 <= u_at + 2 * JF * ROW
        at = [h_at]

        def local(name, shape, dt=F32):
            t = place(name, shape, dt, offset=at[0])
            n = 4
            for s in shape[1:]:
                n *= s
            at[0] += (n + 31) // 32 * 32
            return t

        KT = local("KT", [P, TT, MH, P])
        VT = local("VT", [P, TT, MH, VP])
        OS = local("OS", [P, TT, VP])
        DW = local("DW", [P, 1344])
        VW = local("VW", [P, TT, P])
        HN = local("HN", [P, TT, P])
        C0 = local("C0", [P, MH, P])
        N0R = local("N0R", [MH, P])
        assert at[0] <= h_at + 16 * ROW
        at[0] = h_at
        PR = local("PR", [P, 2, 1600])
        PT = local("PT", [P, 2, 1472])
        AT = local("AT", [P, TT, P])
        assert at[0] <= h_at + 16 * ROW
        MA_HI = place("MA_HI", [P, MH, T], F32R, offset=u_at + 8 * ROW)
        MA_LO = place("MA_LO", [P, MH, T], F32R, offset=u_at + 4 * ROW)
        MB_HI = place("MB_HI", [P, MH, T], F32R, offset=u_at)
        MB_LO = place("MB_LO", [P, MH, T], F32R, offset=u_at + 12 * ROW)
        CN = place("CN", [P, 2, 2, P], offset=trig_at)
        NN = place("NN", [1, 2, P], offset=trig_at + 2048)
        KSTAGE = place("KSTAGE", [P, TT, ROPE], offset=trig_at + 3072)

        PS = ctx.enter_context(nc.psum_tensor("PS", [P, 8, 512], F32))
        PSF = PS[:].rearrange("p b n -> p (b n)")

        def pair(b, rows=P, n=HT):
            return PS[0:rows, b:b + 2, 0:n]

        def halves(ap, n=HT):
            return ap.rearrange("p (a n) -> p a n", n=n)

        raw_in = [sem(f"raw_in{i}") for i in range(NRAW)]
        w_hi, w_lo, w_used = sem("w_hi"), sem("w_lo"), sem("w_used")
        x_in, g_in, trig_in, bias_in, cache_in, state_in = (sem(n) for n in (
            "x_in", "g_in", "trig_in", "bias_in", "cache_in", "state_in"))
        consts, consts0 = sem("consts"), sem("consts0")
        g_T, g_cols, g_half = sem("g_T"), sem("g_cols"), sem("g_half")
        x_T, x_cols = sem("x_T"), sem("x_cols")
        out_sem = sem("out_sem")
        dve_step, act_step, pool_step = sem("dve_step"), sem("act_step"), sem("pool_step")
        steps = {"dve": 0, "act": 0, "pool": 0}

        def settle(eng, key, s, ins):
            steps[key] += 1
            ins.then_inc(s, 1)
            eng.wait_ge(s, steps[key])

        def names(prefix, *what):
            return {w: sem(f"{prefix}_{w}") for w in what}

        class Since:

            def __init__(self, sem_, base):
                self.sem, self.base = sem_, base

        def stages(prefix, count, **per_stage):
            sems = {w: sem(f"{prefix}_{w}") for w in per_stage}
            return [{w: Since(sems[w], i * total) for w, total in per_stage.items()}
                    for i in range(count)]

        post = stages("post", 3, y_sq=KD, acc=KD, sum=1, root=1, t=KD // 2, x_even=KD // 2, x_odd=KD // 2)
        pre = stages("pre", 3, sq=KD, sum=1, root=1, h=KD, hi=KD, lo_even=KD // 2, lo_odd=KD // 2, used=KD - 1)
        ff = stages("ff", 2, silu=JF, mul=JF, u_hi=JF, u_lo=JF)

        def raw_slot(b):
            return RAW[:, b % NRAW]

        def load_wait(sp, b):
            if b >= NRAW:
                sp.wait_ge(w_lo, b - NRAW + 1)

        def load_ffn(sp, b0, wg, wu, wd):
            gv = wg.rearrange("(k p) f -> p k f", p=P)
            uv = wu.rearrange("(k p) f -> p k f", p=P)
            dv = wd.rearrange("(k p) f -> p k f", p=P)

            def tiles(i, first=False):
                for q in range(4):
                    b = b0 + q
                    if not (first and b < NRAW):
                        sp.wait_ge(w_lo, b0 + i * 4 + q - NRAW + 1)
                    src = (gv, uv)[q % 2]
                    sp.dma_start(raw_slot(b), src[:, :, bass.ds(i * (2 * P) + (q // 2) * P, P)]).then_inc(
                        raw_in[b % NRAW], 16)

            tiles(0, first=True)
            with sp.Fori(1, JF // 2) as i:
                tiles(i)
            b1 = b0 + NB_GU
            with sp.Fori(0, KD) as m:
                k0 = 0
                for q, n in enumerate(DOWN_PARTS):
                    sp.wait_ge(w_lo, m * 4 + (b1 + q - NRAW + 1))
                    sp.dma_start(raw_slot(b1 + q)[:, 0:n, :], dv[:, k0:k0 + n, bass.ds(m * P, P)]).then_inc(
                        raw_in[(b1 + q) % NRAW], 16)
                    k0 += n

        def split_hi(act, b, n=8, count=None, target=None):
            act.wait_ge(raw_in[b % NRAW], arrived(b) if target is None else target)
            if count is None:
                if b >= NW:
                    act.wait_ge(w_used, b - NW + 1)
            else:
                act.wait_ge(w_used, count - NW + 1)
            nc.scalar.activation(W_HI[:, b % NW, 0:n, :], raw_slot(b)[:, 0:n, :], ACT.Copy).then_inc(w_hi, 1)

        def split_lo(dve, b, n=8, count=None):
            dve.wait_ge(w_hi, (b if count is None else count) + 1)
            nc.vector.tensor_tensor(W_LO[:, b % NW, 0:n, :], raw_slot(b)[:, 0:n, :],
                                    W_HI[:, b % NW, 0:n, :].bitcast(F32), ALU.subtract).then_inc(w_lo, 1)

        def weights_ready(pe, count):
            pe.wait_ge(w_hi, count + 1)
            pe.wait_ge(w_lo, count + 1)

        def passes(w_hi_t, w_lo_t, a_hi, a_lo):
            return ((w_hi_t, a_hi), (w_hi_t, a_lo), (w_lo_t, a_hi))

        def product(b, t, hi, lo, bank, start, stop, m=P, rows=P, n=HT):
            wh, wl = W_HI[0:rows, b % NW, t, 0:m], W_LO[0:rows, b % NW, t, 0:m]
            last = None
            for i, (w, x) in enumerate(passes(wh, wl, hi, lo)):
                for s in range(2):
                    last = nc.tensor.matmul(PS[0:m, bank + s, 0:n], w, x[:, s * n:(s + 1) * n],
                                            start=start and i == 0, stop=stop and i == 2)
            return last

        def sum_over_features(src, bank, start, stop):
            for s in range(2):
                last = nc.tensor.matmul(PS[:, bank + s, 0:HT], ONES[:], src[:, s * HT:(s + 1) * HT],
                                        start=start, stop=stop)
            return last

        def post_pe(pe, e):
            pe.wait_ge(e["acc"].sem, KD + e["acc"].base)
            sum_over_features(ACC[:], 0, True, True).then_inc(e["sum"].sem, 1)

        def post_act(act, e):
            act.wait_ge(e["sum"].sem, 1 + e["sum"].base)
            nc.scalar.activation(halves(RB[:]), pair(0), ACT.Sqrt, bias=EPSC[:], scale=1.0 / D).then_inc(e["root"].sem, 1)

        def post_dve(dve, e):
            dve.wait_ge(e["root"].sem, 1 + e["root"].base)
            settle(dve, "dve", dve_step, nc.vector.reciprocal(RB[:], RB[:]))
            for k in range(KD):
                ins = nc.vector.tensor_tensor(Y[:, k], Y[:, k], RB[:], ALU.mult)
                if k % 2:
                    ins.then_inc(e["t"].sem, 1)
                else:
                    settle(dve, "dve", dve_step, ins)
                    nc.vector.tensor_tensor(X[:, k], X[:, k], Y[:, k], ALU.add).then_inc(e["x_even"].sem, 1)

        def post_pool(pool, e):
            for k in range(1, KD, 2):
                pool.wait_ge(e["t"].sem, k // 2 + 1 + e["t"].base)
                nc.gpsimd.tensor_tensor(X[:, k], X[:, k], Y[:, k], ALU.add).then_inc(e["x_odd"].sem, 1)

        def x_wait(eng, e, k):
            if e is None:
                eng.wait_ge(x_cols, k + 2)
            else:
                done = e["x_odd"] if k % 2 else e["x_even"]
                eng.wait_ge(done.sem, k // 2 + 1 + done.base)

        def pre_act(act, e, before):
            for k in range(KD):
                x_wait(act, before, k)
                if k >= 2:
                    act.wait_ge(e["used"].sem, k - 1 + e["used"].base)
                nc.scalar.activation(PAIR[:, k % 2], X[:, k], ACT.Square).then_inc(e["sq"].sem, 1)
            act.wait_ge(e["sum"].sem, 1 + e["sum"].base)
            nc.scalar.activation(halves(RB[:]), pair(2), ACT.Sqrt, bias=EPSC[:], scale=1.0 / D).then_inc(e["root"].sem, 1)
            for k in range(KD):
                act.wait_ge(e["h"].sem, k + 1 + e["h"].base)
                nc.scalar.activation(H_HI[:, k], TF[:, k % 2], ACT.Copy).then_inc(e["hi"].sem, 1)

        def pre_pe(pe, e):
            for k in range(KD):
                pe.wait_ge(e["sq"].sem, k + 1 + e["sq"].base)
                last = sum_over_features(PAIR[:, k % 2], 2, k == 0, k == KD - 1)
                last.then_inc(e["sum"].sem if k == KD - 1 else e["used"].sem, 1)

        def pre_dve(dve, e, gain):
            g0 = GROW[gain]
            dve.wait_ge(e["root"].sem, 1 + e["root"].base)
            settle(dve, "dve", dve_step, nc.vector.reciprocal(RB[:], RB[:]))

            def low(k):
                dve.wait_ge(e["hi"].sem, k + 1 + e["hi"].base)
                nc.vector.tensor_tensor(H_LO[:, k], TF[:, k % 2], H_HI[:, k].bitcast(F32),
                                        ALU.subtract).then_inc(e["lo_even"].sem, 1)
            for k in range(KD):
                if k >= 2:
                    done = e["lo_odd"] if k % 2 else e["lo_even"]
                    dve.wait_ge(done.sem, k // 2 + done.base)
                nc.vector.scalar_tensor_tensor(out=TF[:, k % 2], in0=X[:, k], scalar=GCOLS[:, g0 + k:g0 + k + 1],
                                               in1=RB[:], op0=ALU.mult, op1=ALU.mult).then_inc(e["h"].sem, 1)
                if k % 2:
                    low(k - 1)

        def pre_pool(pool, e):
            for k in range(1, KD, 2):
                pool.wait_ge(e["hi"].sem, k + 1 + e["hi"].base)
                nc.gpsimd.tensor_tensor(H_LO[:, k], TF[:, k % 2], H_HI[:, k].bitcast(F32),
                                        ALU.subtract).then_inc(e["lo_odd"].sem, 1)

        def h_wait(pe, e, k):
            pe.wait_ge(e["hi"].sem, k + 1 + e["hi"].base)
            low = e["lo_odd"] if k % 2 else e["lo_even"]
            pe.wait_ge(low.sem, k // 2 + 1 + low.base)

        def ffn_pe(pe, f, e, p, b0):
            def gate_up(i, first=False):
                for jj in range(2):
                    j = i * 2 + jj
                    for q in range(2):
                        b = b0 + 2 * jj + q
                        weights_ready(pe, i * 4 + b)
                        if not (first and jj == 0):
                            done = f["mul"] if q else f["silu"]
                            pe.wait_ge(done.sem, j + done.base)
                        for k in range(KD):
                            if first and jj == 0 and q == 0:
                                h_wait(pe, e, k)
                            last = product(b, k, H_HI[:, k], H_LO[:, k], 2 * q, k == 0, k == KD - 1)
                        last.then_inc(w_used, 1)

            gate_up(0, first=True)
            with pe.Fori(1, JF // 2) as i:
                gate_up(i)
            b1 = b0 + NB_GU

            def down(i, first=False):
                for mm in range(2):
                    m = i * 2 + mm
                    if not first:
                        pe.wait_ge(p["y_sq"].sem, m - 1 + p["y_sq"].base)
                    k = 0
                    for q, n in enumerate(DOWN_PARTS):
                        b = b1 + q
                        weights_ready(pe, i * 8 + (b1 + 4 * mm + q))
                        if first and mm == 0:
                            pe.wait_ge(f["u_lo"].sem, k + n + f["u_lo"].base)
                        for t in range(n):
                            last = product(b, t, U_HI[:, k], U_LO[:, k], 4 + 2 * mm, k == 0, k == JF - 1)
                            k += 1
                        last.then_inc(w_used, 1)

            down(0, first=True)
            with pe.Fori(1, KD // 2) as i:
                down(i)

        def down_target(b1, q, m):
            return arrived(b1 + q) + 16 * m if isinstance(m, int) else m * 16 + arrived(b1 + q)

        def ffn_act(act, f, p, b0, post_gain):
            b1 = b0 + NB_GU

            def gate_up(i, last=False):
                for jj in range(2):
                    j = i * 2 + jj
                    act.wait_ge(w_used, i * 4 + (b0 + 2 * jj + 1))
                    if not (isinstance(i, int) and i == 0):
                        act.wait_ge(f["mul"].sem, j - 1 + f["mul"].base)
                    nc.scalar.activation(halves(PAIR[:, jj]), pair(0), ACT.Silu).then_inc(f["silu"].sem, 1)
                    for q in range(2):
                        b = b0 + 2 * jj + q + 2
                        if last and jj == 1:
                            split_hi(act, b1 + q, DOWN_PARTS[q])
                        else:
                            split_hi(act, b, 8, i * 4 + b, i * 16 + arrived(b))
                    act.wait_ge(f["mul"].sem, j + 1 + f["mul"].base)
                    nc.scalar.activation(U_HI[:, bass.ds(j, 1), :], TF[:, jj:jj + 1, :], ACT.Copy).then_inc(f["u_hi"].sem, 1)

            gate_up(0)
            with act.Fori(1, JF // 2 - 1) as i:
                gate_up(i)
            gate_up(JF // 2 - 1, last=True)

            def down(i, first=False, last=False):
                for mm in range(2):
                    m = i * 2 + mm
                    for q in range(4):
                        nq = q + 2
                        over = nq // 4
                        if not (last and mm == 1 and over):
                            b = b1 + nq % 4
                            split_hi(act, b, DOWN_PARTS[nq % 4], i * 8 + (b1 + 4 * mm + nq),
                                     i * 32 + (arrived(b) + 16 * (mm + over)))
                        elif b0 == 0:
                            split_hi(act, MIX0 + nq % 4)
                    act.wait_ge(w_used, i * 8 + (b1 + 4 * mm + 4))
                    y_out(act, p, m, mm, 4 + 2 * mm, post_gain, first)

            down(0, first=True)
            with act.Fori(1, KD // 2 - 1) as i:
                down(i)
            down(KD // 2 - 1, last=True)

        def y_out(act, p, m, slot, bank, gain, first):
            if not first:
                act.wait_ge(p["acc"].sem, m - 1 + p["acc"].base)
            nc.scalar.activation(halves(Y[:, bass.ds(m, 1), :].rearrange("p a t -> p (a t)")), pair(bank), ACT.Copy,
                                 scale=GCOLS[:, bass.ds(m + GROW[gain], 1)])
            nc.scalar.activation(halves(PAIR[:, slot]), pair(bank), ACT.Square).then_inc(p["y_sq"].sem, 1)

        def ffn_dve(dve, f, b0):
            b1 = b0 + NB_GU

            def gate_up(i, last=False):
                for jj in range(2):
                    j = i * 2 + jj
                    b = b0 + 2 * jj + 2
                    tail = last and jj == 1
                    if tail:
                        split_lo(dve, b1, DOWN_PARTS[0])
                    else:
                        split_lo(dve, b, 8, i * 4 + b)
                    dve.wait_ge(f["silu"].sem, j + 1 + f["silu"].base)
                    dve.wait_ge(w_used, i * 4 + (b0 + 2 * jj + 2))
                    if not (isinstance(i, int) and i == 0):
                        dve.wait_ge(f["u_lo"].sem, j - 1 + f["u_lo"].base)
                    nc.vector.tensor_tensor(halves(TF[:, jj]), halves(PAIR[:, jj]), pair(2), ALU.mult).then_inc(f["mul"].sem, 1)
                    if tail:
                        split_lo(dve, b1 + 1, DOWN_PARTS[1])
                    else:
                        split_lo(dve, b + 1, 8, i * 4 + (b + 1))
                    dve.wait_ge(f["u_hi"].sem, j + 1 + f["u_hi"].base)
                    nc.vector.tensor_tensor(U_LO[:, bass.ds(j, 1), :], TF[:, jj:jj + 1, :],
                                            U_HI[:, bass.ds(j, 1), :].bitcast(F32), ALU.subtract).then_inc(f["u_lo"].sem, 1)

            gate_up(0)
            with dve.Fori(1, JF // 2 - 1) as i:
                gate_up(i)
            gate_up(JF // 2 - 1, last=True)

            def down(i, last=False):
                for mm in range(2):
                    for q in range(4):
                        nq = q + 2
                        if not (last and mm == 1 and nq >= 4):
                            split_lo(dve, b1 + nq % 4, DOWN_PARTS[nq % 4], i * 8 + (b1 + 4 * mm + nq))
                        elif b0 == 0:
                            split_lo(dve, MIX0 + nq % 4)

            with dve.Fori(0, KD // 2 - 1) as i:
                down(i)
            down(KD // 2 - 1, last=True)

        def acc_pool(pool, p):
            for m in range(KD):
                pool.wait_ge(p["y_sq"].sem, m + 1 + p["y_sq"].base)
                if m == 0:
                    nc.gpsimd.tensor_copy(ACC[:], PAIR[:, 0]).then_inc(p["acc"].sem, 1)
                else:
                    pool.wait_ge(p["acc"].sem, m + p["acc"].base)
                    nc.gpsimd.tensor_tensor(ACC[:], ACC[:], PAIR[:, m % 2], ALU.add).then_inc(p["acc"].sem, 1)


        def start_pool(pool):
            nc.gpsimd.memset(IDENT[:], 0.0).then_inc(consts0, 1)
            nc.gpsimd.memset(PERM[:], 0.0).then_inc(consts0, 1)
            nc.gpsimd.memset(SEL[:], 0.0).then_inc(consts0, 1)
            nc.gpsimd.memset(EPSC[:], EPS)
            nc.gpsimd.memset(S5[:], 1.0)
            nc.gpsimd.memset(ONES[:], 1.0)
            nc.gpsimd.memset(GC[:], 0.0)
            nc.gpsimd.memset(EMC[:], 1.0)
            pool.wait_ge(consts0, 3)
            nc.gpsimd.affine_select(out=IDENT[:], in_=IDENT[:], compare_op=ALU.not_equal, fill=1.0, base=0,
                                    pattern=[[-1, P]], channel_multiplier=1).then_inc(consts, 1)
            nc.gpsimd.affine_select(out=PERM[:].rearrange("p (q a c) -> p q a c", a=2, c=ROPE // 2),
                                    in_=PERM[:].rearrange("p (q a c) -> p q a c", a=2, c=ROPE // 2),
                                    compare_op=ALU.not_equal, fill=1.0, base=ROPE // 2,
                                    pattern=[[ROPE, P // ROPE], [-(ROPE // 2), 2], [1, ROPE // 2]],
                                    channel_multiplier=-1).then_inc(consts, 1)
            nc.gpsimd.affine_select(out=SEL[:], in_=SEL[:], compare_op=ALU.not_equal, fill=1.0, base=0,
                                    pattern=[[1, MH], [0, P]], channel_multiplier=-1).then_inc(consts, 1)
            pool.dma_start(TRIG[:], rope_table).then_inc(trig_in, 16)
            pool.dma_start(BIAS[:, 0:1], a["b_igate"].rearrange("l h -> h l")).then_inc(bias_in, 16)
            pool.dma_start(BIAS[:, 1:2], a["b_fgate"].rearrange("l h -> h l")).then_inc(bias_in, 16)
            pool.dma_start(BIAS[:, 2:3], a["state_m"].rearrange("l b h -> h (l b)")).then_inc(bias_in, 16)
            pool.dma_start(M0B[:], a["state_m"][0].to_broadcast([P, MH])).then_inc(bias_in, 16)

        def start_sp(sp):
            for name, k in GAINS:
                g = a[name][0]
                g = g if name == "m_head_g" else g.rearrange("(k p) -> k p", p=P)
                sp.dma_start(GROWS[GROW[name]:GROW[name] + k, :], g).then_inc(g_in, 16)
            sp.dma_start(XIN[0:DEC, TT - 1, :], a["x_sample"][0]).then_inc(x_in, 16)
            sp.dma_start(XIN[:, 0:4, :], a["x_prompt"][0].rearrange("(t p) d -> p t d", p=P)).then_inc(x_in, 16)

        X_BANKS = (0, 1, 4, 5)

        def start_pe(pe):
            pe.wait_ge(consts, 3)
            pe.wait_ge(g_in, 16 * len(GAINS))
            nc.tensor.transpose(PS[:, 7, 0:NG], GROWS[:], IDENT[0:NG, 0:NG]).then_inc(g_T, 1)
            pe.wait_ge(x_in, 32)
            for k in range(KD):
                last = nc.tensor.transpose(PS[:, 6, k * DEC:(k + 1) * DEC], XIN[0:DEC, TT - 1, k * P:(k + 1) * P],
                                           IDENT[0:DEC, 0:DEC])
            last.then_inc(x_T, 1)
            for k in range(KD):
                if k >= 4:
                    pe.wait_ge(x_cols, k - 2)
                for t in range(4):
                    last = nc.tensor.transpose(PS[:, X_BANKS[k % 4], t * P:(t + 1) * P],
                                               XIN[:, t, k * P:(k + 1) * P], IDENT[:])
                last.then_inc(x_T, 1)

        def start_dve(dve):
            dve.wait_ge(g_T, 1)
            settle(dve, "dve", dve_step, nc.vector.tensor_copy(GCOLS[:], PS[:, 7, 0:NG]))
            for name in ("ff1_post_g", "ff2_post_g"):
                g = GCOLS[:, GROW[name]:GROW[name] + KD]
                nc.vector.tensor_scalar(g, g, 0.5, None, ALU.mult).then_inc(g_half, 1)
            dve.wait_ge(x_T, 1)
            nc.vector.tensor_copy(X[:, :, SEQ:T], PS[:, 6, :].rearrange("p (k t) -> p k t", k=KD)).then_inc(x_cols, 1)
            for k in range(KD):
                dve.wait_ge(x_T, k + 2)
                nc.vector.tensor_copy(X[:, k, 0:SEQ], PS[:, X_BANKS[k % 4], :]).then_inc(x_cols, 1)

        def finish_pe(pe):
            for k in range(KD):
                x_wait(pe, post[2], k)
                b = 2 * (k % 4)
                if k >= 4:
                    pe.wait_ge(o["copied"], k - 3)
                for t in range(4):
                    nc.tensor.transpose(PS[:, b, t * P:(t + 1) * P], X[:, k, t * P:(t + 1) * P], IDENT[:])
                nc.tensor.transpose(PS[0:DEC, b + 1, 0:P], X[:, k, SEQ:T], IDENT[:]).then_inc(o["T"], 1)

        def finish_act(act):
            for k in range(KD):
                act.wait_ge(o["T"], k + 1)
                b = 2 * (k % 4)
                nc.scalar.activation(XIN[:, 0:4, k * P:(k + 1) * P],
                                     PS[:, b, :].rearrange("p (t f) -> p t f", t=4), ACT.Copy)
                nc.scalar.activation(XIN[0:DEC, 4, k * P:(k + 1) * P], PS[0:DEC, b + 1, 0:P],
                                     ACT.Copy).then_inc(o["copied"], 1)

        def finish_sp(sp):
            for h in range(2):
                sp.wait_ge(o["copied"], 4 * (h + 1))
                c = slice(h * D // 2, (h + 1) * D // 2)
                sp.dma_start(y_prompt[0].rearrange("(t p) d -> p t d", p=P)[:, :, c], XIN[:, 0:4, c]).then_inc(out_sem, 16)
                sp.dma_start(y_sample[0][:, c], XIN[0:DEC, 4, c]).then_inc(out_sem, 16)
            sp.wait_ge(out_sem, 64)
            sp.wait_ge(st["stored"], 64)
            sp.wait_ge(m1["c_stored"], 32)
            sp.wait_ge(m2["state_out"], 64 * MH)

        o = names("out", "T", "copied")
        m1 = names("m1", "cache_T", "cache_hi", "cache_lo", "kr_c", "proj", "aq_sum", "aq_root", "cq", "c_sum", "c_root",
                   "c", "cq_lo", "c_lo", "ig", "lf1", "abs_z", "soft", "lf", "mm", "em", "perm", "c_T", "c_staged", "c_stored",
                   "kr", "k_scaled", "kn_T", "kn_a", "kn_d", "gate_T", "gate_c", "v_T", "v_a", "v_d", "q_T", "q_a", "q_d",
                   "rs", "perm_q", "qr", "rope_in", "kr_T", "kr_staged")
        st = names("st", "stored")

        def load_mix(sp):
            w_in, w_uq, w_ukv, w_out = (a[n][0] for n in ("w_in", "w_uq", "w_ukv", "w_out"))
            wv = w_in.rearrange("(k p) f -> p k f", p=P)
            c_gate, c_aq = 4 * MW, 4 * MW + 2 * MH
            c_ckv = c_aq + QL
            c_ar = c_ckv + KVL

            def one(b, *parts):
                load_wait(sp, b)
                for dst, src in parts:
                    sp.dma_start(dst, src).then_inc(raw_in[b % NRAW], 16)

            for i in range(KQ):
                one(B_AQ + i, (raw_slot(B_AQ + i), wv[:, :, c_aq + i * P:c_aq + (i + 1) * P]))
            for i in range(KC):
                one(B_CKV + i, (raw_slot(B_CKV + i), wv[:, :, c_ckv + i * P:c_ckv + (i + 1) * P]))
            one(B_SMALL, *((raw_slot(B_SMALL)[:, :, at_:at_ + n], wv[:, :, lo:lo + n])
                           for at_, lo, n in ((0, c_ar, ROPE), (32, c_gate, MH), (64, c_gate + MH, MH))))

            def heads(b0, c0):
                with sp.Fori(0, 2) as i:
                    for t in range(4):
                        sp.wait_ge(w_lo, i * 4 + (b0 + t - NRAW + 1))
                        sp.dma_start(raw_slot(b0 + t), wv[:, :, bass.ds(i * (4 * P) + (c0 + t * P), P)]).then_inc(
                            raw_in[(b0 + t) % NRAW], 16)

            heads(B_QK, 0)
            kv = w_ukv.rearrange("(k p) (h c) -> p k h c", p=P, c=NOPE + AV)
            uq = w_uq.rearrange("(k p) (h c) -> p k h c", p=P, c=QK)

            def columns_of(b, w, nk, h0, h1, c0, c1):
                dst = raw_slot(b).rearrange("p t c -> p (t c)")
                width = (h1 - h0) * (c1 - c0)
                one(b, *((dst[:, k * width:(k + 1) * width].rearrange("p (h c) -> p h c", c=c1 - c0), w[:, k, h0:h1, c0:c1])
                         for k in range(nk)))

            columns_of(B_UKV, kv, KC, 0, AH, 0, NOPE)
            columns_of(B_UKV + 1, kv, KC, 0, AH, NOPE, NOPE + AV)
            columns_of(B_UQ, uq, KQ, 0, 4, 0, NOPE)
            columns_of(B_UQ + 1, uq, KQ, 4, AH, 0, NOPE)
            columns_of(B_UQ + 2, uq, KQ, 0, AH, NOPE, QK)
            heads(B_VO, 2 * MW)
            wo = w_out.rearrange("(k p) f -> p k f", p=P)
            with sp.Fori(0, 2) as i:
                for t in range(4):
                    sp.wait_ge(w_lo, i * 4 + (B_OUT + t - NRAW + 1))
                    sp.dma_start(raw_slot(B_OUT + t), wo[:, :, bass.ds(i * (4 * P) + t * P, P)]).then_inc(
                        raw_in[(B_OUT + t) % NRAW], 16)

        KEY_TILES = [(i * P, P) for i in range(4)] + [(SEQ, DEC), (T, P), (T + P, P)]
        FRAMES = [(i * P, P) for i in range(4)] + [(SEQ, DEC)]

        def mix1_pe(pe):
            pe.wait_ge(cache_in, 32)
            for k in range(KC):
                for t in range(2):
                    nc.tensor.transpose(PS[:, 6, (2 * k + t) * P:(2 * k + t + 1) * P], CIN[:, t, k * P:(k + 1) * P], IDENT[:])
            for t in range(2):
                last = nc.tensor.transpose(PS[0:ROPE, 7, t * P:(t + 1) * P], KIN[:, t, :], IDENT[:])
            last.then_inc(m1["cache_T"], 1)

            def tile(b, bank, m=P, first=False):
                weights_ready(pe, b)
                for k in range(KD):
                    if first:
                        h_wait(pe, pre[1], k)
                    last = product(b, k, H_HI[:, k], H_LO[:, k], bank, k == 0, k == KD - 1, m=m)
                return last

            for i in range(KQ):
                tile(B_AQ + i, 2 * i, first=i == 0).then_inc(w_used, 1)
            pe.wait_ge(m1["cache_lo"], 1)
            pe.wait_ge(m1["kr_c"], 1)
            tile(B_CKV, 6).then_inc(w_used, 1)
            pe.wait_ge(m1["proj"], 1)
            tile(B_CKV + 1, 0).then_inc(w_used, 1)
            pe.wait_ge(m1["proj"], 3)
            for i in range(KQ):
                last = sum_over_features((PAIR[:, 0], PAIR[:, 1], ACC[:])[i], 2, i == 0, i == KQ - 1)
            last.then_inc(m1["aq_sum"], 1)
            tile(B_SMALL, 4, m=64 + MH).then_inc(w_used, 1)
            pe.wait_ge(m1["proj"], 5)
            for i in range(KC):
                last = sum_over_features(TF[:, i], 6, i == 0, i == KC - 1)
            last.then_inc(m1["c_sum"], 1)

            def heads(b0, seen):
                with pe.Fori(0, 2) as i:
                    for t in range(4):
                        weights_ready(pe, i * 4 + (b0 + t))
                        pe.wait_ge(m1["proj"], i * 4 + (seen + t - 1))
                        for k in range(KD):
                            last = product(b0 + t, k, H_HI[:, k], H_LO[:, k], 2 * (t % 2), k == 0, k == KD - 1)
                        last.then_inc(w_used, 1)

            pe.wait_ge(m1["aq_root"], 1)
            heads(B_QK, 6)
            pe.wait_ge(m1["proj"], 6)
            for s in range(2):
                last = nc.tensor.matmul(PS[0:ROPE, 4 + s, 0:HT], PERM[0:ROPE, 0:ROPE], ARS[:, s * HT:(s + 1) * HT],
                                        start=True, stop=True)
            last.then_inc(m1["perm"], 1)
            pe.wait_ge(m1["c"], KC)
            pe.wait_ge(m1["c_root"], 1)
            pe.wait_ge(m1["proj"], 13)
            for t, (c, n) in enumerate(FRAMES):
                bank, off = ((6, 0), (6, 256), (7, 0), (7, 256), (0, 0))[t]
                for k in range(KC):
                    last = nc.tensor.transpose(PS[0:n, bank, off + k * P:off + (k + 1) * P], CRAW[:, k, c:c + n], IDENT[:])
            last.then_inc(m1["c_T"], 1)
            pe.wait_ge(m1["c_lo"], KC)
            pe.wait_ge(m1["cache_lo"], 1)
            weights_ready(pe, B_UKV)
            NK = TK // 2
            for n in range(AH // 2):
                if n < 2:
                    pe.wait_ge(m1["kr"] if n else m1["proj"], 1 if n else 14)
                else:
                    pe.wait_ge(m1["kn_a"], n - 1)
                    pe.wait_ge(m1["kn_d"], n - 1)
                for k in range(KC):
                    last = product(B_UKV, k * 4 + n, C_HI[:, k], C_LO[:, k], 2 + 2 * (n % 2), k == 0, k == KC - 1, n=NK)
                last.then_inc(w_used if n == AH // 2 - 1 else m1["kn_T"], 1)
            pe.wait_ge(m1["em"], 1)
            pe.wait_ge(m1["mm"], 1)
            pe.wait_ge(m1["c_staged"], 1)
            for j, src in enumerate((GR, EM)):
                for t, (c, n) in enumerate(FRAMES):
                    last = nc.tensor.transpose(PS[0:n, 7, (j * TT + t) * MH:(j * TT + t + 1) * MH], src[:, c:c + n],
                                               IDENT[0:MH, 0:MH])
            last.then_inc(m1["gate_T"], 1)
            weights_ready(pe, B_UKV + 1)
            s_w = (B_UKV + 1) % NW
            for s, (c, n) in enumerate(KEY_TILES):
                if s == 3:
                    pe.wait_ge(m1["gate_c"], 1)
                if s >= 4:
                    pe.wait_ge(m1["v_d"] if s % 2 else m1["v_a"], s // 2 - 1)
                for k in range(KC):
                    for i, (x, w) in enumerate(passes(C_HI[:, k, c:c + n], C_LO[:, k, c:c + n],
                                                      W_HI[:, s_w, 4 * k:4 * k + 4, :].rearrange("p t c -> p (t c)"),
                                                      W_LO[:, s_w, 4 * k:4 * k + 4, :].rearrange("p t c -> p (t c)"))):
                        last = nc.tensor.matmul(PS[0:n, (0, 1, 6, 7)[s % 4], :], x, w,
                                                start=k == 0 and i == 0, stop=k == KC - 1 and i == 2)
                last.then_inc(w_used if s == 6 else m1["v_T"], 1)
            pe.wait_ge(m1["cq_lo"], KQ)
            for n in range(4):
                b = B_UQ + n // 2
                weights_ready(pe, b)
                if n < 2:
                    pe.wait_ge(m1["kn_a"], n + 3)
                    pe.wait_ge(m1["kn_d"], n + 3)
                else:
                    pe.wait_ge(m1["q_a"], n - 1)
                    pe.wait_ge(m1["q_d"], n - 1)
                for k in range(KQ):
                    last = product(b, 2 * k + n % 2, CQ_HI[:, k], CQ_LO[:, k], 2 + 2 * (n % 2), k == 0, k == KQ - 1)
                last.then_inc(w_used if n % 2 else m1["q_T"], 1)
            weights_ready(pe, B_UQ + 2)
            for r in range(2):
                pe.wait_ge(m1["q_a"], r + 3)
                pe.wait_ge(m1["q_d"], r + 3)
                for k in range(KQ):
                    last = product(B_UQ + 2, 2 * k + r, CQ_HI[:, k], CQ_LO[:, k], 2 + 2 * r, k == 0, k == KQ - 1)
                last.then_inc(w_used if r else m1["q_T"], 1)
            pe.wait_ge(m1["v_a"], 4)
            pe.wait_ge(m1["v_d"], 3)
            for r in range(2):
                pe.wait_ge(m1["rs"], r + 1)
                for s in range(2):
                    last = nc.tensor.matmul(PS[:, (6, 0)[r] + s, 0:HT], PERM[:], TF[:, r, s * HT:(s + 1) * HT],
                                            start=True, stop=True)
                last.then_inc(m1["perm_q"], 1)
            pe.wait_ge(m1["qr"], 2)
            heads(B_VO, 14)
            pe.wait_ge(m1["kr"], 1)
            for t, (c, n) in enumerate(FRAMES):
                last = nc.tensor.transpose(PS[0:n, 4, t * ROPE:(t + 1) * ROPE], KR[:, c:c + n], IDENT[0:ROPE, 0:ROPE])
            last.then_inc(m1["kr_T"], 1)

        def mix1_act(act):
            act.wait_ge(m1["cache_T"], 1)
            nc.scalar.activation(C_HI[:, :, T:TK], PS[:, 6, :].rearrange("p (k t) -> p k t", k=KC),
                                 ACT.Copy).then_inc(m1["cache_hi"], 1)
            nc.scalar.activation(KR[:, T:TK], PS[0:ROPE, 7, 0:PAST], ACT.Copy).then_inc(m1["kr_c"], 1)
            for i in range(KQ):
                act.wait_ge(w_used, B_AQ + i + 1)
                nc.scalar.activation(halves(AQRAW[:, i]), pair(2 * i), ACT.Copy)
                nc.scalar.activation(halves((PAIR[:, 0], PAIR[:, 1], ACC[:])[i]), pair(2 * i),
                                     ACT.Square).then_inc(m1["proj"], 1)
                split_hi(act, B_AQ + i + 2)
            for i in range(KC):
                act.wait_ge(w_used, B_CKV + i + 1)
                nc.scalar.activation(halves(CRAW[:, i, 0:T]), pair((6, 0)[i]), ACT.Copy)
                nc.scalar.activation(halves(TF[:, i]), pair((6, 0)[i]), ACT.Square).then_inc(m1["proj"], 1)
                split_hi(act, B_CKV + i + 2)
            act.wait_ge(m1["aq_sum"], 1)
            nc.scalar.activation(halves(RB[:]), pair(2), ACT.Sqrt, bias=EPSC[:], scale=1.0 / QL).then_inc(m1["aq_root"], 1)
            act.wait_ge(w_used, B_SMALL + 1)
            nc.scalar.activation(halves(ARS[:]), pair(4, ROPE), ACT.Copy)
            nc.scalar.activation(halves(IG[:]), PS[32:32 + MH, 4:6, 0:HT], ACT.Copy)
            nc.scalar.activation(halves(LF[:]), PS[64:64 + MH, 4:6, 0:HT], ACT.Copy).then_inc(m1["proj"], 1)
            split_hi(act, B_SMALL + 2)
            act.wait_ge(m1["c_sum"], 1)
            nc.scalar.activation(halves(PAIR[:, 0]), pair(6), ACT.Sqrt, bias=EPSC[:], scale=1.0 / KVL).then_inc(m1["c_root"], 1)
            act.wait_ge(m1["lf1"], 1)
            settle(act, "act", act_step, nc.scalar.activation(GR[:], LF[:], ACT.Abs))
            settle(act, "act", act_step, nc.scalar.activation(GR[:], GR[:], ACT.Exp, scale=-1.0))
            nc.scalar.activation(GR[:], GR[:], ACT.Ln, bias=1.0).then_inc(m1["soft"], 1)

            def heads(b0, dst):
                with act.Fori(0, 2) as i:
                    for t in range(4):
                        act.wait_ge(w_used, i * 4 + (b0 + t + 1))
                        nc.scalar.activation(halves(dst[:, bass.ds(i * 4 + t, 1), :].rearrange("p a t -> p (a t)")),
                                             pair(2 * (t % 2)), ACT.Copy).then_inc(m1["proj"], 1)
                        split_hi(act, b0 + t + 2, 8, i * 4 + (b0 + t + 2), i * 16 + arrived(b0 + t + 2))

            for n in range(2 * MH):
                act.wait_ge(w_used, B_QK + n + 1)
                nc.scalar.activation(halves(PJ1[:, n]), pair(2 * (n % 2)), ACT.Copy).then_inc(m1["proj"], 1)
                split_hi(act, B_QK + n + 2)
            act.wait_ge(m1["c_T"], 1)
            nc.scalar.activation(CSTAGE[:, 0:4], PS[:, 6:8, :].rearrange("p b (t c) -> p (b t) c", t=2), ACT.Copy)
            nc.scalar.activation(CSTAGE[0:DEC, 4], PS[0:DEC, 0, 0:KVL], ACT.Copy).then_inc(m1["c_staged"], 1)
            act.wait_ge(m1["mm"], 1)
            nc.scalar.activation(EM[:], MX[:], ACT.Exp, scale=-1.0).then_inc(m1["em"], 1)
            act.wait_ge(m1["c_stored"], 32)
            for n in range(AH // 2):
                act.wait_ge(w_used if n == 3 else m1["kn_T"], B_UKV + 1 if n == 3 else n + 1)
                nc.scalar.activation(halves(KH[0:NOPE, 2 * n], TK // 2), pair(2 + 2 * (n % 2), NOPE, TK // 2),
                                     ACT.Copy).then_inc(m1["kn_a"], 1)
            split_hi(act, B_UKV + 2, 6)
            act.wait_ge(m1["gate_T"], 1)
            nc.scalar.activation(GC[:, 0:4], PS[:, 7, 0:16].rearrange("p (t h) -> p t h", h=MH), ACT.Copy)
            nc.scalar.activation(GC[0:DEC, 4], PS[0:DEC, 7, 16:20], ACT.Copy)
            nc.scalar.activation(EMC[:, 0:4], PS[:, 7, 20:36].rearrange("p (t h) -> p t h", h=MH), ACT.Copy)
            nc.scalar.activation(EMC[0:DEC, 4], PS[0:DEC, 7, 36:40], ACT.Copy).then_inc(m1["gate_c"], 1)
            for s in range(0, 7, 2):
                n = KEY_TILES[s][1]
                act.wait_ge(w_used if s == 6 else m1["v_T"], B_UKV + 2 if s == 6 else s + 1)
                nc.scalar.activation(VA[0:n, s, 0:AH * AV], PS[0:n, (0, 1, 6, 7)[s % 4], :], ACT.Copy).then_inc(m1["v_a"], 1)
            split_hi(act, B_UKV + 3, 6)
            for n in range(4):
                act.wait_ge(w_used if n % 2 else m1["q_T"], B_UQ + n // 2 + 1 if n % 2 else n // 2 + 1)
                nc.scalar.activation(halves(QH[0:NOPE, 2 * n]), pair(2 + 2 * (n % 2), NOPE), ACT.Copy).then_inc(m1["q_a"], 1)
                if n % 2:
                    split_hi(act, B_UQ + n // 2 + 2, 6 if n == 1 else 8)
            for r in range(2):
                act.wait_ge(w_used if r else m1["q_T"], B_UQ + 3 if r else 3)
                nc.scalar.activation(halves(TF[:, r]), pair(2 + 2 * r), ACT.Copy).then_inc(m1["rs"], 1)
            split_hi(act, B_VO + 1)
            heads(B_VO, PJ2)
            act.wait_ge(m1["kr_T"], 1)
            act.wait_ge(m1["rope_in"], 1)
            nc.scalar.activation(KSTAGE[:, 0:4], PS[:, 4, 0:4 * ROPE].rearrange("p (t c) -> p t c", c=ROPE), ACT.Copy)
            nc.scalar.activation(KSTAGE[0:DEC, 4], PS[0:DEC, 4, 4 * ROPE:5 * ROPE], ACT.Copy).then_inc(m1["kr_staged"], 1)

        def mix1_dve(dve):
            dve.wait_ge(m1["cache_hi"], 1)
            nc.vector.tensor_tensor(C_LO[:, :, T:TK], PS[:, 6, :].rearrange("p (k t) -> p k t", k=KC),
                                    C_HI[:, :, T:TK].bitcast(F32), ALU.subtract).then_inc(m1["cache_lo"], 1)
            for b in range(B_AQ + 2, B_SMALL + 1):
                split_lo(dve, b)
            split_lo(dve, B_SMALL + 1)

            def normed(raw, r, gain, n, done):
                settle(dve, "dve", dve_step, nc.vector.reciprocal(r, r))
                for i in range(n):
                    g = GROW[gain] + i
                    nc.vector.scalar_tensor_tensor(out=raw(i), in0=raw(i), scalar=GCOLS[:, g:g + 1], in1=r,
                                                   op0=ALU.mult, op1=ALU.mult).then_inc(done, 1)

            dve.wait_ge(m1["aq_root"], 1)
            normed(lambda i: AQRAW[:, i], RB[:], "q_a_g", KQ, m1["cq"])
            split_lo(dve, B_SMALL + 2)
            dve.wait_ge(m1["c_root"], 1)
            normed(lambda i: CRAW[:, i, 0:T], PAIR[:, 0], "kv_a_g", KC, m1["c"])

            def heads(b0):
                with dve.Fori(0, 2) as i:
                    for t in range(4):
                        split_lo(dve, b0 + t + 2, 8, i * 4 + (b0 + t + 2))

            heads(B_QK)
            dve.wait_ge(m1["perm"], 1)
            dve.wait_ge(trig_in, 16)
            settle(dve, "dve", dve_step, nc.vector.tensor_tensor(PAIR[0:ROPE, 1], ARS[:], TRIG[0:ROPE, 0], ALU.mult))
            settle(dve, "dve", dve_step, nc.vector.tensor_tensor(
                halves(KR[:, 0:T]), pair(4, ROPE), halves(TRIG[0:ROPE, 1]), ALU.mult))
            nc.vector.tensor_tensor(KR[:, 0:T], KR[:, 0:T], PAIR[0:ROPE, 1], ALU.add).then_inc(m1["kr"], 1)
            dve.wait_ge(m1["lf"], 1)
            for lo, hi in ((0, SEQ), (SEQ, T)):
                last = nc.vector.tensor_tensor_scan(out=BC[:, lo:hi], data0=ONES4[:, lo:hi], data1=LF[:, lo:hi],
                                                    initial=0.0, op0=ALU.mult, op1=ALU.add)
            settle(dve, "dve", dve_step, last)
            settle(dve, "dve", dve_step, nc.vector.tensor_tensor(GR[:], IG[:], BC[:], ALU.subtract))
            nc.vector.tensor_tensor_scan(out=MX[:, 0:SEQ], data0=GR[:, 0:SEQ], data1=GR[:, 0:SEQ],
                                         initial=0.0, op0=ALU.max, op1=ALU.max)
            dve.wait_ge(bias_in, 64)
            settle(dve, "dve", dve_step, nc.vector.tensor_tensor_scan(
                out=MX[:, SEQ:T], data0=GR[:, SEQ:T], data1=GR[:, SEQ:T], initial=BIAS[:, 2:3], op0=ALU.max, op1=ALU.max))
            nc.vector.tensor_scalar(NM[:], MX[:], -1.0, None, ALU.mult)
            settle(dve, "dve", dve_step, nc.vector.tensor_tensor(MX[:], MX[:], BC[:], ALU.add))
            nc.vector.tensor_copy(MEND[:, 0:1], MX[:, SEQ - 1:SEQ])
            nc.vector.tensor_copy(MEND[:, 1:2], MX[:, T - 1:T]).then_inc(m1["mm"], 1)
            dve.wait_ge(m1["c_stored"], 32)
            for n in range(AH // 2):
                dve.wait_ge(w_used if n == 3 else m1["kn_T"], B_UKV + 1 if n == 3 else n + 1)
                nc.vector.tensor_copy(halves(KH[0:NOPE, 2 * n + 1], TK // 2),
                                      PS[NOPE:P, 2 + 2 * (n % 2):4 + 2 * (n % 2), 0:TK // 2]).then_inc(m1["kn_d"], 1)
            split_lo(dve, B_UKV + 2, 6)
            dve.wait_ge(m1["gate_T"], 1)
            nc.vector.memset(VA[:, :, AH * AV:VAW], 0.0)
            for s in range(1, 7, 2):
                n = KEY_TILES[s][1]
                dve.wait_ge(m1["v_T"], s + 1)
                nc.vector.tensor_copy(VA[0:n, s, 0:AH * AV], PS[0:n, (0, 1, 6, 7)[s % 4], :]).then_inc(m1["v_d"], 1)
            split_lo(dve, B_UKV + 3, 6)
            for n in range(4):
                dve.wait_ge(w_used if n % 2 else m1["q_T"], B_UQ + n // 2 + 1 if n % 2 else n // 2 + 1)
                nc.vector.tensor_copy(halves(QH[0:NOPE, 2 * n + 1]),
                                      PS[NOPE:P, 2 + 2 * (n % 2):4 + 2 * (n % 2), 0:HT]).then_inc(m1["q_d"], 1)
                if n % 2:
                    split_lo(dve, B_UQ + n // 2 + 2, 6 if n == 1 else 8)
            split_lo(dve, B_VO + 1)
            for r in range(2):
                dve.wait_ge(m1["rs"], r + 1)
                settle(dve, "dve", dve_step, nc.vector.tensor_tensor(PAIR[:, r], TF[:, r], TRIG[:, 0], ALU.mult))
                dve.wait_ge(m1["perm_q"], r + 1)
                settle(dve, "dve", dve_step, nc.vector.tensor_tensor(
                    halves(RB[:]), pair((6, 0)[r]), halves(TRIG[:, 1]), ALU.mult))
                nc.vector.tensor_tensor(PAIR[:, r], PAIR[:, r], RB[:], ALU.add).then_inc(m1["qr"], 1)
            heads(B_VO)

        def mix1_pool(pool):
            pool.wait_ge(w_used, MIX0)
            pool.dma_start(CIN[:], a["cache_kv_latent"][0, 0].rearrange("(t p) c -> p t c", p=P)).then_inc(cache_in, 16)
            pool.dma_start(KIN[:], a["cache_k_rope"][0, 0].rearrange("(t p) c -> p t c", p=P)).then_inc(cache_in, 16)

            def split(src, hi, lo, done):
                settle(pool, "pool", pool_step, nc.gpsimd.tensor_copy(hi, src))
                nc.gpsimd.tensor_tensor(lo, src, hi.bitcast(F32), ALU.subtract).then_inc(done, 1)

            pool.wait_ge(m1["proj"], 6)
            pool.wait_ge(bias_in, 64)
            settle(pool, "pool", pool_step, nc.gpsimd.tensor_scalar(IG[:], IG[:], BIAS[:, 0:1], None, ALU.add))
            nc.gpsimd.memset(ONES4[:], 1.0)
            nc.gpsimd.tensor_scalar(LF[:], LF[:], BIAS[:, 1:2], None, ALU.add).then_inc(m1["lf1"], 1)
            pool.wait_ge(m1["soft"], 1)
            settle(pool, "pool", pool_step, nc.gpsimd.tensor_scalar(LF[:], LF[:], 0.0, None, ALU.min))
            nc.gpsimd.tensor_tensor(LF[:], LF[:], GR[:], ALU.subtract).then_inc(m1["lf"], 1)
            for i in range(KQ):
                pool.wait_ge(m1["cq"], i + 1)
                split(AQRAW[:, i], CQ_HI[:, i], CQ_LO[:, i], m1["cq_lo"])
            for i in range(KC):
                pool.wait_ge(m1["c"], i + 1)
                split(CRAW[:, i, 0:T], C_HI[:, i, 0:T], C_LO[:, i, 0:T], m1["c_lo"])
            pool.wait_ge(m1["proj"], 14)
            nc.gpsimd.tensor_scalar(PJ1[:, MH:2 * MH], PJ1[:, MH:2 * MH], P ** -0.5, None, ALU.mult).then_inc(m1["k_scaled"], 1)
            pool.wait_ge(m1["c_staged"], 1)
            pool.dma_start(p_kv[0, 0].rearrange("(t p) c -> p t c", p=P), CSTAGE[:, 0:4]).then_inc(m1["c_stored"], 16)
            pool.dma_start(s_kv[0, 0], CSTAGE[0:DEC, 4]).then_inc(m1["c_stored"], 16)
            pool.wait_ge(m1["mm"], 1)
            pool.dma_start(p_m[0].rearrange("b h -> h b"), MEND[:, 0:1]).then_inc(st["stored"], 16)
            pool.dma_start(s_m[0].rearrange("b h -> h b"), MEND[:, 1:2]).then_inc(st["stored"], 16)
            pool.wait_ge(m1["c_stored"], 32)
            pool.wait_ge(m1["kr"], 1)
            pool.wait_ge(m1["k_scaled"], 1)
            for h in range(AH):
                settle(pool, "pool", pool_step, nc.gpsimd.tensor_copy(KH[NOPE:QK, h], KR[:]))
            for h in range(AH):
                if h % 4 == 0:
                    pool.wait_ge(m1["qr"], h // 4 + 1)
                settle(pool, "pool", pool_step, nc.gpsimd.tensor_copy(
                    QH[NOPE:QK, h], PAIR[(h % 4) * ROPE:(h % 4 + 1) * ROPE, h // 4]))
            pool.sem_inc(m1["rope_in"], 1)
            pool.wait_ge(m1["kr_staged"], 1)
            pool.dma_start(p_kr[0, 0].rearrange("(t p) c -> p t c", p=P), KSTAGE[:, 0:4]).then_inc(st["stored"], 16)
            pool.dma_start(s_kr[0, 0], KSTAGE[0:DEC, 4]).then_inc(st["stored"], 16)

        m2 = names("m2", "v_T", "k_T", "v_c", "k_c", "c0_T", "c0_c", "ones_v", "nb_T", "nb", "we", "s_T", "arg", "dexp",
                   "tri", "wgt", "o_T", "os", "sq", "var", "root", "hn", "h_T", "mf", "hi", "lo", "vw", "qw", "st_T",
                   "st_c", "st_v", "sig", "state_out")
        DOFF = {0: 0, 1: 512, 3: 896, 2: 1024, 4: 1280}
        DLEN = {i: SEQ - i * P for i in range(4)}
        DLEN[4] = DEC

        def nb_of(h):
            return RB[:] if h % 2 == 0 else PAIR[:, 0]

        def mix2_pe(pe):
            pe.wait_ge(m1["proj"], 22)
            for t, (c, n) in enumerate(FRAMES):
                for h in range(MH):
                    last = nc.tensor.transpose(PS[0:n, t, h * P:(h + 1) * P], PJ2[:, h, c:c + n], IDENT[:])
                last.then_inc(m2["v_T"], 1)
                if t == 0:
                    pe.wait_ge(m1["kr_staged"], 1)
            pe.wait_ge(m1["k_scaled"], 1)
            for t, (c, n) in enumerate(FRAMES):
                if t >= 3:
                    pe.wait_ge(m2["v_c"], t - 2)
                for h in range(MH):
                    last = nc.tensor.transpose(PS[0:n, (5 + t) % 8, h * P:(h + 1) * P], PJ1[:, MH + h, c:c + n], IDENT[:])
                last.then_inc(m2["k_T"], 1)
            pe.wait_ge(state_in, 48)
            pe.wait_ge(m2["v_c"], 4)
            for h in range(MH):
                nc.tensor.transpose(PS[:, 2, h * P:(h + 1) * P], C0[:, h, :], IDENT[:])
            nc.tensor.transpose(PS[:, 3, 0:MH], N0R[:], IDENT[0:MH, 0:MH]).then_inc(m2["c0_T"], 1)
            pe.wait_ge(m2["c0_c"], 1)
            pe.wait_ge(m2["v_c"], TT)
            pe.wait_ge(m2["k_c"], TT)

            def scores(h):
                for s in range(2):
                    last = nc.tensor.matmul(PS[:, 3 + s, 0:HT], SEL[:, h, :], NM[:, s * HT:(s + 1) * HT], start=True, stop=True)
                last.then_inc(m2["nb_T"], 1)
                if h:
                    pe.wait_ge(m2["wgt"], h)
                for i, (c, n) in enumerate(FRAMES):
                    last = nc.tensor.matmul(PSF[0:n, DOFF[i]:DOFF[i] + DLEN[i]], PJ1[:, MH + h, c:c + n],
                                            PJ1[:, h, c:(SEQ if i < 4 else T)], start=True, stop=True)
                last.then_inc(m2["s_T"], 1)

            def outputs(h):
                pe.wait_ge(m2["wgt"], h + 1)
                pe.wait_ge(m2["ones_v"], 1)
                if h:
                    pe.wait_ge(m2["os"], h)
                for j in range(4):
                    dst = PS[:, 5 + j // 3, (j % 3) * VP:(j % 3 + 1) * VP]
                    for i in range(j + 1):
                        nc.tensor.matmul(dst, DW[:, DOFF[i] + (j - i) * P:DOFF[i] + (j - i + 1) * P], VT[:, i, h, :],
                                         start=i == 0, stop=i == j)
                dst = PS[0:DEC, 6, VP:2 * VP]
                nc.tensor.matmul(dst, DW[0:DEC, DOFF[4]:DOFF[4] + DEC], VT[0:DEC, 4, h, :], start=True, stop=False)
                pe.wait_ge(m2["qw"], h + 1)
                nc.tensor.matmul(dst, PAIR[:, 1, DEC:2 * DEC], C0T[:, h, :], start=False, stop=True).then_inc(m2["o_T"], 1)

            def states(h):
                pe.wait_ge(m2["vw"], h + 1)
                if h:
                    pe.wait_ge(m2["st_c"], h)
                    pe.wait_ge(m2["st_v"], h)
                for i in range(4):
                    nc.tensor.matmul(PS[:, 7, 0:P], VW[:, i, :], KT[:, i, h, :], start=i == 0, stop=i == 3)
                nc.tensor.matmul(PS[:, 7, P:2 * P], VW[0:DEC, 4, :], KT[0:DEC, 4, h, :], start=True, stop=True)
                for i in range(4):
                    nc.tensor.matmul(PS[0:1, 7, 2 * P:3 * P], WE[:, i:i + 1], KT[:, i, h, :], start=i == 0, stop=i == 3)
                nc.tensor.matmul(PS[0:1, 7, 3 * P:4 * P], WE[0:DEC, 4:5], KT[0:DEC, 4, h, :],
                                 start=True, stop=True).then_inc(m2["st_T"], 1)

            def back(h):
                pe.wait_ge(m2["hn"], h + 1)
                for t, (c, n) in enumerate(FRAMES):
                    last = nc.tensor.transpose(PSF[:, 3 * 512 + c:3 * 512 + c + n], HN[0:n, t, :], IDENT[0:n, 0:n])
                last.then_inc(m2["h_T"], 1)

            scores(0)
            for h in range(MH):
                outputs(h)
                states(h)
                if h + 1 < MH:
                    if h:
                        pe.wait_ge(m2["mf"], h)
                    scores(h + 1)
                    pe.wait_ge(m2["nb"], h + 2)
                back(h)

        def mix2_act(act):
            for t, (c, n) in enumerate(FRAMES):
                act.wait_ge(m2["v_T"], t + 1)
                nc.scalar.activation(VT[0:n, t, :, 0:P], PS[0:n, t, :].rearrange("p (h v) -> p h v", h=MH),
                                     ACT.Copy).then_inc(m2["v_c"], 1)
            act.wait_ge(m2["c0_T"], 1)
            nc.scalar.activation(C0T[:, :, 0:P], PS[:, 2, :].rearrange("p (h v) -> p h v", h=MH), ACT.Copy)
            for i in range(2):
                last = nc.scalar.activation(C0T[:, :, P + i], PS[:, 3, 0:MH], ACT.Copy)
            last.then_inc(m2["c0_c"], 1)
            act.wait_ge(m1["proj"], 22)
            nc.scalar.activation(PJ2[:, MH:2 * MH], PJ2[:, MH:2 * MH], ACT.Sigmoid).then_inc(m2["sig"], 1)
            act.wait_ge(m2["ones_v"], 1)

            def decays(h):
                nb = nb_of(h)
                act.wait_ge(m2["nb_T"], h + 1)
                if h >= 1:
                    act.wait_ge(m2["qw"], h)
                    act.wait_ge(m2["o_T"], h)
                    act.wait_ge(m2["vw"], h)
                    act.wait_ge(m2["st_T"], h)
                    act.wait_ge(m2["st_v"], h)
                settle(act, "act", act_step, nc.scalar.activation(halves(nb), pair(3), ACT.Copy))
                nc.scalar.activation(PAIR[:, 1, 0:DEC], nb[:, SEQ:T], ACT.Exp, bias=M0B[:, h:h + 1]).then_inc(m2["nb"], 1)
                nc.scalar.activation(WE[:, 0:4], GC[:, 0:4, h], ACT.Exp, bias=nb[:, SEQ - 1:SEQ])
                nc.scalar.activation(WE[0:DEC, 4:5], GC[0:DEC, 4, h:h + 1], ACT.Exp,
                                     bias=nb[0:DEC, T - 1:T]).then_inc(m2["we"], 1)
                act.wait_ge(m2["arg"], h + 1)
                nc.scalar.activation(DW[:, 0:1280], DW[:, 0:1280], ACT.Exp)
                nc.scalar.activation(DW[0:DEC, 1280:1344], DW[0:DEC, 1280:1344], ACT.Exp).then_inc(m2["dexp"], 1)

            decays(0)
            for h in range(MH):
                act.wait_ge(m2["o_T"], h + 1)
                if h:
                    act.wait_ge(m2["hn"], h)
                nc.scalar.activation(OS[:, 0:3], PS[:, 5, 0:3 * VP].rearrange("p (t v) -> p t v", t=3), ACT.Copy)
                nc.scalar.activation(OS[:, 3], PS[:, 6, 0:VP], ACT.Copy)
                settle(act, "act", act_step, nc.scalar.activation(OS[0:DEC, 4], PS[0:DEC, 6, VP:2 * VP], ACT.Copy))
                act.sem_inc(m2["os"], 1)
                if h:
                    act.wait_ge(m2["h_T"], h)
                nc.scalar.activation(HN[:], OS[:, :, 0:P], ACT.Square).then_inc(m2["sq"], 1)
                act.wait_ge(m2["st_T"], h + 1)
                if h >= 2:
                    act.wait_ge(m2["state_out"], 64 * (h - 1))
                nc.scalar.activation(CN[:, h % 2, 0], PS[:, 7, 0:P], ACT.Copy)
                if h:
                    act.wait_ge(m2["state_out"], 64 * h)
                nc.scalar.activation(NN[:, 0], PS[0:1, 7, 2 * P:3 * P], ACT.Copy).then_inc(m2["st_c"], 1)
                act.wait_ge(m2["var"], h + 1)
                nc.scalar.activation(S5[:, 3], S5[:, 2], ACT.Sqrt, bias=EPSC[:], scale=1.0 / P).then_inc(m2["root"], 1)
                if h + 1 < MH:
                    decays(h + 1)
                act.wait_ge(m2["mf"], h + 1)
                nc.scalar.activation(MA_HI[:, h], TF[:, h % 2], ACT.Copy).then_inc(m2["hi"], 1)

        def mix2_dve(dve):
            for t, (c, n) in enumerate(FRAMES):
                dve.wait_ge(m2["k_T"], t + 1)
                nc.vector.tensor_copy(KT[0:n, t], PS[0:n, (5 + t) % 8, :].rearrange("p (h v) -> p h v", h=MH)).then_inc(m2["k_c"], 1)
            dve.wait_ge(m2["ones_v"], 1)

            def args(h):
                nb = nb_of(h)
                dve.wait_ge(m2["nb"], h + 1)
                nc.vector.tensor_tensor(PAIR[:, 1, DEC:2 * DEC], PJ1[:, h, SEQ:T], PAIR[:, 1, 0:DEC], ALU.mult).then_inc(m2["qw"], 1)
                if h:
                    dve.wait_ge(m2["o_T"], h)
                for i, (c, n) in enumerate(FRAMES):
                    end = SEQ if i < 4 else T
                    last = nc.vector.tensor_scalar(DW[0:n, DOFF[i]:DOFF[i] + DLEN[i]], nb[0:n, c:end],
                                                   GC[0:n, i, h:h + 1], 0.0, ALU.add, ALU.min)
                last.then_inc(m2["arg"], 1)

            def weights(h):
                dve.wait_ge(m2["tri"], h + 1)
                dve.wait_ge(m2["s_T"], h + 1)
                nc.vector.tensor_tensor(DW[:, 0:1280], DW[:, 0:1280], PSF[:, 0:1280], ALU.mult)
                nc.vector.tensor_tensor(DW[0:DEC, 1280:1344], DW[0:DEC, 1280:1344], PSF[0:DEC, 1280:1344],
                                        ALU.mult).then_inc(m2["wgt"], 1)

            args(0)
            weights(0)
            for h in range(MH):
                dve.wait_ge(m2["sq"], h + 1)
                den = OS[:, :, P:P + 1].rearrange("p t o -> p (t o)")
                settle(dve, "dve", dve_step, nc.vector.tensor_scalar(S5[:, 0], den, -1.0, None, ALU.mult))
                settle(dve, "dve", dve_step, nc.vector.tensor_tensor(S5[:, 0], S5[:, 0], den, ALU.max))
                settle(dve, "dve", dve_step, nc.vector.tensor_tensor(S5[:, 0], S5[:, 0], EMC[:, :, h], ALU.max))
                settle(dve, "dve", dve_step, nc.vector.reciprocal(S5[:, 1], S5[:, 0]))
                settle(dve, "dve", dve_step, nc.vector.tensor_reduce(S5[:, 2], HN[:], AX, ALU.add))
                settle(dve, "dve", dve_step, nc.vector.tensor_tensor(S5[:, 2], S5[:, 2], S5[:, 1], ALU.mult))
                nc.vector.tensor_tensor(S5[:, 2], S5[:, 2], S5[:, 1], ALU.mult).then_inc(m2["var"], 1)
                dve.wait_ge(m2["st_c"], h + 1)
                if h >= 2:
                    dve.wait_ge(m2["state_out"], 64 * (h - 1))
                wst = PAIR[:, 1, DEC - 1:DEC]
                nc.vector.scalar_tensor_tensor(out=CN[:, h % 2, 1], in0=C0[:, h, :], scalar=wst, in1=PS[:, 7, P:2 * P],
                                               op0=ALU.mult, op1=ALU.add)
                if h:
                    dve.wait_ge(m2["state_out"], 64 * h)
                nc.vector.scalar_tensor_tensor(out=NN[:, 1], in0=N0[:, h, :], scalar=wst[0:1], in1=PS[0:1, 7, 3 * P:4 * P],
                                               op0=ALU.mult, op1=ALU.add).then_inc(m2["st_v"], 1)
                if h + 1 < MH:
                    args(h + 1)
                dve.wait_ge(m2["root"], h + 1)
                settle(dve, "dve", dve_step, nc.vector.reciprocal(S5[:, 4], S5[:, 3]))
                settle(dve, "dve", dve_step, nc.vector.tensor_tensor(S5[:, 4], S5[:, 4], S5[:, 1], ALU.mult))
                nc.vector.tensor_tensor(HN[:], OS[:, :, 0:P], S5[:, 4:5, :].rearrange("p o t -> p t o").to_broadcast([P, TT, P]),
                                        ALU.mult).then_inc(m2["hn"], 1)
                if h + 1 < MH:
                    weights(h + 1)
                dve.wait_ge(m2["h_T"], h + 1)
                dve.wait_ge(m2["sig"], 1)
                if h >= 2:
                    dve.wait_ge(m2["lo"], h - 1)
                g = GROW["m_head_g"] + h
                nc.vector.scalar_tensor_tensor(out=TF[:, h % 2], in0=PSF[:, 3 * 512:3 * 512 + T], scalar=GCOLS[:, g:g + 1],
                                               in1=PJ2[:, MH + h], op0=ALU.mult, op1=ALU.mult).then_inc(m2["mf"], 1)

        def mix2_pool(pool):
            pool.wait_ge(w_used, B_OUT)
            pool.dma_start(C0[:], a["state_C"][0, 0].rearrange("h v k -> v h k")).then_inc(state_in, 16)
            pool.dma_start(N0R[:], a["state_n"][0, 0]).then_inc(state_in, 16)
            pool.wait_ge(m1["kr_T"], 1)
            pool.dma_start(N0[:], a["state_n"][0, 0:1]).then_inc(state_in, 16)
            nc.gpsimd.memset(VT[:, :, :, P:VP], 1.0)
            nc.gpsimd.memset(OS[:], 1.0).then_inc(m2["ones_v"], 1)

            def low(h):
                pool.wait_ge(m2["hi"], h + 1)
                nc.gpsimd.tensor_tensor(MA_LO[:, h], TF[:, h % 2], MA_HI[:, h].bitcast(F32), ALU.subtract).then_inc(m2["lo"], 1)

            for h in range(MH):
                pool.wait_ge(m2["dexp"], h + 1)
                for i in (0, 1, 2, 3, 4):
                    n = FRAMES[i][1]
                    blk = DW[0:n, DOFF[i]:DOFF[i] + n]
                    last = nc.gpsimd.affine_select(out=blk, in_=blk, compare_op=ALU.is_ge, fill=0.0, base=0,
                                                   pattern=[[1, n]], channel_multiplier=-1)
                last.then_inc(m2["tri"], 1)
                pool.wait_ge(m2["we"], h + 1)
                pool.wait_ge(m2["v_c"], TT)
                if h:
                    pool.wait_ge(m2["st_T"], h)
                for i, (c, n) in enumerate(FRAMES):
                    last = nc.gpsimd.tensor_scalar(VW[0:n, i], VT[0:n, i, h, 0:P], WE[0:n, i:i + 1], None, ALU.mult)
                last.then_inc(m2["vw"], 1)
                if h:
                    low(h - 1)
                pool.wait_ge(m2["st_c"], h + 1)
                pool.wait_ge(m2["st_v"], h + 1)
                pool.dma_start(p_C[0, 0, h], CN[:, h % 2, 0]).then_inc(m2["state_out"], 16)
                pool.dma_start(s_C[0, 0, h], CN[:, h % 2, 1]).then_inc(m2["state_out"], 16)
                pool.dma_start(p_n[0, 0, h:h + 1, :], NN[:, 0]).then_inc(m2["state_out"], 16)
                pool.dma_start(s_n[0, 0, h:h + 1, :], NN[:, 1]).then_inc(m2["state_out"], 16)
            low(MH - 1)

        m3 = names("m3", "s", "max", "bias", "p", "p_T", "pt_a", "pt_d", "o", "at", "a_T", "hi", "lo")
        SOFF = {3: 0, 2: 512, 0: 896, 1: 1024, 4: 1536}
        POFF = {3: 0, 2: 512, 0: 896, 1: 1024, 4: 1280}
        SLEN = {0: P, 1: 2 * P, 2: 3 * P, 3: 4 * P, 4: DEC + PAST}
        GROUP_A = [(3, i * P, P, i) for i in range(4)]
        GROUP_B = [(2, i * P, P, i) for i in range(3)] + [(0, 0, P, 0)]
        GROUP_C = [(1, 0, P, 0), (1, P, P, 1), (4, DEC, P, 5), (4, DEC + P, P, 6), (4, 0, DEC, 4)]

        def rows_of(j):
            return DEC if j == 4 else P

        def columns(group, base):
            out, at_ = [], base
            for blk in group:
                out.append((*blk, at_))
                at_ += rows_of(blk[0])
            return out

        BLOCKS = [columns(GROUP_A, 0), columns(GROUP_B, 512), columns(GROUP_C, 1024)]

        def mix3_pe(pe):
            pe.wait_ge(m2["wgt"], MH)
            pe.wait_ge(m2["mf"], MH)
            pe.wait_ge(m1["rope_in"], 1)

            def scores(h):
                if h:
                    pe.wait_ge(m3["p"], h)
                for j in (3, 2, 0, 1, 4):
                    n = rows_of(j)
                    k0 = SEQ if j == 4 else 0
                    last = nc.tensor.matmul(PSF[0:n, SOFF[j]:SOFF[j] + SLEN[j]], QH[:, h, j * P:j * P + n],
                                            KH[:, h, k0:k0 + SLEN[j]], start=True, stop=True)
                last.then_inc(m3["s"], 1)

            def turn(h):
                pe.wait_ge(m3["p"], h + 1)
                for g, bank in enumerate((4, 5, 4)):
                    if g == 2:
                        pe.wait_ge(m3["pt_d"], 2 * h + 1)
                    elif h:
                        pe.wait_ge(m3["pt_a"] if g else m3["pt_d"], h if g else 2 * h)
                        if g == 0 and h >= 3 and h % 2:
                            pe.wait_ge(m3["lo"], h // 2)
                    at_ = 0
                    for j, k0, kn, _, _ in BLOCKS[g]:
                        n = rows_of(j)
                        last = nc.tensor.transpose(PS[0:kn, bank, at_:at_ + n], PR[0:n, h % 2, POFF[j] + k0:POFF[j] + k0 + kn],
                                                   IDENT[0:n, 0:n])
                        at_ += n
                    last.then_inc(m3["p_T"], 1)

            def values(h):
                pe.wait_ge(m3["pt_d"], 2 * h + 2)
                pe.wait_ge(m3["pt_a"], h + 1)
                if h >= 2:
                    pe.wait_ge(m3["at"], h - 1)
                for j in range(TT):
                    blks = [b for g in BLOCKS for b in g if b[0] == j]
                    n = rows_of(j)
                    for i, (_, _, kn, kt, col) in enumerate(blks):
                        last = nc.tensor.matmul(PS[0:n, 6 + h % 2, 96 * j:96 * (j + 1)], PT[0:kn, h % 2, col:col + n],
                                                VA[0:kn, kt, AV * h:AV * h + 96], start=i == 0, stop=i == len(blks) - 1)
                last.then_inc(m3["o"], 1)

            def merge(c):
                pe.wait_ge(m3["at"], 2 * c + 2)
                for t, (f, n) in enumerate(FRAMES):
                    if t == 0:
                        pe.wait_ge(m3["pt_d"], 2 * min(2 * c + 2, AH - 1) + 2)
                        pe.wait_ge(m3["pt_a"], min(2 * c + 2, AH - 1) + 1)
                    last = nc.tensor.transpose(PSF[:, 4 * 512 + f:4 * 512 + f + n], AT[0:n, t, :], IDENT[0:n, 0:n])
                last.then_inc(m3["a_T"], 1)

            scores(0)
            for h in range(AH):
                turn(h)
                if h + 1 < AH:
                    scores(h + 1)
                if h and h % 2 == 0:
                    merge(h // 2 - 1)
                values(h)
            merge(AH // 2 - 1)

        def mix3_dve(dve):
            def softmax_max(h):
                dve.wait_ge(m3["s"], h + 1)
                if h:
                    dve.wait_ge(m3["p"], h)
                for j in range(4):
                    c = SOFF[j] + SLEN[j]
                    last = nc.vector.memset(PSF[0:DEC, c - DEC:c], MASKED)
                settle(dve, "dve", dve_step, last)
                for j in range(TT):
                    n = rows_of(j)
                    last = nc.vector.tensor_reduce(S5[0:n, 0, j:j + 1], PSF[0:n, SOFF[j]:SOFF[j] + SLEN[j]], AX, ALU.max,
                                                   negate=True)
                settle(dve, "dve", dve_step, last)
                nc.vector.tensor_scalar(S5[:, 1 + 4 * (h % 2)], S5[:, 0], A_SCALE, None, ALU.mult).then_inc(m3["bias"], 1)

            def turned(h, first):
                if h >= 2:
                    dve.wait_ge(m3["o"], h - 1)
                if first:
                    dve.wait_ge(m3["p_T"], 3 * h + 1)
                    nc.vector.tensor_copy(PT[:, h % 2, 0:512], PS[:, 4, :]).then_inc(m3["pt_d"], 1)
                else:
                    dve.wait_ge(m3["p_T"], 3 * h + 3)
                    nc.vector.tensor_copy(PT[:, h % 2, 1024:1408], PS[:, 4, 0:384])
                    nc.vector.tensor_copy(PT[0:DEC, h % 2, 1408:1472], PS[0:DEC, 4, 384:448]).then_inc(m3["pt_d"], 1)

            softmax_max(0)
            for h in range(AH):
                turned(h, True)
                turned(h, False)
                if h + 1 < AH:
                    softmax_max(h + 1)
                if h and h % 2 == 0:
                    low(dve, h // 2 - 1)
                dve.wait_ge(m3["o"], h + 1)
                sums = S5[:, 2 + 4 * (h % 2)]
                settle(dve, "dve", dve_step, nc.vector.reciprocal(S5[:, 3], sums))
                if h >= 2 and h % 2 == 0:
                    dve.wait_ge(m3["a_T"], h // 2)
                o_ = PS[:, 6 + h % 2, 0:480].rearrange("p (t v) -> p t v", v=96)[:, :, 0:AV]
                r_ = S5[:, 3:4, :].rearrange("p o t -> p t o")
                c = AV * (h % 2)
                nc.vector.tensor_tensor(AT[:, 0:4, c:c + AV], o_[:, 0:4], r_[:, 0:4].to_broadcast([P, 4, AV]), ALU.mult)
                nc.vector.tensor_tensor(AT[0:DEC, 4:5, c:c + AV], o_[0:DEC, 4:5], r_[0:DEC, 4:5].to_broadcast([DEC, 1, AV]),
                                        ALU.mult).then_inc(m3["at"], 1)
            low(dve, AH // 2 - 1)

        def low(dve, c):
            dve.wait_ge(m3["hi"], c + 1)
            nc.vector.tensor_tensor(MB_LO[:, c], PSF[:, 4 * 512:4 * 512 + T], MB_HI[:, c].bitcast(F32),
                                    ALU.subtract).then_inc(m3["lo"], 1)

        def mix3_act(act):
            act.wait_ge(m2["h_T"], MH)
            act.wait_ge(m2["st_T"], MH)
            act.wait_ge(m2["st_v"], MH)

            def exps(h):
                act.wait_ge(m3["bias"], h + 1)
                if h >= 2:
                    act.wait_ge(m3["p_T"], 3 * (h - 1))
                for j in range(TT):
                    n = rows_of(j)
                    last = nc.scalar.activation(PR[0:n, h % 2, POFF[j]:POFF[j] + SLEN[j]], PSF[0:n, SOFF[j]:SOFF[j] + SLEN[j]],
                                                ACT.Exp, bias=S5[0:n, 1 + 4 * (h % 2), j:j + 1], scale=A_SCALE,
                                                accum_out=S5[0:n, 2 + 4 * (h % 2), j:j + 1])
                last.then_inc(m3["p"], 1)

            exps(0)
            for h in range(AH):
                act.wait_ge(m3["p_T"], 3 * h + 2)
                if h >= 2:
                    act.wait_ge(m3["o"], h - 1)
                nc.scalar.activation(PT[:, h % 2, 512:1024], PS[:, 5, :], ACT.Copy).then_inc(m3["pt_a"], 1)
                if h and h % 2 == 0:
                    high(act, h // 2 - 1)
                if h + 1 < AH:
                    exps(h + 1)
            high(act, AH // 2 - 1)

        def high(act, c):
            act.wait_ge(m3["a_T"], c + 1)
            nc.scalar.activation(MB_HI[:, c], PSF[:, 4 * 512:4 * 512 + T], ACT.Copy).then_inc(m3["hi"], 1)

        def out_pe(pe, p):
            pe.wait_ge(m2["lo"], MH)
            pe.wait_ge(m3["lo"], AH // 2)

            def tiles(i, first=False):
                for t in range(4):
                    weights_ready(pe, i * 4 + (B_OUT + t))
                    if not (first and t < 2):
                        pe.wait_ge(p["y_sq"].sem, i * 4 + (t - 1) + p["y_sq"].base)
                    for k in range(KD):
                        hi, lo = (MA_HI[:, k], MA_LO[:, k]) if k < MH else (MB_HI[:, k - MH], MB_LO[:, k - MH])
                        last = product(B_OUT + t, k, hi, lo, 4 + 2 * (t % 2), k == 0, k == KD - 1)
                    last.then_inc(w_used, 1)

            tiles(0, first=True)
            tiles(1)

        def out_act(act, p):
            for m in range(KD):
                act.wait_ge(w_used, B_OUT + m + 1)
                y_out(act, p, m, m % 2, 4 + 2 * (m % 2), "mix_post_g", m < 2)
                split_hi(act, B_OUT + m + 2)

        def out_dve(dve):
            for m in range(KD):
                split_lo(dve, B_OUT + m + 2)

        block = ctx.enter_context(nc.Block())

        @block.sync
        def _(sp):
            start_sp(sp)
            load_ffn(sp, 0, a["ff1_w_gate"][0], a["ff1_w_up"][0], a["ff1_w_down"][0])
            load_mix(sp)
            load_ffn(sp, FF2_0, a["ff2_w_gate"][0], a["ff2_w_up"][0], a["ff2_w_down"][0])
            finish_sp(sp)

        @block.gpsimd
        def _(pool):
            start_pool(pool)
            pre_pool(pool, pre[0])
            acc_pool(pool, post[0])
            post_pool(pool, post[0])
            pre_pool(pool, pre[1])
            mix1_pool(pool)
            mix2_pool(pool)
            acc_pool(pool, post[1])
            post_pool(pool, post[1])
            pre_pool(pool, pre[2])
            acc_pool(pool, post[2])
            post_pool(pool, post[2])

        @block.scalar
        def _(act):
            pre_act(act, pre[0], None)
            split_hi(act, 0)
            split_hi(act, 1)
            ffn_act(act, ff[0], post[0], 0, "ff1_post_g")
            post_act(act, post[0])
            pre_act(act, pre[1], post[0])
            mix1_act(act)
            mix2_act(act)
            mix3_act(act)
            out_act(act, post[1])
            post_act(act, post[1])
            pre_act(act, pre[2], post[1])
            ffn_act(act, ff[1], post[2], FF2_0, "ff2_post_g")
            post_act(act, post[2])
            finish_act(act)

        @block.vector
        def _(dve):
            start_dve(dve)
            pre_dve(dve, pre[0], "ff1_pre_g")
            split_lo(dve, 0)
            split_lo(dve, 1)
            ffn_dve(dve, ff[0], 0)
            post_dve(dve, post[0])
            pre_dve(dve, pre[1], "mix_pre_g")
            mix1_dve(dve)
            mix2_dve(dve)
            mix3_dve(dve)
            out_dve(dve)
            post_dve(dve, post[1])
            pre_dve(dve, pre[2], "ff2_pre_g")
            ffn_dve(dve, ff[1], FF2_0)
            post_dve(dve, post[2])

        @block.tensor
        def _(pe):
            start_pe(pe)
            pre_pe(pe, pre[0])
            ffn_pe(pe, ff[0], pre[0], post[0], 0)
            post_pe(pe, post[0])
            pre_pe(pe, pre[1])
            mix1_pe(pe)
            mix2_pe(pe)
            mix3_pe(pe)
            out_pe(pe, post[1])
            post_pe(pe, post[1])
            pre_pe(pe, pre[2])
            ffn_pe(pe, ff[1], pre[2], post[2], FF2_0)
            post_pe(pe, post[2])
            finish_pe(pe)


INPUTS = ["x_prompt", "x_sample", "cache_kv_latent", "cache_k_rope", "state_C", "state_n", "state_m",
          "ff1_pre_g", "ff1_w_gate", "ff1_w_up", "ff1_w_down", "ff1_post_g",
          "mix_pre_g", "w_in", "b_igate", "b_fgate", "q_a_g", "w_uq", "kv_a_g", "w_ukv", "m_head_g", "w_out",
          "mix_post_g", "ff2_pre_g", "ff2_w_gate", "ff2_w_up", "ff2_w_down", "ff2_post_g"]
OUTPUTS = [(1, SEQ, D), (1, DEC, D),
           (1, 1, SEQ, KVL), (1, 1, SEQ, ROPE), (1, 1, MH, P, P), (1, 1, MH, P), (1, 1, MH),
           (1, 1, DEC, KVL), (1, 1, DEC, ROPE), (1, 1, MH, P, P), (1, 1, MH, P), (1, 1, MH)]


def kernel(**inputs):
    import numpy as np
    import concourse.bacc as bacc
    from concourse.bass_utils import run_bass_kernel_spmd

    half = ROPE // 2
    pos = np.concatenate([np.arange(SEQ), PAST + np.arange(DEC)]).astype(np.float32)
    freq = (np.float32(10000.0) ** (-np.arange(half, dtype=np.float32) / np.float32(half))).astype(np.float32)
    ang = (freq[:, None] * pos[None, :]).astype(np.float32)
    cos, sin = np.cos(ang), np.sin(ang)
    rope = np.stack([np.concatenate([cos, cos]), np.concatenate([-sin, sin])], axis=1)
    rope = np.ascontiguousarray(np.concatenate([rope] * (P // ROPE)), dtype=np.float32)

    nc = bacc.Bacc("TRN2", target_bir_lowering=False, num_devices=1)
    arrays, aps = {}, {}
    for name in INPUTS:
        x = np.ascontiguousarray(inputs[name])
        arrays[f"in_{name}"] = x
        aps[name] = nc.dram_tensor(f"in_{name}", x.shape, mybir.dt.from_np(x.dtype), kind="ExternalInput").ap()
    arrays["rope_table"] = rope
    table = nc.dram_tensor("rope_table", rope.shape, F32, kind="ExternalInput").ap()
    outs = [nc.dram_tensor(f"out_{i}", s, F32, kind="ExternalOutput").ap() for i, s in enumerate(OUTPUTS)]
    build(nc, aps, table, outs)
    r = run_bass_kernel_spmd(nc, [arrays], core_ids=[0])
    return tuple(r.results[0][f"out_{i}"] for i in range(len(OUTPUTS)))
```

```python
from contextlib import ExitStack

import concourse.bass as bass
from concourse import mybir

P = 128
D = 1024
KD = D // P
SEQ = 512
DEC = 64
T = SEQ + DEC
HT = T // 2
PAST = 256
TT = 5
FF = 2816
JF = FF // P
EPS = 1e-6
MH = 4
AH = 8
NOPE = 64
ROPE = 32
QK = NOPE + ROPE
AV = 64
QL = 384
KQ = QL // P
KVL = 256
KC = KVL // P
TK = T + PAST
MW = MH * P
A_SCALE = QK ** -0.5
MASKED = -3.0e38
NRAW = 4
NW = 2
DOWN_PARTS = (6, 6, 5, 5)
VP = 130
VAW = AH * AV + 32

F32 = mybir.dt.float32
F32R = mybir.dt.float32r
ACT = mybir.ActivationFunctionType
ALU = mybir.AluOpType
AX = mybir.AxisListType.X

GAINS = (("ff1_pre_g", KD), ("ff1_post_g", KD), ("mix_pre_g", KD), ("mix_post_g", KD), ("ff2_pre_g", KD),
         ("ff2_post_g", KD), ("q_a_g", KQ), ("kv_a_g", KC), ("m_head_g", MH))
GROW = {}
_n = 0
for _name, _k in GAINS:
    GROW[_name] = _n
    _n += _k
NG = _n

NB_GU = 2 * JF
NB_DOWN = KD * len(DOWN_PARTS)
NB_FF = NB_GU + NB_DOWN
MIX0 = NB_FF
B_AQ = MIX0
B_CKV = B_AQ + KQ
B_SMALL = B_CKV + KC
B_QK = B_SMALL + 1
B_UKV = B_QK + 2 * MH
B_UQ = B_UKV + 2
B_VO = B_UQ + 3
B_OUT = B_VO + 2 * MH
FF2_0 = B_OUT + KD
NB = FF2_0 + NB_FF
LOADS = [1] * NB
LOADS[B_SMALL] = 3
LOADS[B_UKV] = LOADS[B_UKV + 1] = KC
for _b in range(3):
    LOADS[B_UQ + _b] = KQ


def arrived(b):
    return 16 * sum(LOADS[c] for c in range(b % NRAW, b + 1, NRAW))


def build(nc, a, rope_table, outs):
    (y_prompt, y_sample, p_kv, p_kr, p_C, p_n, p_m, s_kv, s_kr, s_C, s_n, s_m) = outs
    ctx = ExitStack()
    with ctx:
        def sem(name):
            return ctx.enter_context(nc.semaphore(name))

        top = [(nc.sbuf_base + 31) // 32 * 32]

        def place(name, shape, dt=F32, offset=None):
            n = 4
            for s in shape[1:]:
                n *= s
            if offset is None:
                offset = top[0]
                top[0] += (n + 31) // 32 * 32
            return nc.alloc_sbuf_tensor_at(name, shape, dt, offset=offset)

        ROW = T * 4
        X = place("X", [P, KD, T])
        h_at = top[0]
        H_HI = place("H_HI", [P, KD, T], F32R)
        H_LO = place("H_LO", [P, KD, T], F32R)
        u_at = top[0]
        U_HI = place("U_HI", [P, JF, T], F32R)
        U_LO = place("U_LO", [P, JF, T], F32R)
        RAW = place("RAW", [P, NRAW, 8, P])
        W_HI = place("W_HI", [P, NW, 8, P], F32R)
        W_LO = place("W_LO", [P, NW, 8, P], F32R)
        RB = place("RB", [P, T])
        PAIR = place("PAIR", [P, 2, T])
        TF = place("TF", [P, 2, T])
        acc_at = top[0]
        ACC = place("ACC", [P, T])
        IDENT = place("IDENT", [P, P])
        ONES = place("ONES", [P, P])
        PERM = place("PERM", [P, P])
        trig_at = top[0]
        TRIG = place("TRIG", [P, 2, T])
        GCOLS = place("GCOLS", [P, NG])
        SEL = place("SEL", [MH, MH, P])
        GC = place("GC", [P, TT, MH])
        EMC = place("EMC", [P, TT, MH])
        BIAS = place("BIAS", [MH, 4])
        MEND = place("MEND", [MH, 2])
        M0B = place("M0B", [P, MH])
        WE = place("WE", [P, TT])
        S5 = place("S5", [P, 8, TT])
        EPSC = place("EPSC", [P, 1])
        WARM = place("WARM", [P, 1])
        ROOT = place("ROOT", [P, TT])
        INV = place("INV", [P, TT])
        assert top[0] <= nc.sbuf_usable_end, (top[0], nc.sbuf_usable_end)
        XIN = place("XIN", [P, TT, D], offset=u_at)
        GROWS = place("GROWS", [NG, P], offset=u_at + TT * D * 4)
        Y = place("Y", [P, KD, T], offset=h_at)
        PJ1 = place("PJ1", [P, 2 * MH, T], offset=u_at)
        PJ2 = place("PJ2", [P, 2 * MH, T], offset=u_at + 8 * ROW)
        CQ_HI = place("CQ_HI", [P, KQ, T], F32R, offset=u_at + 8 * ROW)
        CQ_LO = place("CQ_LO", [P, KQ, T], F32R, offset=u_at + 11 * ROW)
        qh_at = u_at + 16 * ROW
        QH = place("QH", [QK, AH, T], offset=qh_at)
        C_HI = place("C_HI", [P, KC, TK], F32R, offset=qh_at)
        C_LO = place("C_LO", [P, KC, TK], F32R, offset=qh_at + KC * TK * 4)
        kh_at = u_at + 24 * ROW
        KH = place("KH", [QK, AH, TK], offset=kh_at)
        CRAW = place("CRAW", [P, KC, TK], offset=kh_at)
        AQRAW = place("AQRAW", [P, KQ, T], offset=kh_at + KC * TK * 4)
        CIN = place("CIN", [P, 2, KVL], offset=kh_at + KC * TK * 4 + 3 * ROW)
        KIN = place("KIN", [P, 2, ROPE], offset=kh_at + KC * TK * 4 + 3 * ROW + 2048)
        CSTAGE = place("CSTAGE", [P, TT, KVL], offset=kh_at + KC * TK * 4 + 3 * ROW + 2304)
        ARS = place("ARS", [ROPE, T], offset=kh_at + KC * TK * 4 + 3 * ROW + 2304 + 5120)
        ONES4 = place("ONES4", [MH, T], offset=kh_at + KC * TK * 4 + 4 * ROW + 2304 + 5120)
        assert KC * TK * 4 + 5 * ROW + 2304 + 5120 <= AH * TK * 4
        va_at = kh_at + AH * TK * 4
        VA = place("VA", [P, 7, VAW], offset=va_at)
        IG, LF, BC, GR, MX, EM = (place(n, [MH, T], offset=va_at + i * ROW) for i, n in
                                  enumerate(("IG", "LF", "BC", "GR", "MX", "EM")))
        assert 6 * ROW <= 7 * VAW * 4
        rest_at = va_at + 7 * VAW * 4
        KR = place("KR", [ROPE, TK], offset=rest_at)
        assert rest_at + TK * 4 <= u_at + 2 * JF * ROW
        NM = place("NM", [MH, T], offset=acc_at)
        C0T = place("C0T", [P, MH, VP], offset=rest_at)
        N0 = place("N0", [1, MH, P], offset=rest_at + MH * VP * 4)
        assert rest_at + MH * VP * 4 + 2048 <= u_at + 2 * JF * ROW
        at = [h_at]

        def local(name, shape, dt=F32):
            t = place(name, shape, dt, offset=at[0])
            n = 4
            for s in shape[1:]:
                n *= s
            at[0] += (n + 31) // 32 * 32
            return t

        KT = local("KT", [P, TT, MH, P])
        VT = local("VT", [P, TT, MH, VP])
        OS = local("OS", [P, TT, VP])
        DW = local("DW", [P, 1344])
        VW = local("VW", [P, TT, P])
        HN = local("HN", [P, TT, P])
        C0 = local("C0", [P, MH, P])
        N0R = local("N0R", [MH, P])
        assert at[0] <= h_at + 16 * ROW
        at[0] = h_at
        PR = local("PR", [P, 2, 1600])
        PT = local("PT", [P, 2, 1472])
        AT = local("AT", [P, TT, P])
        assert at[0] <= h_at + 16 * ROW
        MA_HI = place("MA_HI", [P, MH, T], F32R, offset=u_at + 8 * ROW)
        MA_LO = place("MA_LO", [P, MH, T], F32R, offset=u_at + 4 * ROW)
        MB_HI = place("MB_HI", [P, MH, T], F32R, offset=u_at)
        MB_LO = place("MB_LO", [P, MH, T], F32R, offset=u_at + 12 * ROW)
        CN = place("CN", [P, 2, 2, P], offset=trig_at)
        NN = place("NN", [1, 2, P], offset=trig_at + 2048)
        KSTAGE = place("KSTAGE", [P, TT, ROPE], offset=trig_at + 3072)

        PS = ctx.enter_context(nc.psum_tensor("PS", [P, 8, 512], F32))
        PSF = PS[:].rearrange("p b n -> p (b n)")

        def pair(b, rows=P, n=HT):
            return PS[0:rows, b:b + 2, 0:n]

        def halves(ap, n=HT):
            return ap.rearrange("p (a n) -> p a n", n=n)

        raw_in = [sem(f"raw_in{i}") for i in range(NRAW)]
        w_hi, w_lo, w_used = sem("w_hi"), sem("w_lo"), sem("w_used")
        x_in, g_in, trig_in, bias_in, cache_in, state_in = (sem(n) for n in (
            "x_in", "g_in", "trig_in", "bias_in", "cache_in", "state_in"))
        consts, consts0 = sem("consts"), sem("consts0")
        g_T, g_cols, g_half = sem("g_T"), sem("g_cols"), sem("g_half")
        x_in_half = [sem(f"x_in_half{h}") for h in range(2)]
        x_T, x_cols = sem("x_T"), sem("x_cols")
        out_sem = sem("out_sem")
        dve_step, act_step, pool_step = sem("dve_step"), sem("act_step"), sem("pool_step")
        steps = {"dve": 0, "act": 0, "pool": 0}

        def settle(eng, key, s, ins):
            steps[key] += 1
            ins.then_inc(s, 1)
            eng.wait_ge(s, steps[key])

        def names(prefix, *what):
            return {w: sem(f"{prefix}_{w}") for w in what}

        class Since:

            def __init__(self, sem_, base):
                self.sem, self.base = sem_, base

        def stages(prefix, count, **per_stage):
            sems = {w: sem(f"{prefix}_{w}") for w in per_stage}
            return [{w: Since(sems[w], i * total) for w, total in per_stage.items()}
                    for i in range(count)]

        post = stages("post", 3, y_sq=KD, y_copy=KD, acc=KD - 1, sum=1, root=1, inv=1, spread=1, t=KD, x=KD)
        pre = stages("pre", 3, hi=KD, lo=KD, sq_even=KD // 2, sq_odd=KD // 2, sq=KD // 2,
                     sum=1, root=1, inv=1, spread=1)
        ff = stages("ff", 2, gate=JF, up=JF, silu=JF, mul=JF, u_hi=JF, u_lo=JF)

        def raw_slot(b):
            return RAW[:, b % NRAW]

        def load_wait(sp, b):
            if b >= NRAW:
                sp.wait_ge(w_lo, b - NRAW + 1)

        def load_ffn(sp, b0, wg, wu, wd):
            gv = wg.rearrange("(k p) f -> p k f", p=P)
            uv = wu.rearrange("(k p) f -> p k f", p=P)
            dv = wd.rearrange("(k p) f -> p k f", p=P)

            def tiles(i, first=False):
                for q in range(4):
                    b = b0 + q
                    if not (first and b < NRAW):
                        sp.wait_ge(w_lo, b0 + i * 4 + q - NRAW + 1)
                    src = (gv, uv)[q % 2]
                    sp.dma_start(raw_slot(b), src[:, :, bass.ds(i * (2 * P) + (q // 2) * P, P)]).then_inc(
                        raw_in[b % NRAW], 16)

            tiles(0, first=True)
            with sp.Fori(1, JF // 2) as i:
                tiles(i)
            b1 = b0 + NB_GU
            with sp.Fori(0, KD) as m:
                k0 = 0
                for q, n in enumerate(DOWN_PARTS):
                    sp.wait_ge(w_lo, m * 4 + (b1 + q - NRAW + 1))
                    sp.dma_start(raw_slot(b1 + q)[:, 0:n, :], dv[:, k0:k0 + n, bass.ds(m * P, P)]).then_inc(
                        raw_in[(b1 + q) % NRAW], 16)
                    k0 += n

        def split_hi(act, b, n=8, count=None, target=None):
            act.wait_ge(raw_in[b % NRAW], arrived(b) if target is None else target)
            if count is None:
                if b >= NW:
                    act.wait_ge(w_used, b - NW + 1)
            else:
                act.wait_ge(w_used, count - NW + 1)
            nc.scalar.activation(W_HI[:, b % NW, 0:n, :], raw_slot(b)[:, 0:n, :], ACT.Copy).then_inc(w_hi, 1)

        def split_lo(dve, b, n=8, count=None):
            dve.wait_ge(w_hi, (b if count is None else count) + 1)
            nc.vector.tensor_tensor(W_LO[:, b % NW, 0:n, :], raw_slot(b)[:, 0:n, :],
                                    W_HI[:, b % NW, 0:n, :].bitcast(F32), ALU.subtract).then_inc(w_lo, 1)

        def weights_ready(pe, count):
            pe.wait_ge(w_hi, count + 1)
            pe.wait_ge(w_lo, count + 1)

        def passes(w_hi_t, w_lo_t, a_hi, a_lo):
            return ((w_hi_t, a_hi), (w_hi_t, a_lo), (w_lo_t, a_hi))

        def product(b, t, hi, lo, bank, start, stop, m=P, rows=P, n=HT):
            wh, wl = W_HI[0:rows, b % NW, t, 0:m], W_LO[0:rows, b % NW, t, 0:m]
            last = None
            for i, (w, x) in enumerate(passes(wh, wl, hi, lo)):
                for s in range(2):
                    last = nc.tensor.matmul(PS[0:m, bank + s, 0:n], w, x[:, s * n:(s + 1) * n],
                                            start=start and i == 0, stop=stop and i == 2)
            return last

        NS = 96
        FRAMES = [(i * P, P) for i in range(4)] + [(SEQ, DEC)]

        def frame_sums(src, bank, start, stop):
            for t in (0, 4, 1, 2, 3):
                c, n = FRAMES[t]
                last = nc.tensor.matmul(PS[0:n, bank, t * NS:(t + 1) * NS], src[:, c:c + n], ONES[:, 0:NS],
                                        start=start and t == 0, stop=stop and t == 3)
            return last

        def frame_roots(bank, width):
            cols = PS[:, bank, 0:4 * NS].rearrange("p (t c) -> p t c", c=NS)[:, :, 0]
            nc.scalar.activation(ROOT[:, 0:4], cols, ACT.Sqrt, bias=EPSC[:], scale=1.0 / width)
            return nc.scalar.activation(ROOT[0:DEC, 4:5], PS[0:DEC, bank, 4 * NS:4 * NS + 1], ACT.Sqrt,
                                        bias=EPSC[0:DEC], scale=1.0 / width)

        def spread(bank):
            for t, (c, n) in enumerate(FRAMES):
                last = nc.tensor.matmul(PSF[:, bank * 512 + c:bank * 512 + c + n], INV[0:n, t:t + 1].to_broadcast([n, P]),
                                        IDENT[0:n, 0:n], start=True, stop=True)
            return last

        def spread_at(bank):
            return PSF[:, bank * 512:bank * 512 + T]

        POST_SUM, POST_SPREAD, PRE_SUM, PRE_SPREAD = 0, 2, 7, 6

        def post_pe(pe, e):
            pe.wait_ge(e["acc"].sem, KD - 1 + e["acc"].base)
            frame_sums(ACC[:], POST_SUM, True, False)
            pe.wait_ge(e["y_sq"].sem, KD + e["y_sq"].base)
            frame_sums(PAIR[:, 1], POST_SUM, False, True).then_inc(e["sum"].sem, 1)
            pe.wait_ge(e["inv"].sem, 1 + e["inv"].base)
            spread(POST_SPREAD).then_inc(e["spread"].sem, 1)

        def post_act(act, e):
            act.wait_ge(e["sum"].sem, 1 + e["sum"].base)
            frame_roots(POST_SUM, D).then_inc(e["root"].sem, 1)

        def post_dve(dve, e, p=None):
            dve.wait_ge(e["root"].sem, 1 + e["root"].base)
            nc.vector.reciprocal(INV[:], ROOT[:]).then_inc(e["inv"].sem, 1)
            dve.wait_ge(e["spread"].sem, 1 + e["spread"].base)
            for k in range(KD):
                nc.vector.tensor_tensor(Y[:, k], Y[:, k], spread_at(POST_SPREAD), ALU.mult).then_inc(e["t"].sem, 1)
                if p is not None and k >= 2:
                    low_dve(dve, p, k - 2)
            if p is not None:
                low_dve(dve, p, KD - 2)
                low_dve(dve, p, KD - 1)

        def post_pool(pool, e):
            for k in range(KD):
                pool.wait_ge(e["t"].sem, k + 1 + e["t"].base)
                nc.gpsimd.tensor_tensor(X[:, k], X[:, k], Y[:, k], ALU.add).then_inc(e["x"].sem, 1)

        def x_wait(eng, e, k):
            if e is None:
                eng.wait_ge(x_cols, k + 2)
            else:
                eng.wait_ge(e["x"].sem, k + 1 + e["x"].base)

        SQ_SUM = [PAIR[:, 0], PAIR[:, 1], TF[:, 0], TF[:, 1]]
        SQ_ODD = [ACC[:], RB[:]]

        def pre_act(act, e, before, gain, split=None):
            for k in range(KD):
                x_wait(act, before, k)
                g = GROW[gain] + k
                nc.scalar.activation(H_HI[:, k], X[:, k], ACT.Copy, scale=GCOLS[:, g:g + 1]).then_inc(e["hi"].sem, 1)
                if split is not None and k % 4 == 3:
                    split_hi(act, k // 4)
                i = k // 2
                if k % 2:
                    nc.scalar.activation(SQ_SUM[i], X[:, k - 1], ACT.Square).then_inc(e["sq_even"].sem, 1)
                    if i >= 2:
                        act.wait_ge(e["sq"].sem, i - 1 + e["sq"].base)
                    nc.scalar.activation(SQ_ODD[i % 2], X[:, k], ACT.Square).then_inc(e["sq_odd"].sem, 1)

        def pre_root_act(act, e):
            act.wait_ge(e["sum"].sem, 1 + e["sum"].base)
            frame_roots(PRE_SUM, D).then_inc(e["root"].sem, 1)

        def pre_sum_pe(pe, e):
            for i in range(KD // 2):
                pe.wait_ge(e["sq"].sem, i + 1 + e["sq"].base)
                last = frame_sums(SQ_SUM[i], PRE_SUM, i == 0, i == KD // 2 - 1)
            last.then_inc(e["sum"].sem, 1)

        def pre_spread_pe(pe, e):
            pe.wait_ge(e["inv"].sem, 1 + e["inv"].base)
            spread(PRE_SPREAD).then_inc(e["spread"].sem, 1)

        PRE_GAINS = ("ff1_pre_g", "mix_pre_g", "ff2_pre_g")

        def low_dve(dve, e, k):
            dve.wait_ge(e["hi"].sem, k + 1 + e["hi"].base)
            g = GROW[PRE_GAINS[pre.index(e)]] + k
            nc.vector.scalar_tensor_tensor(out=H_LO[:, k], in0=X[:, k], scalar=GCOLS[:, g:g + 1],
                                           in1=H_HI[:, k].bitcast(F32), op0=ALU.mult, op1=ALU.subtract).then_inc(e["lo"].sem, 1)
            if k % 2 and k < KD - 1:
                add_squares(dve, e, k // 2)

        def add_squares(dve, e, i):
            dve.wait_ge(e["sq_even"].sem, i + 1 + e["sq_even"].base)
            dve.wait_ge(e["sq_odd"].sem, i + 1 + e["sq_odd"].base)
            nc.vector.tensor_tensor(SQ_SUM[i], SQ_SUM[i], SQ_ODD[i % 2], ALU.add).then_inc(e["sq"].sem, 1)

        def pre_dve(dve, e):
            add_squares(dve, e, KD // 2 - 1)
            dve.wait_ge(e["root"].sem, 1 + e["root"].base)
            nc.vector.reciprocal(INV[:], ROOT[:]).then_inc(e["inv"].sem, 1)

        def pre_factor_dve(dve, e):
            dve.wait_ge(e["spread"].sem, 1 + e["spread"].base)
            settle(dve, "dve", dve_step, nc.vector.tensor_copy(RB[:], spread_at(PRE_SPREAD)))

        def h_wait(pe, e, k):
            pe.wait_ge(e["hi"].sem, k + 1 + e["hi"].base)
            pe.wait_ge(e["lo"].sem, k + 1 + e["lo"].base)

        def ffn_pe(pe, f, e, p, b0):
            def gate_up(i, first=False):
                for jj in range(2):
                    j = i * 2 + jj
                    for q in range(2):
                        b = b0 + 2 * jj + q
                        weights_ready(pe, i * 4 + b)
                        if not (first and jj == 0):
                            done = f["up"] if q else f["gate"]
                            pe.wait_ge(done.sem, j + done.base)
                        for k in range(KD):
                            if first and jj == 0 and q == 0:
                                h_wait(pe, e, k)
                            if first and jj == 0 and q == 1 and k == KD // 2:
                                pre_spread_pe(pe, e)
                            last = product(b, k, H_HI[:, k], H_LO[:, k], 2 * q, k == 0, k == KD - 1)
                        last.then_inc(w_used, 1)
                        if first and jj == 0 and q == 0:
                            pre_sum_pe(pe, e)

            gate_up(0, first=True)
            with pe.Fori(1, JF // 2) as i:
                gate_up(i)
            b1 = b0 + NB_GU

            def down(i, first=False):
                for mm in range(2):
                    m = i * 2 + mm
                    if not first:
                        pe.wait_ge(p["y_copy"].sem, m - 1 + p["y_copy"].base)
                    k = 0
                    for q, n in enumerate(DOWN_PARTS):
                        b = b1 + q
                        weights_ready(pe, i * 8 + (b1 + 4 * mm + q))
                        if first and mm == 0:
                            pe.wait_ge(f["u_lo"].sem, k + n + f["u_lo"].base)
                        for t in range(n):
                            last = product(b, t, U_HI[:, k], U_LO[:, k], 4 + 2 * mm, k == 0, k == JF - 1)
                            k += 1
                        last.then_inc(w_used, 1)

            down(0, first=True)
            with pe.Fori(1, KD // 2) as i:
                down(i)

        def down_target(b1, q, m):
            return arrived(b1 + q) + 16 * m if isinstance(m, int) else m * 16 + arrived(b1 + q)

        def ffn_act(act, f, p, b0, post_gain):
            b1 = b0 + NB_GU

            def gate_up(i, last=False):
                for jj in range(2):
                    j = i * 2 + jj
                    for q in range(2):
                        b = b0 + 2 * jj + q + 2
                        if q:
                            act.wait_ge(f["gate"].sem, j + 1 + f["gate"].base)
                            nc.scalar.activation(PAIR[:, jj], PAIR[:, jj], ACT.Silu).then_inc(f["silu"].sem, 1)
                        if last and jj == 1:
                            split_hi(act, b1 + q, DOWN_PARTS[q])
                        else:
                            split_hi(act, b, 8, i * 4 + b, i * 16 + arrived(b))
                    act.wait_ge(f["mul"].sem, j + 1 + f["mul"].base)
                    nc.scalar.activation(U_HI[:, bass.ds(j, 1), :], TF[:, jj:jj + 1, :], ACT.Copy).then_inc(f["u_hi"].sem, 1)

            nc.scalar.activation(WARM[:], EPSC[:], ACT.Silu)
            gate_up(0)
            with act.Fori(1, JF // 2 - 1) as i:
                gate_up(i)
            gate_up(JF // 2 - 1, last=True)
            nc.scalar.activation(WARM[:], EPSC[:], ACT.Sqrt)

            def down(i, first=False, last=False):
                for mm in range(2):
                    m = i * 2 + mm
                    for q in range(4):
                        nq = q + 2
                        over = nq // 4
                        if not (last and mm == 1 and over):
                            b = b1 + nq % 4
                            split_hi(act, b, DOWN_PARTS[nq % 4], i * 8 + (b1 + 4 * mm + nq),
                                     i * 32 + (arrived(b) + 16 * (mm + over)))
                        elif b0 == 0:
                            split_hi(act, MIX0 + nq % 4)
                    act.wait_ge(w_used, i * 8 + (b1 + 4 * mm + 4))
                    y_out(act, p, m, mm, 4 + 2 * mm, post_gain, first)

            down(0, first=True)
            with act.Fori(1, KD // 2 - 1) as i:
                down(i)
            down(KD // 2 - 1, last=True)

        def y_out(act, p, m, slot, bank, gain, first):
            if not first:
                act.wait_ge(p["acc"].sem, m - 1 + p["acc"].base)
            nc.scalar.activation(halves(PAIR[:, slot]), pair(bank), ACT.Square).then_inc(p["y_sq"].sem, 1)
            nc.scalar.activation(halves(Y[:, bass.ds(m, 1), :].rearrange("p a t -> p (a t)")), pair(bank), ACT.Copy,
                                 scale=GCOLS[:, bass.ds(m + GROW[gain], 1)]).then_inc(p["y_copy"].sem, 1)

        def ffn_dve(dve, f, e, b0):
            b1 = b0 + NB_GU

            def gate_up(i, last=False):
                for jj in range(2):
                    j = i * 2 + jj
                    b = b0 + 2 * jj + 2
                    tail = last and jj == 1
                    dve.wait_ge(w_used, i * 4 + (b0 + 2 * jj + 1))
                    if not (isinstance(i, int) and i == 0):
                        dve.wait_ge(f["mul"].sem, j - 1 + f["mul"].base)
                    elif jj == 0:
                        pre_factor_dve(dve, e)
                    nc.vector.tensor_tensor(halves(PAIR[:, jj]), pair(0), halves(RB[:]), ALU.mult).then_inc(f["gate"].sem, 1)
                    if tail:
                        split_lo(dve, b1, DOWN_PARTS[0])
                    else:
                        split_lo(dve, b, 8, i * 4 + b)
                    dve.wait_ge(w_used, i * 4 + (b0 + 2 * jj + 2))
                    if not (isinstance(i, int) and i == 0):
                        dve.wait_ge(f["u_lo"].sem, j - 1 + f["u_lo"].base)
                    nc.vector.tensor_tensor(halves(TF[:, jj]), pair(2), halves(RB[:]), ALU.mult).then_inc(f["up"].sem, 1)
                    dve.wait_ge(f["silu"].sem, j + 1 + f["silu"].base)
                    dve.wait_ge(f["up"].sem, j + 1 + f["up"].base)
                    nc.vector.tensor_tensor(TF[:, jj], TF[:, jj], PAIR[:, jj], ALU.mult).then_inc(f["mul"].sem, 1)
                    if tail:
                        split_lo(dve, b1 + 1, DOWN_PARTS[1])
                    else:
                        split_lo(dve, b + 1, 8, i * 4 + (b + 1))
                    dve.wait_ge(f["u_hi"].sem, j + 1 + f["u_hi"].base)
                    nc.vector.tensor_tensor(U_LO[:, bass.ds(j, 1), :], TF[:, jj:jj + 1, :],
                                            U_HI[:, bass.ds(j, 1), :].bitcast(F32), ALU.subtract).then_inc(f["u_lo"].sem, 1)

            gate_up(0)
            with dve.Fori(1, JF // 2 - 1) as i:
                gate_up(i)
            gate_up(JF // 2 - 1, last=True)

            def down(i, last=False):
                for mm in range(2):
                    for q in range(4):
                        nq = q + 2
                        if not (last and mm == 1 and nq >= 4):
                            split_lo(dve, b1 + nq % 4, DOWN_PARTS[nq % 4], i * 8 + (b1 + 4 * mm + nq))
                        elif b0 == 0:
                            split_lo(dve, MIX0 + nq % 4)

            with dve.Fori(0, KD // 2 - 1) as i:
                down(i)
            down(KD // 2 - 1, last=True)

        def acc_pool(pool, p):
            for m in range(KD - 1):
                pool.wait_ge(p["y_sq"].sem, m + 1 + p["y_sq"].base)
                if m == 0:
                    nc.gpsimd.tensor_copy(ACC[:], PAIR[:, 0]).then_inc(p["acc"].sem, 1)
                else:
                    pool.wait_ge(p["acc"].sem, m + p["acc"].base)
                    nc.gpsimd.tensor_tensor(ACC[:], ACC[:], PAIR[:, m % 2], ALU.add).then_inc(p["acc"].sem, 1)


        def start_pool(pool):
            nc.gpsimd.memset(IDENT[:], 0.0).then_inc(consts0, 1)
            nc.gpsimd.memset(PERM[:], 0.0).then_inc(consts0, 1)
            nc.gpsimd.memset(SEL[:], 0.0).then_inc(consts0, 1)
            nc.gpsimd.memset(EPSC[:], EPS)
            nc.gpsimd.memset(S5[:], 1.0)
            nc.gpsimd.memset(ROOT[:], 1.0)
            nc.gpsimd.memset(ONES[:], 1.0)
            nc.gpsimd.memset(GC[:], 0.0)
            nc.gpsimd.memset(EMC[:], 1.0)
            pool.wait_ge(consts0, 3)
            nc.gpsimd.affine_select(out=IDENT[:], in_=IDENT[:], compare_op=ALU.not_equal, fill=1.0, base=0,
                                    pattern=[[-1, P]], channel_multiplier=1).then_inc(consts, 1)
            nc.gpsimd.affine_select(out=PERM[:].rearrange("p (q a c) -> p q a c", a=2, c=ROPE // 2),
                                    in_=PERM[:].rearrange("p (q a c) -> p q a c", a=2, c=ROPE // 2),
                                    compare_op=ALU.not_equal, fill=1.0, base=ROPE // 2,
                                    pattern=[[ROPE, P // ROPE], [-(ROPE // 2), 2], [1, ROPE // 2]],
                                    channel_multiplier=-1).then_inc(consts, 1)
            nc.gpsimd.affine_select(out=SEL[:], in_=SEL[:], compare_op=ALU.not_equal, fill=1.0, base=0,
                                    pattern=[[1, MH], [0, P]], channel_multiplier=-1).then_inc(consts, 1)
            pool.dma_start(TRIG[:], rope_table).then_inc(trig_in, 16)
            pool.dma_start(BIAS[:, 0:1], a["b_igate"].rearrange("l h -> h l")).then_inc(bias_in, 16)
            pool.dma_start(BIAS[:, 1:2], a["b_fgate"].rearrange("l h -> h l")).then_inc(bias_in, 16)
            pool.dma_start(BIAS[:, 2:3], a["state_m"].rearrange("l b h -> h (l b)")).then_inc(bias_in, 16)
            pool.dma_start(M0B[:], a["state_m"][0].to_broadcast([P, MH])).then_inc(bias_in, 16)

        def start_sp(sp):
            for name, k in GAINS:
                g = a[name][0]
                g = g if name == "m_head_g" else g.rearrange("(k p) -> k p", p=P)
                sp.dma_start(GROWS[GROW[name]:GROW[name] + k, :], g).then_inc(g_in, 16)
            sp.dma_start(XIN[0:DEC, TT - 1, :], a["x_sample"][0]).then_inc(x_in, 16)
            for h in range(2):
                c = slice(h * D // 2, (h + 1) * D // 2)
                sp.dma_start(XIN[:, 0:4, c], a["x_prompt"][0].rearrange("(t p) d -> p t d", p=P)[:, :, c]).then_inc(
                    x_in_half[h], 16)

        X_BANKS = (3, 4, 5, 7)

        def start_pe(pe):
            pe.wait_ge(consts, 3)
            pe.wait_ge(g_in, 16 * len(GAINS))
            nc.tensor.transpose(PS[:, 0, 0:NG], GROWS[:], IDENT[0:NG, 0:NG]).then_inc(g_T, 1)
            pe.wait_ge(x_in, 16)
            for k in range(KD):
                last = nc.tensor.transpose(PS[:, 6, k * DEC:(k + 1) * DEC], XIN[0:DEC, TT - 1, k * P:(k + 1) * P],
                                           IDENT[0:DEC, 0:DEC])
            last.then_inc(x_T, 1)
            for k in range(KD):
                if k % 4 == 0:
                    pe.wait_ge(x_in_half[k // 4], 16)
                if k >= 4:
                    pe.wait_ge(x_cols, k - 2)
                for t in range(4):
                    last = nc.tensor.transpose(PS[:, X_BANKS[k % 4], t * P:(t + 1) * P],
                                               XIN[:, t, k * P:(k + 1) * P], IDENT[:])
                last.then_inc(x_T, 1)

        def start_dve(dve):
            dve.wait_ge(g_T, 1)
            settle(dve, "dve", dve_step, nc.vector.tensor_copy(GCOLS[:], PS[:, 0, 0:NG]))
            for name in ("ff1_post_g", "ff2_post_g"):
                g = GCOLS[:, GROW[name]:GROW[name] + KD]
                nc.vector.tensor_scalar(g, g, 0.5, None, ALU.mult).then_inc(g_half, 1)
            dve.wait_ge(x_T, 1)
            nc.vector.tensor_copy(X[:, :, SEQ:T], PS[:, 6, :].rearrange("p (k t) -> p k t", k=KD)).then_inc(x_cols, 1)
            for k in range(KD):
                dve.wait_ge(x_T, k + 2)
                nc.vector.tensor_copy(X[:, k, 0:SEQ], PS[:, X_BANKS[k % 4], :]).then_inc(x_cols, 1)
                if k:
                    low_dve(dve, pre[0], k - 1)
                if k == 4:
                    split_lo(dve, 0)
            split_lo(dve, 1)
            low_dve(dve, pre[0], KD - 1)

        OUT_BANKS = (0, 4, 6)

        def finish_pe(pe):
            for k in range(KD):
                x_wait(pe, post[2], k)
                b = OUT_BANKS[k % 3]
                if k >= 3:
                    pe.wait_ge(o["copied"], k - 2)
                for t in range(4):
                    nc.tensor.transpose(PS[:, b, t * P:(t + 1) * P], X[:, k, t * P:(t + 1) * P], IDENT[:])
                nc.tensor.transpose(PS[0:DEC, b + 1, 0:P], X[:, k, SEQ:T], IDENT[:]).then_inc(o["T"], 1)

        def finish_act(act):
            for k in range(KD):
                act.wait_ge(o["T"], k + 1)
                b = OUT_BANKS[k % 3]
                nc.scalar.activation(XIN[:, 0:4, k * P:(k + 1) * P],
                                     PS[:, b, :].rearrange("p (t f) -> p t f", t=4), ACT.Copy)
                nc.scalar.activation(XIN[0:DEC, 4, k * P:(k + 1) * P], PS[0:DEC, b + 1, 0:P],
                                     ACT.Copy).then_inc(o["copied"], 1)

        def finish_sp(sp):
            for h in range(2):
                sp.wait_ge(o["copied"], 4 * (h + 1))
                c = slice(h * D // 2, (h + 1) * D // 2)
                sp.dma_start(y_prompt[0].rearrange("(t p) d -> p t d", p=P)[:, :, c], XIN[:, 0:4, c]).then_inc(out_sem, 16)
                sp.dma_start(y_sample[0][:, c], XIN[0:DEC, 4, c]).then_inc(out_sem, 16)
            sp.wait_ge(out_sem, 64)
            sp.wait_ge(st["stored"], 64)
            sp.wait_ge(m1["c_stored"], 32)
            sp.wait_ge(m2["state_out"], 64 * MH)

        o = names("out", "T", "copied")
        m1 = names("m1", "cache_T", "cache_hi", "cache_lo", "kr_c", "proj", "sq", "aq_sum", "aq_root", "aq_inv", "aq_spread",
                   "cq", "c_sum", "c_root", "c_inv", "c_spread", "c", "cq_lo", "c_lo", "lf1", "soft", "lf", "mm", "em",
                   "perm", "c_T", "c_staged", "c_stored", "kr", "kn_T", "kn_a", "kn_d", "gate_T", "gate_c", "v_T", "v_a",
                   "v_d", "q_T", "q_a", "q_d", "rs", "perm_q", "qr", "rope_in", "kr_T", "kr_staged")
        st = names("st", "stored")

        def load_mix(sp):
            w_in, w_uq, w_ukv, w_out = (a[n][0] for n in ("w_in", "w_uq", "w_ukv", "w_out"))
            wv = w_in.rearrange("(k p) f -> p k f", p=P)
            c_gate, c_aq = 4 * MW, 4 * MW + 2 * MH
            c_ckv = c_aq + QL
            c_ar = c_ckv + KVL

            def one(b, *parts):
                load_wait(sp, b)
                for dst, src in parts:
                    sp.dma_start(dst, src).then_inc(raw_in[b % NRAW], 16)

            for i in range(KQ):
                one(B_AQ + i, (raw_slot(B_AQ + i), wv[:, :, c_aq + i * P:c_aq + (i + 1) * P]))
            for i in range(KC):
                one(B_CKV + i, (raw_slot(B_CKV + i), wv[:, :, c_ckv + i * P:c_ckv + (i + 1) * P]))
            one(B_SMALL, *((raw_slot(B_SMALL)[:, :, at_:at_ + n], wv[:, :, lo:lo + n])
                           for at_, lo, n in ((0, c_ar, ROPE), (32, c_gate, MH), (64, c_gate + MH, MH))))

            def heads(b0, c0):
                with sp.Fori(0, 2) as i:
                    for t in range(4):
                        sp.wait_ge(w_lo, i * 4 + (b0 + t - NRAW + 1))
                        sp.dma_start(raw_slot(b0 + t), wv[:, :, bass.ds(i * (4 * P) + (c0 + t * P), P)]).then_inc(
                            raw_in[(b0 + t) % NRAW], 16)

            heads(B_QK, 0)
            kv = w_ukv.rearrange("(k p) (h c) -> p k h c", p=P, c=NOPE + AV)
            uq = w_uq.rearrange("(k p) (h c) -> p k h c", p=P, c=QK)

            def columns_of(b, w, nk, h0, h1, c0, c1):
                dst = raw_slot(b).rearrange("p t c -> p (t c)")
                width = (h1 - h0) * (c1 - c0)
                one(b, *((dst[:, k * width:(k + 1) * width].rearrange("p (h c) -> p h c", c=c1 - c0), w[:, k, h0:h1, c0:c1])
                         for k in range(nk)))

            columns_of(B_UKV, kv, KC, 0, AH, 0, NOPE)
            columns_of(B_UKV + 1, kv, KC, 0, AH, NOPE, NOPE + AV)
            columns_of(B_UQ, uq, KQ, 0, AH, NOPE, QK)
            columns_of(B_UQ + 1, uq, KQ, 0, 4, 0, NOPE)
            columns_of(B_UQ + 2, uq, KQ, 4, AH, 0, NOPE)
            heads(B_VO, 2 * MW)
            wo = w_out.rearrange("(k p) f -> p k f", p=P)
            with sp.Fori(0, 2) as i:
                for t in range(4):
                    sp.wait_ge(w_lo, i * 4 + (B_OUT + t - NRAW + 1))
                    sp.dma_start(raw_slot(B_OUT + t), wo[:, :, bass.ds(i * (4 * P) + t * P, P)]).then_inc(
                        raw_in[(B_OUT + t) % NRAW], 16)

        KEY_TILES = [(i * P, P) for i in range(4)] + [(SEQ, DEC), (T, P), (T + P, P)]

        def mix1_pe(pe):
            pe.wait_ge(cache_in, 32)
            for k in range(KC):
                for t in range(2):
                    nc.tensor.transpose(PS[:, 6, (2 * k + t) * P:(2 * k + t + 1) * P], CIN[:, t, k * P:(k + 1) * P], IDENT[:])
            for t in range(2):
                last = nc.tensor.transpose(PS[0:ROPE, 7, t * P:(t + 1) * P], KIN[:, t, :], IDENT[:])
            last.then_inc(m1["cache_T"], 1)

            def tile(b, bank, m=P, first=False, at_half=None):
                weights_ready(pe, b)
                for k in range(KD):
                    if at_half is not None and k == KD // 2:
                        at_half()
                    if first:
                        h_wait(pe, pre[1], k)
                    last = product(b, k, H_HI[:, k], H_LO[:, k], bank, k == 0, k == KD - 1, m=m)
                return last

            tile(B_AQ, 0, first=True).then_inc(w_used, 1)
            pe.wait_ge(m1["cache_lo"], 1)
            pe.wait_ge(m1["kr_c"], 1)
            pre_sum_pe(pe, pre[1])
            tile(B_AQ + 1, 2, at_half=lambda: pre_spread_pe(pe, pre[1])).then_inc(w_used, 1)
            tile(B_AQ + 2, 4).then_inc(w_used, 1)
            pe.wait_ge(m1["proj"], 1)
            tile(B_CKV, 6).then_inc(w_used, 1)
            tile(B_CKV + 1, 0).then_inc(w_used, 1)
            for i in range(KQ):
                pe.wait_ge(m1["sq"], i + 1)
                last = frame_sums((PAIR[:, 0], PAIR[:, 1], ACC[:])[i], 2, i == 0, i == KQ - 1)
            last.then_inc(m1["aq_sum"], 1)
            pe.wait_ge(m1["proj"], 3)
            tile(B_SMALL, 4, m=64 + MH).then_inc(w_used, 1)
            pe.wait_ge(m1["aq_inv"], 1)
            spread(2).then_inc(m1["aq_spread"], 1)
            for i in range(KC):
                pe.wait_ge(m1["sq"], KQ + i + 1)
                last = frame_sums(TF[:, i], 6, i == 0, i == KC - 1)
            last.then_inc(m1["c_sum"], 1)

            for n in range(2 * MH):
                if n == 1:
                    pe.wait_ge(m1["cq"], KQ)
                pe.wait_ge(m1["proj"], n + 5)
                tile(B_QK + n, 2 * (n % 2)).then_inc(w_used, 1)
                if n == 0:
                    pe.wait_ge(m1["c_inv"], 1)
                    spread(6).then_inc(m1["c_spread"], 1)
                if n == 1:
                    pe.wait_ge(m1["proj"], 6)
                    for s in range(2):
                        last = nc.tensor.matmul(PS[0:ROPE, 4 + s, 0:HT], PERM[0:ROPE, 0:ROPE],
                                                ARS[:, s * HT:(s + 1) * HT], start=True, stop=True)
                    last.then_inc(m1["perm"], 1)
                if n == 4:
                    pe.wait_ge(m1["c"], KC)
                    pe.wait_ge(m1["kr"], 1)
                    for t, (c, rows) in enumerate(FRAMES):
                        bank, off = ((6, 0), (6, 256), (7, 0), (7, 256), (4, 0))[t]
                        for k in range(KC):
                            last = nc.tensor.transpose(PS[0:rows, bank, off + k * P:off + (k + 1) * P],
                                                       CRAW[:, k, c:c + rows], IDENT[:])
                    last.then_inc(m1["c_T"], 1)
            pe.wait_ge(m1["c_lo"], KC)
            pe.wait_ge(m1["cache_lo"], 1)
            weights_ready(pe, B_UKV)
            NK = TK // 2
            for n in range(AH // 2):
                if n < 2:
                    pe.wait_ge(m1["proj"] if n else m1["c_staged"], 14 if n else 1)
                else:
                    pe.wait_ge(m1["kn_a"], n - 1)
                    pe.wait_ge(m1["kn_d"], n - 1)
                for k in range(KC):
                    last = product(B_UKV, k * 4 + n, C_HI[:, k], C_LO[:, k], 4 - 2 * (n % 2), k == 0, k == KC - 1, n=NK)
                last.then_inc(w_used if n == AH // 2 - 1 else m1["kn_T"], 1)
            pe.wait_ge(m1["em"], 1)
            pe.wait_ge(m1["mm"], 1)
            pe.wait_ge(m1["c_staged"], 1)
            for j, src in enumerate((GR, EM)):
                for t, (c, n) in enumerate(FRAMES):
                    last = nc.tensor.transpose(PS[0:n, 7, (j * TT + t) * MH:(j * TT + t + 1) * MH], src[:, c:c + n],
                                               IDENT[0:MH, 0:MH])
            last.then_inc(m1["gate_T"], 1)
            weights_ready(pe, B_UKV + 1)
            s_w = (B_UKV + 1) % NW
            for s, (c, n) in enumerate(KEY_TILES):
                if s == 3:
                    pe.wait_ge(m1["gate_c"], 1)
                if s >= 4:
                    pe.wait_ge(m1["v_d"] if s % 2 else m1["v_a"], s // 2 - 1)
                for k in range(KC):
                    for i, (x, w) in enumerate(passes(C_HI[:, k, c:c + n], C_LO[:, k, c:c + n],
                                                      W_HI[:, s_w, 4 * k:4 * k + 4, :].rearrange("p t c -> p (t c)"),
                                                      W_LO[:, s_w, 4 * k:4 * k + 4, :].rearrange("p t c -> p (t c)"))):
                        last = nc.tensor.matmul(PS[0:n, (0, 1, 6, 7)[s % 4], :], x, w,
                                                start=k == 0 and i == 0, stop=k == KC - 1 and i == 2)
                last.then_inc(w_used if s == 6 else m1["v_T"], 1)
            pe.wait_ge(m1["cq_lo"], KQ)
            weights_ready(pe, B_UQ)
            for r in range(2):
                pe.wait_ge(m1["kn_a"], r + 3)
                pe.wait_ge(m1["kn_d"], r + 3)
                for k in range(KQ):
                    last = product(B_UQ, 2 * k + r, CQ_HI[:, k], CQ_LO[:, k], 4 - 2 * r, k == 0, k == KQ - 1)
                last.then_inc(w_used if r else m1["q_T"], 1)
            for n in range(4):
                b = B_UQ + 1 + n // 2
                weights_ready(pe, b)
                if n < 2:
                    pe.wait_ge(m1["rs"], n + 1)
                else:
                    pe.wait_ge(m1["q_a"], n - 1)
                    pe.wait_ge(m1["q_d"], n - 1)
                for k in range(KQ):
                    last = product(b, 2 * k + n % 2, CQ_HI[:, k], CQ_LO[:, k], 4 - 2 * (n % 2), k == 0, k == KQ - 1)
                last.then_inc(w_used if n % 2 else m1["q_T"], 1)
                if n == 1:
                    pe.wait_ge(m1["v_a"], 4)
                    pe.wait_ge(m1["v_d"], 3)
                    for r in range(2):
                        pe.wait_ge(m1["rs"], r + 1)
                        for s in range(2):
                            last = nc.tensor.matmul(PS[:, (6, 0)[r] + s, 0:HT], PERM[:], TF[:, r, s * HT:(s + 1) * HT],
                                                    start=True, stop=True)
                        last.then_inc(m1["perm_q"], 1)
            pe.wait_ge(m1["qr"], 2)
            pe.wait_ge(m1["q_a"], 4)
            pe.wait_ge(m1["q_d"], 4)
            with pe.Fori(0, 2) as i:
                for t in range(4):
                    weights_ready(pe, i * 4 + (B_VO + t))
                    pe.wait_ge(m1["proj"], i * 4 + (13 + t))
                    for k in range(KD):
                        last = product(B_VO + t, k, H_HI[:, k], H_LO[:, k], 2 * (t % 2), k == 0, k == KD - 1)
                    last.then_inc(w_used, 1)
            pe.wait_ge(m1["kr"], 1)
            for t, (c, n) in enumerate(FRAMES):
                last = nc.tensor.transpose(PS[0:n, 4, t * ROPE:(t + 1) * ROPE], KR[:, c:c + n], IDENT[0:ROPE, 0:ROPE])
            last.then_inc(m1["kr_T"], 1)

        def mix1_act(act):
            act.wait_ge(m1["cache_T"], 1)
            nc.scalar.activation(C_HI[:, :, T:TK], PS[:, 6, :].rearrange("p (k t) -> p k t", k=KC),
                                 ACT.Copy).then_inc(m1["cache_hi"], 1)
            nc.scalar.activation(KR[:, T:TK], PS[0:ROPE, 7, 0:PAST], ACT.Copy).then_inc(m1["kr_c"], 1)
            pre_root_act(act, pre[1])
            for i in range(KQ + KC):
                split_hi(act, B_AQ + i + 2)
                act.wait_ge(m1["proj"], i + 1)
                raw = AQRAW[:, i] if i < KQ else CRAW[:, i - KQ, 0:T]
                sq = (PAIR[:, 0], PAIR[:, 1], ACC[:], TF[:, 0], TF[:, 1])[i]
                nc.scalar.activation(sq, raw, ACT.Square).then_inc(m1["sq"], 1)
            act.wait_ge(m1["aq_sum"], 1)
            frame_roots(2, QL).then_inc(m1["aq_root"], 1)
            split_hi(act, B_SMALL + 2)
            act.wait_ge(m1["c_sum"], 1)
            act.wait_ge(m1["aq_inv"], 1)
            frame_roots(6, KVL).then_inc(m1["c_root"], 1)
            act.wait_ge(m1["lf1"], 1)
            settle(act, "act", act_step, nc.scalar.activation(GR[:], LF[:], ACT.Abs))
            settle(act, "act", act_step, nc.scalar.activation(GR[:], GR[:], ACT.Exp, scale=-1.0))
            nc.scalar.activation(GR[:], GR[:], ACT.Ln, bias=1.0).then_inc(m1["soft"], 1)
            for n in range(2 * MH):
                split_hi(act, B_QK + n + 2)
                if n == 4:
                    act.wait_ge(m1["c_T"], 1)
                    nc.scalar.activation(CSTAGE[:, 0:4], PS[:, 6:8, :].rearrange("p b (t c) -> p (b t) c", t=2), ACT.Copy)
                    nc.scalar.activation(CSTAGE[0:DEC, 4], PS[0:DEC, 4, 0:KVL], ACT.Copy).then_inc(m1["c_staged"], 1)
                if n == 6:
                    act.wait_ge(m1["mm"], 1)
                    nc.scalar.activation(EM[:], MX[:], ACT.Exp, scale=-1.0).then_inc(m1["em"], 1)
            act.wait_ge(m1["c_stored"], 32)
            for n in range(AH // 2):
                act.wait_ge(w_used if n == 3 else m1["kn_T"], B_UKV + 1 if n == 3 else n + 1)
                nc.scalar.activation(halves(KH[0:NOPE, 2 * n], TK // 2), pair(4 - 2 * (n % 2), NOPE, TK // 2),
                                     ACT.Copy).then_inc(m1["kn_a"], 1)
            split_hi(act, B_UKV + 2, 6)
            act.wait_ge(m1["gate_T"], 1)
            nc.scalar.activation(GC[:, 0:4], PS[:, 7, 0:16].rearrange("p (t h) -> p t h", h=MH), ACT.Copy)
            nc.scalar.activation(GC[0:DEC, 4], PS[0:DEC, 7, 16:20], ACT.Copy)
            nc.scalar.activation(EMC[:, 0:4], PS[:, 7, 20:36].rearrange("p (t h) -> p t h", h=MH), ACT.Copy)
            nc.scalar.activation(EMC[0:DEC, 4], PS[0:DEC, 7, 36:40], ACT.Copy).then_inc(m1["gate_c"], 1)
            for s in range(0, 7, 2):
                n = KEY_TILES[s][1]
                act.wait_ge(w_used if s == 6 else m1["v_T"], B_UKV + 2 if s == 6 else s + 1)
                nc.scalar.activation(VA[0:n, s, 0:AH * AV], PS[0:n, (0, 1, 6, 7)[s % 4], :], ACT.Copy).then_inc(m1["v_a"], 1)
            split_hi(act, B_UKV + 3, 6)
            for r in range(2):
                act.wait_ge(w_used if r else m1["q_T"], B_UQ + 1 if r else 1)
                nc.scalar.activation(halves(TF[:, r]), pair(4 - 2 * r), ACT.Copy).then_inc(m1["rs"], 1)
            split_hi(act, B_UQ + 2, 6)
            for n in range(4):
                act.wait_ge(w_used if n % 2 else m1["q_T"], B_UQ + n // 2 + 2 if n % 2 else n // 2 + 2)
                nc.scalar.activation(halves(QH[0:NOPE, 2 * n]), pair(4 - 2 * (n % 2), NOPE), ACT.Copy).then_inc(m1["q_a"], 1)
                if n % 2:
                    split_hi(act, B_UQ + n // 2 + 3)
            with act.Fori(0, 2) as i:
                for t in range(4):
                    b = B_VO + t + 2
                    split_hi(act, b, 8, i * 4 + b, i * 16 + arrived(b))
            act.wait_ge(m1["kr_T"], 1)
            act.wait_ge(m1["rope_in"], 1)
            nc.scalar.activation(KSTAGE[:, 0:4], PS[:, 4, 0:4 * ROPE].rearrange("p (t c) -> p t c", c=ROPE), ACT.Copy)
            nc.scalar.activation(KSTAGE[0:DEC, 4], PS[0:DEC, 4, 4 * ROPE:5 * ROPE], ACT.Copy).then_inc(m1["kr_staged"], 1)

        def mix1_dve(dve):
            dve.wait_ge(m1["cache_hi"], 1)
            nc.vector.tensor_tensor(C_LO[:, :, T:TK], PS[:, 6, :].rearrange("p (k t) -> p k t", k=KC),
                                    C_HI[:, :, T:TK].bitcast(F32), ALU.subtract).then_inc(m1["cache_lo"], 1)
            pre_dve(dve, pre[1])

            def evacuate(dst, src, count, scale=None, rows=None):
                dve.wait_ge(w_used, count)
                return scaled(dst, src, scale)

            def scaled(dst, src, scale=None, factor=RB[:]):
                if scale is None:
                    return nc.vector.tensor_tensor(halves(dst), src, halves(factor), ALU.mult)
                return nc.vector.scalar_tensor_tensor(out=halves(dst), in0=src, scalar=scale, in1=halves(factor),
                                                      op0=ALU.mult, op1=ALU.mult)

            def inverse(root, inv):
                dve.wait_ge(m1[root], 1)
                nc.vector.reciprocal(INV[:], ROOT[:]).then_inc(m1[inv], 1)

            def normed(raw, bank, gain, n, done):
                for i in range(n):
                    g = GROW[gain] + i
                    nc.vector.scalar_tensor_tensor(out=raw(i), in0=raw(i), scalar=GCOLS[:, g:g + 1], in1=spread_at(bank),
                                                   op0=ALU.mult, op1=ALU.mult).then_inc(done, 1)

            def qk(n):
                evacuate(PJ1[:, n], pair(2 * (n % 2)), B_QK + n + 1, None if n < MH else P ** -0.5).then_inc(m1["proj"], 1)
                split_lo(dve, B_QK + n + 2)

            split_lo(dve, B_AQ + 2)
            pre_factor_dve(dve, pre[1])
            for i in range(KQ + KC):
                dst = AQRAW[:, i] if i < KQ else CRAW[:, i - KQ, 0:T]
                evacuate(dst, pair((0, 2, 4, 6, 0)[i]), B_AQ + i + 1).then_inc(m1["proj"], 1)
                if i:
                    split_lo(dve, B_AQ + i + 2)
            inverse("aq_root", "aq_inv")
            dve.wait_ge(w_used, B_SMALL + 1)
            for row, dst, n in ((0, ARS, ROPE), (32, IG, MH), (64, LF, MH)):
                last = scaled(dst[:], PS[row:row + n, 4:6, 0:HT], factor=RB[row:row + n, :])
            last.then_inc(m1["proj"], 1)
            split_lo(dve, B_SMALL + 2)
            dve.wait_ge(m1["aq_spread"], 1)
            normed(lambda i: AQRAW[:, i], 2, "q_a_g", KQ, m1["cq"])
            inverse("c_root", "c_inv")
            qk(0)
            dve.wait_ge(m1["c_spread"], 1)
            normed(lambda i: CRAW[:, i, 0:T], 6, "kv_a_g", KC, m1["c"])
            qk(1)
            dve.wait_ge(m1["perm"], 1)
            dve.wait_ge(trig_in, 16)
            settle(dve, "dve", dve_step, nc.vector.tensor_tensor(PAIR[0:ROPE, 1], ARS[:], TRIG[0:ROPE, 0], ALU.mult))
            settle(dve, "dve", dve_step, nc.vector.tensor_tensor(
                halves(KR[:, 0:T]), pair(4, ROPE), halves(TRIG[0:ROPE, 1]), ALU.mult))
            nc.vector.tensor_tensor(KR[:, 0:T], KR[:, 0:T], PAIR[0:ROPE, 1], ALU.add).then_inc(m1["kr"], 1)
            qk(2)
            dve.wait_ge(m1["lf"], 1)
            dve.wait_ge(m1["cq"], KQ)
            for lo, hi in ((0, SEQ), (SEQ, T)):
                last = nc.vector.tensor_tensor_scan(out=BC[:, lo:hi], data0=ONES4[:, lo:hi], data1=LF[:, lo:hi],
                                                    initial=0.0, op0=ALU.mult, op1=ALU.add)
            settle(dve, "dve", dve_step, last)
            settle(dve, "dve", dve_step, nc.vector.tensor_tensor(GR[:], IG[:], BC[:], ALU.subtract))
            qk(3)
            nc.vector.tensor_tensor_scan(out=MX[:, 0:SEQ], data0=GR[:, 0:SEQ], data1=GR[:, 0:SEQ],
                                         initial=0.0, op0=ALU.max, op1=ALU.max)
            dve.wait_ge(bias_in, 64)
            settle(dve, "dve", dve_step, nc.vector.tensor_tensor_scan(
                out=MX[:, SEQ:T], data0=GR[:, SEQ:T], data1=GR[:, SEQ:T], initial=BIAS[:, 2:3], op0=ALU.max, op1=ALU.max))
            qk(4)
            nc.vector.tensor_scalar(NM[:], MX[:], -1.0, None, ALU.mult)
            settle(dve, "dve", dve_step, nc.vector.tensor_tensor(MX[:], MX[:], BC[:], ALU.add))
            nc.vector.tensor_copy(MEND[:, 0:1], MX[:, SEQ - 1:SEQ])
            nc.vector.tensor_copy(MEND[:, 1:2], MX[:, T - 1:T]).then_inc(m1["mm"], 1)
            for n in range(5, 2 * MH):
                qk(n)
            dve.wait_ge(m1["c_stored"], 32)
            for n in range(AH // 2):
                dve.wait_ge(w_used if n == 3 else m1["kn_T"], B_UKV + 1 if n == 3 else n + 1)
                nc.vector.tensor_copy(halves(KH[0:NOPE, 2 * n + 1], TK // 2),
                                      PS[NOPE:P, 4 - 2 * (n % 2):6 - 2 * (n % 2), 0:TK // 2]).then_inc(m1["kn_d"], 1)
            split_lo(dve, B_UKV + 2, 6)
            dve.wait_ge(m1["gate_T"], 1)
            nc.vector.memset(VA[:, :, AH * AV:VAW], 0.0)
            for s in range(1, 7, 2):
                n = KEY_TILES[s][1]
                dve.wait_ge(m1["v_T"], s + 1)
                nc.vector.tensor_copy(VA[0:n, s, 0:AH * AV], PS[0:n, (0, 1, 6, 7)[s % 4], :]).then_inc(m1["v_d"], 1)
            split_lo(dve, B_UKV + 3, 6)
            for n in range(4):
                if n == 0:
                    split_lo(dve, B_UQ + 2, 6)
                dve.wait_ge(w_used if n % 2 else m1["q_T"], B_UQ + n // 2 + 2 if n % 2 else n // 2 + 2)
                nc.vector.tensor_copy(halves(QH[0:NOPE, 2 * n + 1]),
                                      PS[NOPE:P, 4 - 2 * (n % 2):6 - 2 * (n % 2), 0:HT]).then_inc(m1["q_d"], 1)
                if n % 2:
                    split_lo(dve, B_UQ + n // 2 + 3)
                if n == 1:
                    for r in range(2):
                        dve.wait_ge(m1["rs"], r + 1)
                        settle(dve, "dve", dve_step, nc.vector.tensor_tensor(PAIR[:, r], TF[:, r], TRIG[:, 0], ALU.mult))
                        dve.wait_ge(m1["perm_q"], r + 1)
                        settle(dve, "dve", dve_step, nc.vector.tensor_tensor(
                            halves(TF[:, r]), pair((6, 0)[r]), halves(TRIG[:, 1]), ALU.mult))
                        nc.vector.tensor_tensor(PAIR[:, r], PAIR[:, r], TF[:, r], ALU.add).then_inc(m1["qr"], 1)
            with dve.Fori(0, 2) as i:
                for t in range(4):
                    split_lo(dve, B_VO + t + 2, 8, i * 4 + (B_VO + t + 2))
                    dve.wait_ge(w_used, i * 4 + (B_VO + t + 1))
                    nc.vector.tensor_tensor(halves(PJ2[:, bass.ds(i * 4 + t, 1), :].rearrange("p a t -> p (a t)")),
                                            pair(2 * (t % 2)), halves(RB[:]), ALU.mult).then_inc(m1["proj"], 1)

        def cache_pool(pool):
            pool.wait_ge(w_used, MIX0)
            pool.dma_start(CIN[:], a["cache_kv_latent"][0, 0].rearrange("(t p) c -> p t c", p=P)).then_inc(cache_in, 16)
            pool.dma_start(KIN[:], a["cache_k_rope"][0, 0].rearrange("(t p) c -> p t c", p=P)).then_inc(cache_in, 16)

        def mix1_pool(pool):
            def split(src, hi, lo, done):
                settle(pool, "pool", pool_step, nc.gpsimd.tensor_copy(hi, src))
                nc.gpsimd.tensor_tensor(lo, src, hi.bitcast(F32), ALU.subtract).then_inc(done, 1)

            pool.wait_ge(m1["proj"], 6)
            pool.wait_ge(bias_in, 64)
            settle(pool, "pool", pool_step, nc.gpsimd.tensor_scalar(IG[:], IG[:], BIAS[:, 0:1], None, ALU.add))
            nc.gpsimd.memset(ONES4[:], 1.0)
            nc.gpsimd.tensor_scalar(LF[:], LF[:], BIAS[:, 1:2], None, ALU.add).then_inc(m1["lf1"], 1)
            pool.wait_ge(m1["soft"], 1)
            settle(pool, "pool", pool_step, nc.gpsimd.tensor_scalar(LF[:], LF[:], 0.0, None, ALU.min))
            nc.gpsimd.tensor_tensor(LF[:], LF[:], GR[:], ALU.subtract).then_inc(m1["lf"], 1)
            for i in range(KQ):
                pool.wait_ge(m1["cq"], i + 1)
                split(AQRAW[:, i], CQ_HI[:, i], CQ_LO[:, i], m1["cq_lo"])
            for i in range(KC):
                pool.wait_ge(m1["c"], i + 1)
                split(CRAW[:, i, 0:T], C_HI[:, i, 0:T], C_LO[:, i, 0:T], m1["c_lo"])
            pool.wait_ge(m1["c_staged"], 1)
            pool.dma_start(p_kv[0, 0].rearrange("(t p) c -> p t c", p=P), CSTAGE[:, 0:4]).then_inc(m1["c_stored"], 16)
            pool.dma_start(s_kv[0, 0], CSTAGE[0:DEC, 4]).then_inc(m1["c_stored"], 16)
            pool.wait_ge(m1["mm"], 1)
            pool.dma_start(p_m[0].rearrange("b h -> h b"), MEND[:, 0:1]).then_inc(st["stored"], 16)
            pool.dma_start(s_m[0].rearrange("b h -> h b"), MEND[:, 1:2]).then_inc(st["stored"], 16)
            pool.wait_ge(m1["c_stored"], 32)
            pool.wait_ge(m1["kr"], 1)
            pool.wait_ge(m1["c_lo"], KC)
            for h in range(AH):
                settle(pool, "pool", pool_step, nc.gpsimd.tensor_copy(KH[NOPE:QK, h], KR[:]))
            for h in range(AH):
                if h % 4 == 0:
                    pool.wait_ge(m1["qr"], h // 4 + 1)
                settle(pool, "pool", pool_step, nc.gpsimd.tensor_copy(
                    QH[NOPE:QK, h], PAIR[(h % 4) * ROPE:(h % 4 + 1) * ROPE, h // 4]))
            pool.sem_inc(m1["rope_in"], 1)
            pool.wait_ge(m1["kr_staged"], 1)
            pool.dma_start(p_kr[0, 0].rearrange("(t p) c -> p t c", p=P), KSTAGE[:, 0:4]).then_inc(st["stored"], 16)
            pool.dma_start(s_kr[0, 0], KSTAGE[0:DEC, 4]).then_inc(st["stored"], 16)

        m2 = names("m2", "v_T", "k_T", "v_c", "k_c", "c0_T", "c0_c", "ones_v", "nb_T", "nb", "we", "s_T", "arg", "dexp",
                   "tri", "wgt", "o_T", "os", "sq", "var", "root", "hn", "h_T", "mf", "hi", "lo", "vw", "qw", "st_T",
                   "st_c", "st_v", "sig", "state_out")
        DOFF = {0: 0, 1: 512, 3: 896, 2: 1024, 4: 1280}
        DLEN = {i: SEQ - i * P for i in range(4)}
        DLEN[4] = DEC

        def nb_of(h):
            return RB[:] if h % 2 == 0 else PAIR[:, 0]

        def mix2_pe(pe):
            pe.wait_ge(m1["proj"], 22)
            for t, (c, n) in enumerate(FRAMES):
                for h in range(MH):
                    last = nc.tensor.transpose(PS[0:n, t, h * P:(h + 1) * P], PJ2[:, h, c:c + n], IDENT[:])
                last.then_inc(m2["v_T"], 1)
                if t == 0:
                    pe.wait_ge(m1["kr_staged"], 1)
            for t, (c, n) in enumerate(FRAMES):
                if t >= 3:
                    pe.wait_ge(m2["v_c"], t - 2)
                for h in range(MH):
                    last = nc.tensor.transpose(PS[0:n, (5 + t) % 8, h * P:(h + 1) * P], PJ1[:, MH + h, c:c + n], IDENT[:])
                last.then_inc(m2["k_T"], 1)
            pe.wait_ge(state_in, 48)
            pe.wait_ge(m2["v_c"], 4)
            for h in range(MH):
                nc.tensor.transpose(PS[:, 2, h * P:(h + 1) * P], C0[:, h, :], IDENT[:])
            nc.tensor.transpose(PS[:, 3, 0:MH], N0R[:], IDENT[0:MH, 0:MH]).then_inc(m2["c0_T"], 1)
            pe.wait_ge(m2["c0_c"], 1)
            pe.wait_ge(m2["v_c"], TT)
            pe.wait_ge(m2["k_c"], TT)

            def scores(h):
                for s in range(2):
                    last = nc.tensor.matmul(PS[:, 3 + s, 0:HT], SEL[:, h, :], NM[:, s * HT:(s + 1) * HT], start=True, stop=True)
                last.then_inc(m2["nb_T"], 1)
                if h:
                    pe.wait_ge(m2["wgt"], h)
                for i, (c, n) in enumerate(FRAMES):
                    last = nc.tensor.matmul(PSF[0:n, DOFF[i]:DOFF[i] + DLEN[i]], PJ1[:, MH + h, c:c + n],
                                            PJ1[:, h, c:(SEQ if i < 4 else T)], start=True, stop=True)
                last.then_inc(m2["s_T"], 1)

            def outputs(h):
                pe.wait_ge(m2["wgt"], h + 1)
                pe.wait_ge(m2["ones_v"], 1)
                if h:
                    pe.wait_ge(m2["os"], h)
                for j in range(4):
                    dst = PS[:, 5 + j // 3, (j % 3) * VP:(j % 3 + 1) * VP]
                    for i in range(j + 1):
                        nc.tensor.matmul(dst, DW[:, DOFF[i] + (j - i) * P:DOFF[i] + (j - i + 1) * P], VT[:, i, h, :],
                                         start=i == 0, stop=i == j)
                dst = PS[0:DEC, 6, VP:2 * VP]
                nc.tensor.matmul(dst, DW[0:DEC, DOFF[4]:DOFF[4] + DEC], VT[0:DEC, 4, h, :], start=True, stop=False)
                pe.wait_ge(m2["qw"], h + 1)
                nc.tensor.matmul(dst, PAIR[:, 1, DEC:2 * DEC], C0T[:, h, :], start=False, stop=True).then_inc(m2["o_T"], 1)

            def states(h):
                pe.wait_ge(m2["vw"], h + 1)
                if h:
                    pe.wait_ge(m2["st_c"], h)
                    pe.wait_ge(m2["st_v"], h)
                for i in range(4):
                    nc.tensor.matmul(PS[:, 7, 0:P], VW[:, i, :], KT[:, i, h, :], start=i == 0, stop=i == 3)
                nc.tensor.matmul(PS[:, 7, P:2 * P], VW[0:DEC, 4, :], KT[0:DEC, 4, h, :], start=True, stop=True)
                for i in range(4):
                    nc.tensor.matmul(PS[0:1, 7, 2 * P:3 * P], WE[:, i:i + 1], KT[:, i, h, :], start=i == 0, stop=i == 3)
                nc.tensor.matmul(PS[0:1, 7, 3 * P:4 * P], WE[0:DEC, 4:5], KT[0:DEC, 4, h, :],
                                 start=True, stop=True).then_inc(m2["st_T"], 1)

            def back(h):
                pe.wait_ge(m2["hn"], h + 1)
                for t, (c, n) in enumerate(FRAMES):
                    last = nc.tensor.transpose(PSF[:, 3 * 512 + c:3 * 512 + c + n], HN[0:n, t, :], IDENT[0:n, 0:n])
                last.then_inc(m2["h_T"], 1)

            scores(0)
            for h in range(MH):
                outputs(h)
                states(h)
                if h + 1 < MH:
                    if h:
                        pe.wait_ge(m2["mf"], h)
                    scores(h + 1)
                    pe.wait_ge(m2["nb"], h + 2)
                back(h)

        def mix2_act(act):
            for t, (c, n) in enumerate(FRAMES):
                act.wait_ge(m2["v_T"], t + 1)
                nc.scalar.activation(VT[0:n, t, :, 0:P], PS[0:n, t, :].rearrange("p (h v) -> p h v", h=MH),
                                     ACT.Copy).then_inc(m2["v_c"], 1)
            act.wait_ge(m2["c0_T"], 1)
            nc.scalar.activation(C0T[:, :, 0:P], PS[:, 2, :].rearrange("p (h v) -> p h v", h=MH), ACT.Copy)
            for i in range(2):
                last = nc.scalar.activation(C0T[:, :, P + i], PS[:, 3, 0:MH], ACT.Copy)
            last.then_inc(m2["c0_c"], 1)
            act.wait_ge(m1["proj"], 22)
            nc.scalar.activation(PJ2[:, MH:2 * MH], PJ2[:, MH:2 * MH], ACT.Sigmoid).then_inc(m2["sig"], 1)
            act.wait_ge(m2["ones_v"], 1)

            def decays(h):
                nb = nb_of(h)
                act.wait_ge(m2["nb_T"], h + 1)
                if h >= 1:
                    act.wait_ge(m2["qw"], h)
                    act.wait_ge(m2["o_T"], h)
                    act.wait_ge(m2["vw"], h)
                    act.wait_ge(m2["st_T"], h)
                    act.wait_ge(m2["st_v"], h)
                settle(act, "act", act_step, nc.scalar.activation(halves(nb), pair(3), ACT.Copy))
                nc.scalar.activation(PAIR[:, 1, 0:DEC], nb[:, SEQ:T], ACT.Exp, bias=M0B[:, h:h + 1]).then_inc(m2["nb"], 1)
                nc.scalar.activation(WE[:, 0:4], GC[:, 0:4, h], ACT.Exp, bias=nb[:, SEQ - 1:SEQ])
                nc.scalar.activation(WE[0:DEC, 4:5], GC[0:DEC, 4, h:h + 1], ACT.Exp,
                                     bias=nb[0:DEC, T - 1:T]).then_inc(m2["we"], 1)
                act.wait_ge(m2["arg"], h + 1)
                nc.scalar.activation(DW[:, 0:1280], DW[:, 0:1280], ACT.Exp)
                nc.scalar.activation(DW[0:DEC, 1280:1344], DW[0:DEC, 1280:1344], ACT.Exp).then_inc(m2["dexp"], 1)

            decays(0)
            for h in range(MH):
                act.wait_ge(m2["o_T"], h + 1)
                if h:
                    act.wait_ge(m2["hn"], h)
                nc.scalar.activation(OS[:, 0:3], PS[:, 5, 0:3 * VP].rearrange("p (t v) -> p t v", t=3), ACT.Copy)
                nc.scalar.activation(OS[:, 3], PS[:, 6, 0:VP], ACT.Copy)
                settle(act, "act", act_step, nc.scalar.activation(OS[0:DEC, 4], PS[0:DEC, 6, VP:2 * VP], ACT.Copy))
                act.sem_inc(m2["os"], 1)
                if h:
                    act.wait_ge(m2["h_T"], h)
                nc.scalar.activation(HN[:], OS[:, :, 0:P], ACT.Square).then_inc(m2["sq"], 1)
                act.wait_ge(m2["st_T"], h + 1)
                if h >= 2:
                    act.wait_ge(m2["state_out"], 64 * (h - 1))
                nc.scalar.activation(CN[:, h % 2, 0], PS[:, 7, 0:P], ACT.Copy)
                if h:
                    act.wait_ge(m2["state_out"], 64 * h)
                nc.scalar.activation(NN[:, 0], PS[0:1, 7, 2 * P:3 * P], ACT.Copy).then_inc(m2["st_c"], 1)
                act.wait_ge(m2["var"], h + 1)
                nc.scalar.activation(S5[:, 3], S5[:, 2], ACT.Sqrt, bias=EPSC[:], scale=1.0 / P).then_inc(m2["root"], 1)
                if h + 1 < MH:
                    decays(h + 1)
                act.wait_ge(m2["mf"], h + 1)
                nc.scalar.activation(MA_HI[:, h], TF[:, h % 2], ACT.Copy).then_inc(m2["hi"], 1)

        def mix2_dve(dve):
            for t, (c, n) in enumerate(FRAMES):
                dve.wait_ge(m2["k_T"], t + 1)
                nc.vector.tensor_copy(KT[0:n, t], PS[0:n, (5 + t) % 8, :].rearrange("p (h v) -> p h v", h=MH)).then_inc(m2["k_c"], 1)
            dve.wait_ge(m2["ones_v"], 1)

            def args(h):
                nb = nb_of(h)
                dve.wait_ge(m2["nb"], h + 1)
                nc.vector.tensor_tensor(PAIR[:, 1, DEC:2 * DEC], PJ1[:, h, SEQ:T], PAIR[:, 1, 0:DEC], ALU.mult).then_inc(m2["qw"], 1)
                if h:
                    dve.wait_ge(m2["o_T"], h)
                for i, (c, n) in enumerate(FRAMES):
                    end = SEQ if i < 4 else T
                    last = nc.vector.tensor_scalar(DW[0:n, DOFF[i]:DOFF[i] + DLEN[i]], nb[0:n, c:end],
                                                   GC[0:n, i, h:h + 1], 0.0, ALU.add, ALU.min)
                last.then_inc(m2["arg"], 1)

            def weights(h):
                dve.wait_ge(m2["tri"], h + 1)
                dve.wait_ge(m2["s_T"], h + 1)
                nc.vector.tensor_tensor(DW[:, 0:1280], DW[:, 0:1280], PSF[:, 0:1280], ALU.mult)
                nc.vector.tensor_tensor(DW[0:DEC, 1280:1344], DW[0:DEC, 1280:1344], PSF[0:DEC, 1280:1344],
                                        ALU.mult).then_inc(m2["wgt"], 1)

            args(0)
            weights(0)
            for h in range(MH):
                dve.wait_ge(m2["sq"], h + 1)
                den = OS[:, :, P:P + 1].rearrange("p t o -> p (t o)")
                settle(dve, "dve", dve_step, nc.vector.tensor_scalar(S5[:, 0], den, -1.0, None, ALU.mult))
                settle(dve, "dve", dve_step, nc.vector.tensor_tensor(S5[:, 0], S5[:, 0], den, ALU.max))
                settle(dve, "dve", dve_step, nc.vector.tensor_tensor(S5[:, 0], S5[:, 0], EMC[:, :, h], ALU.max))
                settle(dve, "dve", dve_step, nc.vector.reciprocal(S5[:, 1], S5[:, 0]))
                settle(dve, "dve", dve_step, nc.vector.tensor_reduce(S5[:, 2], HN[:], AX, ALU.add))
                settle(dve, "dve", dve_step, nc.vector.tensor_tensor(S5[:, 2], S5[:, 2], S5[:, 1], ALU.mult))
                nc.vector.tensor_tensor(S5[:, 2], S5[:, 2], S5[:, 1], ALU.mult).then_inc(m2["var"], 1)
                dve.wait_ge(m2["st_c"], h + 1)
                if h >= 2:
                    dve.wait_ge(m2["state_out"], 64 * (h - 1))
                wst = PAIR[:, 1, DEC - 1:DEC]
                nc.vector.scalar_tensor_tensor(out=CN[:, h % 2, 1], in0=C0[:, h, :], scalar=wst, in1=PS[:, 7, P:2 * P],
                                               op0=ALU.mult, op1=ALU.add)
                if h:
                    dve.wait_ge(m2["state_out"], 64 * h)
                nc.vector.scalar_tensor_tensor(out=NN[:, 1], in0=N0[:, h, :], scalar=wst[0:1], in1=PS[0:1, 7, 3 * P:4 * P],
                                               op0=ALU.mult, op1=ALU.add).then_inc(m2["st_v"], 1)
                if h + 1 < MH:
                    args(h + 1)
                dve.wait_ge(m2["root"], h + 1)
                settle(dve, "dve", dve_step, nc.vector.reciprocal(S5[:, 4], S5[:, 3]))
                settle(dve, "dve", dve_step, nc.vector.tensor_tensor(S5[:, 4], S5[:, 4], S5[:, 1], ALU.mult))
                nc.vector.tensor_tensor(HN[:], OS[:, :, 0:P], S5[:, 4:5, :].rearrange("p o t -> p t o").to_broadcast([P, TT, P]),
                                        ALU.mult).then_inc(m2["hn"], 1)
                if h + 1 < MH:
                    weights(h + 1)
                dve.wait_ge(m2["h_T"], h + 1)
                dve.wait_ge(m2["sig"], 1)
                if h >= 2:
                    dve.wait_ge(m2["lo"], h - 1)
                g = GROW["m_head_g"] + h
                nc.vector.scalar_tensor_tensor(out=TF[:, h % 2], in0=PSF[:, 3 * 512:3 * 512 + T], scalar=GCOLS[:, g:g + 1],
                                               in1=PJ2[:, MH + h], op0=ALU.mult, op1=ALU.mult).then_inc(m2["mf"], 1)

        def mix2_pool(pool):
            pool.wait_ge(w_used, B_OUT)
            pool.dma_start(C0[:], a["state_C"][0, 0].rearrange("h v k -> v h k")).then_inc(state_in, 16)
            pool.dma_start(N0R[:], a["state_n"][0, 0]).then_inc(state_in, 16)
            pool.wait_ge(m1["kr_T"], 1)
            pool.dma_start(N0[:], a["state_n"][0, 0:1]).then_inc(state_in, 16)
            nc.gpsimd.memset(VT[:, :, :, P:VP], 1.0)
            nc.gpsimd.memset(OS[:], 1.0).then_inc(m2["ones_v"], 1)

            def low(h):
                pool.wait_ge(m2["hi"], h + 1)
                nc.gpsimd.tensor_tensor(MA_LO[:, h], TF[:, h % 2], MA_HI[:, h].bitcast(F32), ALU.subtract).then_inc(m2["lo"], 1)

            for h in range(MH):
                pool.wait_ge(m2["dexp"], h + 1)
                for i in (0, 1, 2, 3, 4):
                    n = FRAMES[i][1]
                    blk = DW[0:n, DOFF[i]:DOFF[i] + n]
                    last = nc.gpsimd.affine_select(out=blk, in_=blk, compare_op=ALU.is_ge, fill=0.0, base=0,
                                                   pattern=[[1, n]], channel_multiplier=-1)
                last.then_inc(m2["tri"], 1)
                pool.wait_ge(m2["we"], h + 1)
                pool.wait_ge(m2["v_c"], TT)
                if h:
                    pool.wait_ge(m2["st_T"], h)
                for i, (c, n) in enumerate(FRAMES):
                    last = nc.gpsimd.tensor_scalar(VW[0:n, i], VT[0:n, i, h, 0:P], WE[0:n, i:i + 1], None, ALU.mult)
                last.then_inc(m2["vw"], 1)
                if h:
                    low(h - 1)
                pool.wait_ge(m2["st_c"], h + 1)
                pool.wait_ge(m2["st_v"], h + 1)
                pool.dma_start(p_C[0, 0, h], CN[:, h % 2, 0]).then_inc(m2["state_out"], 16)
                pool.dma_start(s_C[0, 0, h], CN[:, h % 2, 1]).then_inc(m2["state_out"], 16)
                pool.dma_start(p_n[0, 0, h:h + 1, :], NN[:, 0]).then_inc(m2["state_out"], 16)
                pool.dma_start(s_n[0, 0, h:h + 1, :], NN[:, 1]).then_inc(m2["state_out"], 16)
            low(MH - 1)

        m3 = names("m3", "s", "max", "bias", "p", "p_T", "pt_a", "pt_d", "o", "at", "a_T", "hi", "lo")
        SOFF = {3: 0, 2: 512, 0: 896, 1: 1024, 4: 1536}
        POFF = {3: 0, 2: 512, 0: 896, 1: 1024, 4: 1280}
        SLEN = {0: P, 1: 2 * P, 2: 3 * P, 3: 4 * P, 4: DEC + PAST}
        GROUP_A = [(3, i * P, P, i) for i in range(4)]
        GROUP_B = [(2, i * P, P, i) for i in range(3)] + [(0, 0, P, 0)]
        GROUP_C = [(1, 0, P, 0), (1, P, P, 1), (4, DEC, P, 5), (4, DEC + P, P, 6), (4, 0, DEC, 4)]

        def rows_of(j):
            return DEC if j == 4 else P

        def columns(group, base):
            out, at_ = [], base
            for blk in group:
                out.append((*blk, at_))
                at_ += rows_of(blk[0])
            return out

        BLOCKS = [columns(GROUP_A, 0), columns(GROUP_B, 512), columns(GROUP_C, 1024)]

        def mix3_pe(pe):
            pe.wait_ge(m2["wgt"], MH)
            pe.wait_ge(m2["mf"], MH)
            pe.wait_ge(m1["rope_in"], 1)

            def scores(h):
                if h:
                    pe.wait_ge(m3["p"], h)
                for j in (3, 2, 0, 1, 4):
                    n = rows_of(j)
                    k0 = SEQ if j == 4 else 0
                    last = nc.tensor.matmul(PSF[0:n, SOFF[j]:SOFF[j] + SLEN[j]], QH[:, h, j * P:j * P + n],
                                            KH[:, h, k0:k0 + SLEN[j]], start=True, stop=True)
                last.then_inc(m3["s"], 1)

            def turn(h):
                pe.wait_ge(m3["p"], h + 1)
                for g, bank in enumerate((4, 5, 4)):
                    if g == 2:
                        pe.wait_ge(m3["pt_d"], 2 * h + 1)
                    elif h:
                        pe.wait_ge(m3["pt_a"] if g else m3["pt_d"], h if g else 2 * h)
                        if g == 0 and h >= 3 and h % 2:
                            pe.wait_ge(m3["lo"], h // 2)
                    at_ = 0
                    for j, k0, kn, _, _ in BLOCKS[g]:
                        n = rows_of(j)
                        last = nc.tensor.transpose(PS[0:kn, bank, at_:at_ + n], PR[0:n, h % 2, POFF[j] + k0:POFF[j] + k0 + kn],
                                                   IDENT[0:n, 0:n])
                        at_ += n
                    last.then_inc(m3["p_T"], 1)

            def values(h):
                pe.wait_ge(m3["pt_d"], 2 * h + 2)
                pe.wait_ge(m3["pt_a"], h + 1)
                if h >= 2:
                    pe.wait_ge(m3["at"], h - 1)
                for j in range(TT):
                    blks = [b for g in BLOCKS for b in g if b[0] == j]
                    n = rows_of(j)
                    for i, (_, _, kn, kt, col) in enumerate(blks):
                        last = nc.tensor.matmul(PS[0:n, 6 + h % 2, 96 * j:96 * (j + 1)], PT[0:kn, h % 2, col:col + n],
                                                VA[0:kn, kt, AV * h:AV * h + 96], start=i == 0, stop=i == len(blks) - 1)
                last.then_inc(m3["o"], 1)

            def merge(c):
                pe.wait_ge(m3["at"], 2 * c + 2)
                for t, (f, n) in enumerate(FRAMES):
                    if t == 0:
                        pe.wait_ge(m3["pt_d"], 2 * min(2 * c + 2, AH - 1) + 2)
                        pe.wait_ge(m3["pt_a"], min(2 * c + 2, AH - 1) + 1)
                    last = nc.tensor.transpose(PSF[:, 4 * 512 + f:4 * 512 + f + n], AT[0:n, t, :], IDENT[0:n, 0:n])
                last.then_inc(m3["a_T"], 1)

            scores(0)
            for h in range(AH):
                turn(h)
                if h + 1 < AH:
                    scores(h + 1)
                if h and h % 2 == 0:
                    merge(h // 2 - 1)
                values(h)
            merge(AH // 2 - 1)

        def mix3_dve(dve):
            def softmax_max(h):
                dve.wait_ge(m3["s"], h + 1)
                if h:
                    dve.wait_ge(m3["p"], h)
                for j in range(4):
                    c = SOFF[j] + SLEN[j]
                    last = nc.vector.memset(PSF[0:DEC, c - DEC:c], MASKED)
                settle(dve, "dve", dve_step, last)
                for j in range(TT):
                    n = rows_of(j)
                    last = nc.vector.tensor_reduce(S5[0:n, 0, j:j + 1], PSF[0:n, SOFF[j]:SOFF[j] + SLEN[j]], AX, ALU.max,
                                                   negate=True)
                settle(dve, "dve", dve_step, last)
                nc.vector.tensor_scalar(S5[:, 1 + 4 * (h % 2)], S5[:, 0], A_SCALE, None, ALU.mult).then_inc(m3["bias"], 1)

            def turned(h, first):
                if h >= 2:
                    dve.wait_ge(m3["o"], h - 1)
                if first:
                    dve.wait_ge(m3["p_T"], 3 * h + 1)
                    nc.vector.tensor_copy(PT[:, h % 2, 0:512], PS[:, 4, :]).then_inc(m3["pt_d"], 1)
                else:
                    dve.wait_ge(m3["p_T"], 3 * h + 3)
                    nc.vector.tensor_copy(PT[:, h % 2, 1024:1408], PS[:, 4, 0:384])
                    nc.vector.tensor_copy(PT[0:DEC, h % 2, 1408:1472], PS[0:DEC, 4, 384:448]).then_inc(m3["pt_d"], 1)

            softmax_max(0)
            for h in range(AH):
                turned(h, True)
                turned(h, False)
                if h + 1 < AH:
                    softmax_max(h + 1)
                if h and h % 2 == 0:
                    low(dve, h // 2 - 1)
                dve.wait_ge(m3["o"], h + 1)
                sums = S5[:, 2 + 4 * (h % 2)]
                settle(dve, "dve", dve_step, nc.vector.reciprocal(S5[:, 3], sums))
                if h >= 2 and h % 2 == 0:
                    dve.wait_ge(m3["a_T"], h // 2)
                o_ = PS[:, 6 + h % 2, 0:480].rearrange("p (t v) -> p t v", v=96)[:, :, 0:AV]
                r_ = S5[:, 3:4, :].rearrange("p o t -> p t o")
                c = AV * (h % 2)
                nc.vector.tensor_tensor(AT[:, 0:4, c:c + AV], o_[:, 0:4], r_[:, 0:4].to_broadcast([P, 4, AV]), ALU.mult)
                nc.vector.tensor_tensor(AT[0:DEC, 4:5, c:c + AV], o_[0:DEC, 4:5], r_[0:DEC, 4:5].to_broadcast([DEC, 1, AV]),
                                        ALU.mult).then_inc(m3["at"], 1)
            low(dve, AH // 2 - 1)

        def low(dve, c):
            dve.wait_ge(m3["hi"], c + 1)
            nc.vector.tensor_tensor(MB_LO[:, c], PSF[:, 4 * 512:4 * 512 + T], MB_HI[:, c].bitcast(F32),
                                    ALU.subtract).then_inc(m3["lo"], 1)

        def mix3_act(act):
            act.wait_ge(m2["h_T"], MH)
            act.wait_ge(m2["st_T"], MH)
            act.wait_ge(m2["st_v"], MH)

            def exps(h):
                act.wait_ge(m3["bias"], h + 1)
                if h >= 2:
                    act.wait_ge(m3["p_T"], 3 * (h - 1))
                for j in range(TT):
                    n = rows_of(j)
                    last = nc.scalar.activation(PR[0:n, h % 2, POFF[j]:POFF[j] + SLEN[j]], PSF[0:n, SOFF[j]:SOFF[j] + SLEN[j]],
                                                ACT.Exp, bias=S5[0:n, 1 + 4 * (h % 2), j:j + 1], scale=A_SCALE,
                                                accum_out=S5[0:n, 2 + 4 * (h % 2), j:j + 1])
                last.then_inc(m3["p"], 1)

            exps(0)
            for h in range(AH):
                act.wait_ge(m3["p_T"], 3 * h + 2)
                if h >= 2:
                    act.wait_ge(m3["o"], h - 1)
                nc.scalar.activation(PT[:, h % 2, 512:1024], PS[:, 5, :], ACT.Copy).then_inc(m3["pt_a"], 1)
                if h and h % 2 == 0:
                    high(act, h // 2 - 1)
                if h + 1 < AH:
                    exps(h + 1)
            high(act, AH // 2 - 1)

        def high(act, c):
            act.wait_ge(m3["a_T"], c + 1)
            nc.scalar.activation(MB_HI[:, c], PSF[:, 4 * 512:4 * 512 + T], ACT.Copy).then_inc(m3["hi"], 1)

        def out_pe(pe, p):
            pe.wait_ge(m2["lo"], MH)
            pe.wait_ge(m3["lo"], AH // 2)

            def tiles(i, first=False):
                for t in range(4):
                    weights_ready(pe, i * 4 + (B_OUT + t))
                    if not (first and t < 2):
                        pe.wait_ge(p["y_copy"].sem, i * 4 + (t - 1) + p["y_copy"].base)
                    for k in range(KD):
                        hi, lo = (MA_HI[:, k], MA_LO[:, k]) if k < MH else (MB_HI[:, k - MH], MB_LO[:, k - MH])
                        last = product(B_OUT + t, k, hi, lo, 4 + 2 * (t % 2), k == 0, k == KD - 1)
                    last.then_inc(w_used, 1)

            tiles(0, first=True)
            tiles(1)

        def out_act(act, p):
            for m in range(KD):
                act.wait_ge(w_used, B_OUT + m + 1)
                y_out(act, p, m, m % 2, 4 + 2 * (m % 2), "mix_post_g", m < 2)
                split_hi(act, B_OUT + m + 2)

        def out_dve(dve):
            for m in range(KD):
                split_lo(dve, B_OUT + m + 2)

        block = ctx.enter_context(nc.Block())

        @block.sync
        def _(sp):
            start_sp(sp)
            load_ffn(sp, 0, a["ff1_w_gate"][0], a["ff1_w_up"][0], a["ff1_w_down"][0])
            load_mix(sp)
            load_ffn(sp, FF2_0, a["ff2_w_gate"][0], a["ff2_w_up"][0], a["ff2_w_down"][0])
            finish_sp(sp)

        @block.gpsimd
        def _(pool):
            start_pool(pool)
            acc_pool(pool, post[0])
            cache_pool(pool)
            post_pool(pool, post[0])
            mix1_pool(pool)
            mix2_pool(pool)
            acc_pool(pool, post[1])
            post_pool(pool, post[1])
            acc_pool(pool, post[2])
            post_pool(pool, post[2])

        @block.scalar
        def _(act):
            pre_act(act, pre[0], None, PRE_GAINS[0], split=True)
            pre_root_act(act, pre[0])
            ffn_act(act, ff[0], post[0], 0, "ff1_post_g")
            post_act(act, post[0])
            pre_act(act, pre[1], post[0], PRE_GAINS[1])
            mix1_act(act)
            mix2_act(act)
            mix3_act(act)
            out_act(act, post[1])
            post_act(act, post[1])
            pre_act(act, pre[2], post[1], PRE_GAINS[2])
            pre_root_act(act, pre[2])
            ffn_act(act, ff[1], post[2], FF2_0, "ff2_post_g")
            post_act(act, post[2])
            finish_act(act)

        @block.vector
        def _(dve):
            start_dve(dve)
            pre_dve(dve, pre[0])
            ffn_dve(dve, ff[0], pre[0], 0)
            post_dve(dve, post[0], pre[1])
            mix1_dve(dve)
            mix2_dve(dve)
            mix3_dve(dve)
            out_dve(dve)
            post_dve(dve, post[1], pre[2])
            pre_dve(dve, pre[2])
            ffn_dve(dve, ff[1], pre[2], FF2_0)
            post_dve(dve, post[2])

        @block.tensor
        def _(pe):
            start_pe(pe)
            ffn_pe(pe, ff[0], pre[0], post[0], 0)
            post_pe(pe, post[0])
            mix1_pe(pe)
            mix2_pe(pe)
            mix3_pe(pe)
            out_pe(pe, post[1])
            post_pe(pe, post[1])
            ffn_pe(pe, ff[1], pre[2], post[2], FF2_0)
            post_pe(pe, post[2])
            finish_pe(pe)


INPUTS = ["x_prompt", "x_sample", "cache_kv_latent", "cache_k_rope", "state_C", "state_n", "state_m",
          "ff1_pre_g", "ff1_w_gate", "ff1_w_up", "ff1_w_down", "ff1_post_g",
          "mix_pre_g", "w_in", "b_igate", "b_fgate", "q_a_g", "w_uq", "kv_a_g", "w_ukv", "m_head_g", "w_out",
          "mix_post_g", "ff2_pre_g", "ff2_w_gate", "ff2_w_up", "ff2_w_down", "ff2_post_g"]
OUTPUTS = [(1, SEQ, D), (1, DEC, D),
           (1, 1, SEQ, KVL), (1, 1, SEQ, ROPE), (1, 1, MH, P, P), (1, 1, MH, P), (1, 1, MH),
           (1, 1, DEC, KVL), (1, 1, DEC, ROPE), (1, 1, MH, P, P), (1, 1, MH, P), (1, 1, MH)]


def kernel(**inputs):
    import numpy as np
    import concourse.bacc as bacc
    from concourse.bass_utils import run_bass_kernel_spmd

    half = ROPE // 2
    pos = np.concatenate([np.arange(SEQ), PAST + np.arange(DEC)]).astype(np.float32)
    freq = (np.float32(10000.0) ** (-np.arange(half, dtype=np.float32) / np.float32(half))).astype(np.float32)
    ang = (freq[:, None] * pos[None, :]).astype(np.float32)
    cos, sin = np.cos(ang), np.sin(ang)
    rope = np.stack([np.concatenate([cos, cos]), np.concatenate([-sin, sin])], axis=1)
    rope = np.ascontiguousarray(np.concatenate([rope] * (P // ROPE)), dtype=np.float32)

    nc = bacc.Bacc("TRN2", target_bir_lowering=False, num_devices=1)
    arrays, aps = {}, {}
    for name in INPUTS:
        x = np.ascontiguousarray(inputs[name])
        arrays[f"in_{name}"] = x
        aps[name] = nc.dram_tensor(f"in_{name}", x.shape, mybir.dt.from_np(x.dtype), kind="ExternalInput").ap()
    arrays["rope_table"] = rope
    table = nc.dram_tensor("rope_table", rope.shape, F32, kind="ExternalInput").ap()
    outs = [nc.dram_tensor(f"out_{i}", s, F32, kind="ExternalOutput").ap() for i, s in enumerate(OUTPUTS)]
    build(nc, aps, table, outs)
    r = run_bass_kernel_spmd(nc, [arrays], core_ids=[0])
    return tuple(r.results[0][f"out_{i}"] for i in range(len(OUTPUTS)))
```

```python
from contextlib import ExitStack

import concourse.bass as bass
from concourse import mybir

P = 128
D = 1024
KD = D // P
SEQ = 512
DEC = 64
T = SEQ + DEC
HT = T // 2
PAST = 256
TT = 5
FF = 2816
JF = FF // P
EPS = 1e-6
MH = 4
AH = 8
NOPE = 64
ROPE = 32
QK = NOPE + ROPE
AV = 64
QL = 384
KQ = QL // P
KVL = 256
KC = KVL // P
TK = T + PAST
MW = MH * P
A_SCALE = QK ** -0.5
MASKED = -3.0e38
NRAW = 4
NW = 2
DOWN_PARTS = (6, 6, 5, 5)
VP = 130
VAW = AH * AV + 32

F32 = mybir.dt.float32
F32R = mybir.dt.float32r
ACT = mybir.ActivationFunctionType
ALU = mybir.AluOpType
AX = mybir.AxisListType.X

GAINS = (("ff1_pre_g", KD), ("ff1_post_g", KD), ("mix_pre_g", KD), ("mix_post_g", KD), ("ff2_pre_g", KD),
         ("ff2_post_g", KD), ("q_a_g", KQ), ("kv_a_g", KC), ("m_head_g", MH))
GROW = {}
_n = 0
for _name, _k in GAINS:
    GROW[_name] = _n
    _n += _k
NG = _n

NB_GU = 2 * JF
NB_DOWN = KD * len(DOWN_PARTS)
NB_FF = NB_GU + NB_DOWN
MIX0 = NB_FF
B_AQ = MIX0
B_CKV = B_AQ + KQ
B_SMALL = B_CKV + KC
B_QK = B_SMALL + 1
B_UKV = B_QK + 2 * MH
B_UQ = B_UKV + 2
B_VO = B_UQ + 3
B_OUT = B_VO + 2 * MH
FF2_0 = B_OUT + KD
NB = FF2_0 + NB_FF
LOADS = [1] * NB
LOADS[B_SMALL] = 3
LOADS[B_UKV] = LOADS[B_UKV + 1] = KC
for _b in range(3):
    LOADS[B_UQ + _b] = KQ


def arrived(b):
    return 16 * sum(LOADS[c] for c in range(b % NRAW, b + 1, NRAW))


def build(nc, a, rope_table, outs):
    (y_prompt, y_sample, p_kv, p_kr, p_C, p_n, p_m, s_kv, s_kr, s_C, s_n, s_m) = outs
    ctx = ExitStack()
    with ctx:
        def sem(name):
            return ctx.enter_context(nc.semaphore(name))

        top = [(nc.sbuf_base + 31) // 32 * 32]

        def place(name, shape, dt=F32, offset=None):
            n = 4
            for s in shape[1:]:
                n *= s
            if offset is None:
                offset = top[0]
                top[0] += (n + 31) // 32 * 32
            return nc.alloc_sbuf_tensor_at(name, shape, dt, offset=offset)

        ROW = T * 4
        X = place("X", [P, KD, T])
        h_at = top[0]
        H_HI = place("H_HI", [P, KD, T], F32R)
        H_LO = place("H_LO", [P, KD, T], F32R)
        u_at = top[0]
        U_HI = place("U_HI", [P, JF, T], F32R)
        U_LO = place("U_LO", [P, JF, T], F32R)
        RAW = place("RAW", [P, NRAW, 8, P])
        W_HI = place("W_HI", [P, NW, 8, P], F32R)
        W_LO = place("W_LO", [P, NW, 8, P], F32R)
        RB = place("RB", [P, T])
        PAIR = place("PAIR", [P, 2, T])
        TF = place("TF", [P, 2, T])
        acc_at = top[0]
        ACC = place("ACC", [P, T])
        IDENT = place("IDENT", [P, P])
        ONES = place("ONES", [P, P])
        PERM = place("PERM", [P, P])
        trig_at = top[0]
        TRIG = place("TRIG", [P, 2, T])
        GCOLS = place("GCOLS", [P, NG])
        SEL = place("SEL", [MH, MH, P])
        GC = place("GC", [P, TT, MH])
        EMC = place("EMC", [P, TT, MH])
        BIAS = place("BIAS", [MH, 4])
        MEND = place("MEND", [MH, 2])
        M0B = place("M0B", [P, MH])
        WE = place("WE", [P, MH, TT])
        S5 = place("S5", [P, 8, TT])
        EPSC = place("EPSC", [P, 1])
        WARM = place("WARM", [P, 1])
        ROOT = place("ROOT", [P, TT])
        INV = place("INV", [P, TT])
        assert top[0] <= nc.sbuf_usable_end, (top[0], nc.sbuf_usable_end)
        XIN = place("XIN", [P, TT, D], offset=u_at)
        GROWS = place("GROWS", [NG, P], offset=u_at + TT * D * 4)
        Y = place("Y", [P, KD, T], offset=h_at)
        PJ1 = place("PJ1", [P, 2 * MH, T], offset=u_at)
        PJ2 = place("PJ2", [P, 2 * MH, T], offset=u_at + 8 * ROW)
        CQ_HI = place("CQ_HI", [P, KQ, T], F32R, offset=u_at + 8 * ROW)
        CQ_LO = place("CQ_LO", [P, KQ, T], F32R, offset=u_at + 11 * ROW)
        qh_at = u_at + 16 * ROW
        QH = place("QH", [QK, AH, T], offset=qh_at)
        C_HI = place("C_HI", [P, KC, TK], F32R, offset=qh_at)
        C_LO = place("C_LO", [P, KC, TK], F32R, offset=qh_at + KC * TK * 4)
        kh_at = u_at + 24 * ROW
        KH = place("KH", [QK, AH, TK], offset=kh_at)
        CRAW = place("CRAW", [P, KC, TK], offset=kh_at)
        AQRAW = place("AQRAW", [P, KQ, T], offset=kh_at + KC * TK * 4)
        CIN = place("CIN", [P, 2, KVL], offset=kh_at + KC * TK * 4 + 3 * ROW)
        KIN = place("KIN", [P, 2, ROPE], offset=kh_at + KC * TK * 4 + 3 * ROW + 2048)
        CSTAGE = place("CSTAGE", [P, TT, KVL], offset=kh_at + KC * TK * 4 + 3 * ROW + 2304)
        ARS = place("ARS", [ROPE, T], offset=kh_at + KC * TK * 4 + 3 * ROW + 2304 + 5120)
        ONES4 = place("ONES4", [MH, T], offset=kh_at + KC * TK * 4 + 4 * ROW + 2304 + 5120)
        assert KC * TK * 4 + 5 * ROW + 2304 + 5120 <= AH * TK * 4
        va_at = kh_at + AH * TK * 4
        VA = place("VA", [P, 7, VAW], offset=va_at)
        IG, LF, BC, GR, MX, EM = (place(n, [MH, T], offset=va_at + i * ROW) for i, n in
                                  enumerate(("IG", "LF", "BC", "GR", "MX", "EM")))
        assert 6 * ROW <= 7 * VAW * 4
        rest_at = va_at + 7 * VAW * 4
        KR = place("KR", [ROPE, TK], offset=rest_at)
        assert rest_at + TK * 4 <= u_at + 2 * JF * ROW
        NM = place("NM", [MH, T], offset=acc_at)
        C0T = place("C0T", [P, MH, VP], offset=rest_at)
        N0 = place("N0", [1, MH, P], offset=rest_at + MH * VP * 4)
        assert rest_at + MH * VP * 4 + 2048 <= u_at + 2 * JF * ROW
        at = [h_at]

        def local(name, shape, dt=F32):
            t = place(name, shape, dt, offset=at[0])
            n = 4
            for s in shape[1:]:
                n *= s
            at[0] += (n + 31) // 32 * 32
            return t

        KT = local("KT", [P, TT, MH, P])
        VT = local("VT", [P, TT, MH, VP])
        OS = local("OS", [P, TT, VP])
        DW = local("DW", [P, 1344])
        VW = local("VW", [P, TT, P])
        HN = local("HN", [P, TT, P])
        C0 = local("C0", [P, MH, P])
        N0R = local("N0R", [MH, P])
        assert at[0] <= h_at + 16 * ROW
        at[0] = h_at
        PR = local("PR", [P, 2, 1600])
        PT = local("PT", [P, 2, 1472])
        AT = local("AT", [P, TT, P])
        assert at[0] <= h_at + 16 * ROW
        MA_HI = place("MA_HI", [P, MH, T], F32R, offset=u_at + 8 * ROW)
        MA_LO = place("MA_LO", [P, MH, T], F32R, offset=u_at + 4 * ROW)
        MB_HI = place("MB_HI", [P, MH, T], F32R, offset=u_at)
        MB_LO = place("MB_LO", [P, MH, T], F32R, offset=u_at + 12 * ROW)
        CN = place("CN", [P, 2, 2, P], offset=trig_at)
        NN = place("NN", [1, 2, P], offset=trig_at + 2048)
        KSTAGE = place("KSTAGE", [P, TT, ROPE], offset=trig_at + 3072)

        PS = ctx.enter_context(nc.psum_tensor("PS", [P, 8, 512], F32))
        PSF = PS[:].rearrange("p b n -> p (b n)")

        def pair(b, rows=P, n=HT):
            return PS[0:rows, b:b + 2, 0:n]

        def halves(ap, n=HT):
            return ap.rearrange("p (a n) -> p a n", n=n)

        raw_in = [sem(f"raw_in{i}") for i in range(NRAW)]
        w_hi, w_lo, w_used = sem("w_hi"), sem("w_lo"), sem("w_used")
        x_in, g_in, trig_in, bias_in, cache_in, state_in = (sem(n) for n in (
            "x_in", "g_in", "trig_in", "bias_in", "cache_in", "state_in"))
        consts, consts0 = sem("consts"), sem("consts0")
        g_T, g_half = sem("g_T"), sem("g_half")
        g_first_in = sem("g_first_in")
        x_in_part = [sem(f"x_in_part{q}") for q in range(4)]
        x_T, x_cols = sem("x_T"), sem("x_cols")
        out_sem = sem("out_sem")
        dve_step, act_step, pool_step = sem("dve_step"), sem("act_step"), sem("pool_step")
        steps = {"dve": 0, "act": 0, "pool": 0}

        def settle(eng, key, s, ins):
            steps[key] += 1
            ins.then_inc(s, 1)
            eng.wait_ge(s, steps[key])

        def names(prefix, *what):
            return {w: sem(f"{prefix}_{w}") for w in what}

        class Since:

            def __init__(self, sem_, base):
                self.sem, self.base = sem_, base

        def stages(prefix, count, **per_stage):
            sems = {w: sem(f"{prefix}_{w}") for w in per_stage}
            return [{w: Since(sems[w], i * total) for w, total in per_stage.items()}
                    for i in range(count)]

        post = stages("post", 3, y_sq=KD, y_copy=KD, acc=KD - 1, sum=1, root=1, inv=1, spread=1, t=KD, x=KD, x_dve=0)
        pre = stages("pre", 3, hi=KD, lo=KD, sq=KD, summed=KD - 1, sum=1, root=1, inv=1, spread=1)
        ff = stages("ff", 2, gate=JF, up=JF, silu=JF, mul=JF, u_hi=JF, u_lo=JF)

        def raw_slot(b):
            return RAW[:, b % NRAW]

        def load_wait(sp, b):
            if b >= NRAW:
                sp.wait_ge(w_lo, b - NRAW + 1)

        def load_ffn(sp, b0, wg, wu, wd, after_first=None):
            gv = wg.rearrange("(k p) f -> p k f", p=P)
            uv = wu.rearrange("(k p) f -> p k f", p=P)
            dv = wd.rearrange("(k p) f -> p k f", p=P)

            def tiles(i, first=False):
                for q in range(4):
                    b = b0 + q
                    if not (first and b < NRAW):
                        sp.wait_ge(w_lo, b0 + i * 4 + q - NRAW + 1)
                    if first and q in (1, 2) and after_first is not None:
                        after_first(q)
                    src = (gv, uv)[q % 2]
                    sp.dma_start(raw_slot(b), src[:, :, bass.ds(i * (2 * P) + (q // 2) * P, P)]).then_inc(
                        raw_in[b % NRAW], 16)

            tiles(0, first=True)
            with sp.Fori(1, JF // 2) as i:
                tiles(i)
            b1 = b0 + NB_GU
            with sp.Fori(0, KD) as m:
                k0 = 0
                for q, n in enumerate(DOWN_PARTS):
                    sp.wait_ge(w_lo, m * 4 + (b1 + q - NRAW + 1))
                    sp.dma_start(raw_slot(b1 + q)[:, 0:n, :], dv[:, k0:k0 + n, bass.ds(m * P, P)]).then_inc(
                        raw_in[(b1 + q) % NRAW], 16)
                    k0 += n

        def split_hi(act, b, n=8, count=None, target=None):
            act.wait_ge(raw_in[b % NRAW], arrived(b) if target is None else target)
            if count is None:
                if b >= NW:
                    act.wait_ge(w_used, b - NW + 1)
            else:
                act.wait_ge(w_used, count - NW + 1)
            nc.scalar.activation(W_HI[:, b % NW, 0:n, :], raw_slot(b)[:, 0:n, :], ACT.Copy).then_inc(w_hi, 1)

        def split_lo(dve, b, n=8, count=None):
            dve.wait_ge(w_hi, (b if count is None else count) + 1)
            nc.vector.tensor_tensor(W_LO[:, b % NW, 0:n, :], raw_slot(b)[:, 0:n, :],
                                    W_HI[:, b % NW, 0:n, :].bitcast(F32), ALU.subtract).then_inc(w_lo, 1)

        def weights_ready(pe, count):
            pe.wait_ge(w_hi, count + 1)
            pe.wait_ge(w_lo, count + 1)

        def passes(w_hi_t, w_lo_t, a_hi, a_lo):
            return ((w_hi_t, a_hi), (w_hi_t, a_lo), (w_lo_t, a_hi))

        def product(b, t, hi, lo, bank, start, stop, m=P, rows=P, n=HT):
            wh, wl = W_HI[0:rows, b % NW, t, 0:m], W_LO[0:rows, b % NW, t, 0:m]
            last = None
            for i, (w, x) in enumerate(passes(wh, wl, hi, lo)):
                for s in range(2):
                    last = nc.tensor.matmul(PS[0:m, bank + s, 0:n], w, x[:, s * n:(s + 1) * n],
                                            start=start and i == 0, stop=stop and i == 2)
            return last

        NS = 96
        FRAMES = [(i * P, P) for i in range(4)] + [(SEQ, DEC)]

        def frame_sums(src, bank, start, stop):
            for t in (0, 4, 1, 2, 3):
                c, n = FRAMES[t]
                last = nc.tensor.matmul(PS[0:n, bank, t * NS:(t + 1) * NS], src[:, c:c + n], ONES[:, 0:NS],
                                        start=start and t == 0, stop=stop and t == 3)
            return last

        def frame_roots(bank, width):
            cols = PS[:, bank, 0:4 * NS].rearrange("p (t c) -> p t c", c=NS)[:, :, 0]
            nc.scalar.activation(ROOT[:, 0:4], cols, ACT.Sqrt, bias=EPSC[:], scale=1.0 / width)
            return nc.scalar.activation(ROOT[0:DEC, 4:5], PS[0:DEC, bank, 4 * NS:4 * NS + 1], ACT.Sqrt,
                                        bias=EPSC[0:DEC], scale=1.0 / width)

        def spread(bank):
            for t, (c, n) in enumerate(FRAMES):
                last = nc.tensor.matmul(PSF[:, bank * 512 + c:bank * 512 + c + n], INV[0:n, t:t + 1].to_broadcast([n, P]),
                                        IDENT[0:n, 0:n], start=True, stop=True)
            return last

        def spread_at(bank):
            return PSF[:, bank * 512:bank * 512 + T]

        POST_SUM, POST_SPREAD, PRE_SUM, PRE_SPREAD = 0, 2, 4, 6

        def post_pe(pe, e):
            pe.wait_ge(e["acc"].sem, KD - 1 + e["acc"].base)
            frame_sums(ACC[:], POST_SUM, True, False)
            pe.wait_ge(e["y_sq"].sem, KD + e["y_sq"].base)
            frame_sums(PAIR[:, 1], POST_SUM, False, True).then_inc(e["sum"].sem, 1)
            pe.wait_ge(e["inv"].sem, 1 + e["inv"].base)
            spread(POST_SPREAD).then_inc(e["spread"].sem, 1)

        def post_act(act, e):
            act.wait_ge(e["sum"].sem, 1 + e["sum"].base)
            frame_roots(POST_SUM, D).then_inc(e["root"].sem, 1)

        def post_dve(dve, e, p=None):
            dve.wait_ge(e["root"].sem, 1 + e["root"].base)
            nc.vector.reciprocal(INV[:], ROOT[:]).then_inc(e["inv"].sem, 1)
            dve.wait_ge(e["spread"].sem, 1 + e["spread"].base)
            for k in range(KD):
                nc.vector.tensor_tensor(Y[:, k], Y[:, k], spread_at(POST_SPREAD), ALU.mult).then_inc(e["t"].sem, 1)
                if p is None and k % 2 == 0:
                    dve.wait_ge(e["t"].sem, k + 1 + e["t"].base)
                    nc.vector.tensor_tensor(X[:, k], X[:, k], Y[:, k], ALU.add).then_inc(e["x_dve"].sem, 1)
                if p is not None and k >= 2:
                    low_dve(dve, p, k - 2)
            if p is not None:
                low_dve(dve, p, KD - 2)
                low_dve(dve, p, KD - 1)

        def post_pool(pool, e):
            for k in range(1, KD, 2) if e is post[2] else range(KD):
                pool.wait_ge(e["t"].sem, k + 1 + e["t"].base)
                nc.gpsimd.tensor_tensor(X[:, k], X[:, k], Y[:, k], ALU.add).then_inc(e["x"].sem, 1)

        def x_wait(eng, e, k):
            if e is None:
                eng.wait_ge(x_cols, k + 2)
            elif e is post[2]:
                done = e["x"] if k % 2 else e["x_dve"]
                eng.wait_ge(done.sem, k // 2 + 1 + done.base)
            else:
                eng.wait_ge(e["x"].sem, k + 1 + e["x"].base)

        SQ = [PAIR[:, 0], PAIR[:, 1], TF[:, 0], TF[:, 1], ACC[:], RB[:]]

        def pre_act(act, e, before, gain, split=None):
            for k in range(KD):
                x_wait(act, before, k)
                g = GROW[gain] + k
                nc.scalar.activation(H_HI[:, k], X[:, k], ACT.Copy, scale=GCOLS[:, g:g + 1]).then_inc(e["hi"].sem, 1)
                if split is not None and k in (1, KD - 1):
                    split_hi(act, k // 4)
                if k >= len(SQ):
                    act.wait_ge(e["summed"].sem, k - len(SQ) + 1 + e["summed"].base)
                nc.scalar.activation(SQ[k % len(SQ)], X[:, k], ACT.Square).then_inc(e["sq"].sem, 1)

        def pre_root_act(act, e):
            act.wait_ge(e["sum"].sem, 1 + e["sum"].base)
            frame_roots(PRE_SUM, D).then_inc(e["root"].sem, 1)

        def pre_sum_pe(pe, e, k):
            pe.wait_ge(e["sq"].sem, k + 1 + e["sq"].base)
            done = e["sum"] if k == KD - 1 else e["summed"]
            frame_sums(SQ[k % len(SQ)], PRE_SUM, k == 0, k == KD - 1).then_inc(done.sem, 1)

        def pre_spread_pe(pe, e):
            pe.wait_ge(e["inv"].sem, 1 + e["inv"].base)
            spread(PRE_SPREAD).then_inc(e["spread"].sem, 1)

        PRE_GAINS = ("ff1_pre_g", "mix_pre_g", "ff2_pre_g")

        def low_dve(dve, e, k):
            dve.wait_ge(e["hi"].sem, k + 1 + e["hi"].base)
            g = GROW[PRE_GAINS[pre.index(e)]] + k
            nc.vector.scalar_tensor_tensor(out=H_LO[:, k], in0=X[:, k], scalar=GCOLS[:, g:g + 1],
                                           in1=H_HI[:, k].bitcast(F32), op0=ALU.mult, op1=ALU.subtract).then_inc(e["lo"].sem, 1)

        def pre_dve(dve, e):
            dve.wait_ge(e["root"].sem, 1 + e["root"].base)
            nc.vector.reciprocal(INV[:], ROOT[:]).then_inc(e["inv"].sem, 1)

        def pre_factor_dve(dve, e):
            dve.wait_ge(e["spread"].sem, 1 + e["spread"].base)
            settle(dve, "dve", dve_step, nc.vector.tensor_copy(RB[:], spread_at(PRE_SPREAD)))

        def h_wait(pe, e, k):
            pe.wait_ge(e["hi"].sem, k + 1 + e["hi"].base)
            pe.wait_ge(e["lo"].sem, k + 1 + e["lo"].base)

        def ffn_pe(pe, f, e, p, b0):
            def gate_up(i, first=False):
                for jj in range(2):
                    j = i * 2 + jj
                    for q in range(2):
                        b = b0 + 2 * jj + q
                        weights_ready(pe, i * 4 + b)
                        if not (first and jj == 0):
                            done = f["up"] if q else f["gate"]
                            pe.wait_ge(done.sem, j + done.base)
                        for k in range(KD):
                            if first and jj == 0 and q == 0:
                                h_wait(pe, e, k)
                            if first and jj == 0 and q == 1 and k == KD // 2:
                                pre_spread_pe(pe, e)
                            last = product(b, k, H_HI[:, k], H_LO[:, k], 2 * q, k == 0, k == KD - 1)
                            if first and jj == 0 and q == 0 and k:
                                pre_sum_pe(pe, e, k - 1)
                        last.then_inc(w_used, 1)
                        if first and jj == 0 and q == 0:
                            pre_sum_pe(pe, e, KD - 1)
                            if b0 == 0:
                                other_gains_pe(pe)

            gate_up(0, first=True)
            with pe.Fori(1, JF // 2) as i:
                gate_up(i)
            b1 = b0 + NB_GU

            def down(i, first=False):
                for mm in range(2):
                    m = i * 2 + mm
                    if not first:
                        pe.wait_ge(p["y_copy"].sem, m - 1 + p["y_copy"].base)
                    k = 0
                    for q, n in enumerate(DOWN_PARTS):
                        b = b1 + q
                        weights_ready(pe, i * 8 + (b1 + 4 * mm + q))
                        if first and mm == 0:
                            pe.wait_ge(f["u_lo"].sem, k + n + f["u_lo"].base)
                        for t in range(n):
                            last = product(b, t, U_HI[:, k], U_LO[:, k], 4 + 2 * mm, k == 0, k == JF - 1)
                            k += 1
                        last.then_inc(w_used, 1)

            down(0, first=True)
            with pe.Fori(1, KD // 2) as i:
                down(i)

        def ffn_act(act, f, p, b0, post_gain):
            b1 = b0 + NB_GU

            def gate_up(i, last=False):
                for jj in range(2):
                    j = i * 2 + jj
                    for q in range(2):
                        b = b0 + 2 * jj + q + 2
                        if q:
                            act.wait_ge(f["gate"].sem, j + 1 + f["gate"].base)
                            nc.scalar.activation(PAIR[:, jj], PAIR[:, jj], ACT.Silu).then_inc(f["silu"].sem, 1)
                        if last and jj == 1:
                            split_hi(act, b1 + q, DOWN_PARTS[q])
                        else:
                            split_hi(act, b, 8, i * 4 + b, i * 16 + arrived(b))
                    act.wait_ge(f["mul"].sem, j + 1 + f["mul"].base)
                    nc.scalar.activation(U_HI[:, bass.ds(j, 1), :], TF[:, jj:jj + 1, :], ACT.Copy).then_inc(f["u_hi"].sem, 1)

            nc.scalar.activation(WARM[:], EPSC[:], ACT.Silu)
            gate_up(0)
            with act.Fori(1, JF // 2 - 1) as i:
                gate_up(i)
            gate_up(JF // 2 - 1, last=True)
            nc.scalar.activation(WARM[:], EPSC[:], ACT.Sqrt)

            def down(i, first=False, last=False):
                for mm in range(2):
                    m = i * 2 + mm
                    for q in range(4):
                        nq = q + 2
                        over = nq // 4
                        if not (last and mm == 1 and over):
                            b = b1 + nq % 4
                            split_hi(act, b, DOWN_PARTS[nq % 4], i * 8 + (b1 + 4 * mm + nq),
                                     i * 32 + (arrived(b) + 16 * (mm + over)))
                        elif b0 == 0:
                            split_hi(act, MIX0 + nq % 4)
                    act.wait_ge(w_used, i * 8 + (b1 + 4 * mm + 4))
                    y_out(act, p, m, mm, 4 + 2 * mm, post_gain, first)

            down(0, first=True)
            with act.Fori(1, KD // 2 - 1) as i:
                down(i)
            down(KD // 2 - 1, last=True)

        def y_out(act, p, m, slot, bank, gain, first):
            if not first:
                act.wait_ge(p["acc"].sem, m - 1 + p["acc"].base)
            nc.scalar.activation(halves(PAIR[:, slot]), pair(bank), ACT.Square).then_inc(p["y_sq"].sem, 1)
            nc.scalar.activation(halves(Y[:, bass.ds(m, 1), :].rearrange("p a t -> p (a t)")), pair(bank), ACT.Copy,
                                 scale=GCOLS[:, bass.ds(m + GROW[gain], 1)]).then_inc(p["y_copy"].sem, 1)

        def ffn_dve(dve, f, e, b0):
            b1 = b0 + NB_GU

            def gate_up(i, last=False):
                for jj in range(2):
                    j = i * 2 + jj
                    b = b0 + 2 * jj + 2
                    tail = last and jj == 1
                    dve.wait_ge(w_used, i * 4 + (b0 + 2 * jj + 1))
                    if not (isinstance(i, int) and i == 0):
                        dve.wait_ge(f["mul"].sem, j - 1 + f["mul"].base)
                    elif jj == 0:
                        pre_factor_dve(dve, e)
                    nc.vector.tensor_tensor(halves(PAIR[:, jj]), pair(0), halves(RB[:]), ALU.mult).then_inc(f["gate"].sem, 1)
                    if tail:
                        split_lo(dve, b1, DOWN_PARTS[0])
                    else:
                        split_lo(dve, b, 8, i * 4 + b)
                    dve.wait_ge(w_used, i * 4 + (b0 + 2 * jj + 2))
                    if not (isinstance(i, int) and i == 0):
                        dve.wait_ge(f["u_lo"].sem, j - 1 + f["u_lo"].base)
                    nc.vector.tensor_tensor(halves(TF[:, jj]), pair(2), halves(RB[:]), ALU.mult).then_inc(f["up"].sem, 1)
                    dve.wait_ge(f["silu"].sem, j + 1 + f["silu"].base)
                    dve.wait_ge(f["up"].sem, j + 1 + f["up"].base)
                    nc.vector.tensor_tensor(TF[:, jj], TF[:, jj], PAIR[:, jj], ALU.mult).then_inc(f["mul"].sem, 1)
                    if tail:
                        split_lo(dve, b1 + 1, DOWN_PARTS[1])
                    else:
                        split_lo(dve, b + 1, 8, i * 4 + (b + 1))
                    dve.wait_ge(f["u_hi"].sem, j + 1 + f["u_hi"].base)
                    nc.vector.tensor_tensor(U_LO[:, bass.ds(j, 1), :], TF[:, jj:jj + 1, :],
                                            U_HI[:, bass.ds(j, 1), :].bitcast(F32), ALU.subtract).then_inc(f["u_lo"].sem, 1)

            gate_up(0)
            with dve.Fori(1, JF // 2 - 1) as i:
                gate_up(i)
            gate_up(JF // 2 - 1, last=True)

            def down(i, last=False):
                for mm in range(2):
                    for q in range(4):
                        nq = q + 2
                        if not (last and mm == 1 and nq >= 4):
                            split_lo(dve, b1 + nq % 4, DOWN_PARTS[nq % 4], i * 8 + (b1 + 4 * mm + nq))
                        elif b0 == 0:
                            split_lo(dve, MIX0 + nq % 4)

            with dve.Fori(0, KD // 2 - 1) as i:
                down(i)
            down(KD // 2 - 1, last=True)

        def acc_pool(pool, p):
            for m in range(KD - 1):
                pool.wait_ge(p["y_sq"].sem, m + 1 + p["y_sq"].base)
                if m == 0:
                    nc.gpsimd.tensor_copy(ACC[:], PAIR[:, 0]).then_inc(p["acc"].sem, 1)
                else:
                    pool.wait_ge(p["acc"].sem, m + p["acc"].base)
                    nc.gpsimd.tensor_tensor(ACC[:], ACC[:], PAIR[:, m % 2], ALU.add).then_inc(p["acc"].sem, 1)


        def start_pool(pool):
            nc.gpsimd.memset(IDENT[:], 0.0).then_inc(consts0, 1)
            pool.wait_ge(consts0, 1)
            nc.gpsimd.affine_select(out=IDENT[:], in_=IDENT[:], compare_op=ALU.not_equal, fill=1.0, base=0,
                                    pattern=[[-1, P]], channel_multiplier=1).then_inc(consts, 1)
            nc.gpsimd.memset(ONES[:], 1.0)
            nc.gpsimd.memset(EPSC[:], EPS)
            nc.gpsimd.memset(ROOT[:], 1.0)
            nc.gpsimd.memset(PERM[:], 0.0).then_inc(consts0, 1)
            nc.gpsimd.memset(SEL[:], 0.0).then_inc(consts0, 1)
            nc.gpsimd.memset(S5[:], 1.0)
            nc.gpsimd.memset(GC[:], 0.0)
            nc.gpsimd.memset(EMC[:], 1.0)
            pool.wait_ge(consts0, 3)
            nc.gpsimd.affine_select(out=PERM[:].rearrange("p (q a c) -> p q a c", a=2, c=ROPE // 2),
                                    in_=PERM[:].rearrange("p (q a c) -> p q a c", a=2, c=ROPE // 2),
                                    compare_op=ALU.not_equal, fill=1.0, base=ROPE // 2,
                                    pattern=[[ROPE, P // ROPE], [-(ROPE // 2), 2], [1, ROPE // 2]],
                                    channel_multiplier=-1).then_inc(consts, 1)
            nc.gpsimd.affine_select(out=SEL[:], in_=SEL[:], compare_op=ALU.not_equal, fill=1.0, base=0,
                                    pattern=[[1, MH], [0, P]], channel_multiplier=-1).then_inc(consts, 1)
            load_gains(pool, GAINS[1:], g_in)
            pool.dma_start(TRIG[:], rope_table).then_inc(trig_in, 16)
            pool.dma_start(BIAS[:, 0:1], a["b_igate"].rearrange("l h -> h l")).then_inc(bias_in, 16)
            pool.dma_start(BIAS[:, 1:2], a["b_fgate"].rearrange("l h -> h l")).then_inc(bias_in, 16)
            pool.dma_start(BIAS[:, 2:3], a["state_m"].rearrange("l b h -> h (l b)")).then_inc(bias_in, 16)
            pool.dma_start(M0B[:], a["state_m"][0].to_broadcast([P, MH])).then_inc(bias_in, 16)

        X_PARTS = 4

        def load_x(sp, q):
            c = slice(q * D // X_PARTS, (q + 1) * D // X_PARTS)
            sp.dma_start(XIN[:, 0:4, c], a["x_prompt"][0].rearrange("(t p) d -> p t d", p=P)[:, :, c]).then_inc(
                x_in_part[q], 16)

        def start_sp(sp):
            load_x(sp, 0)
            sp.dma_start(XIN[0:DEC, TT - 1, :], a["x_sample"][0]).then_inc(x_in, 16)
            load_x(sp, 1)

        def load_gains(eng, which, done):
            for name, k in which:
                g = a[name][0]
                g = g if name == "m_head_g" else g.rearrange("(k p) -> k p", p=P)
                eng.dma_start(GROWS[GROW[name]:GROW[name] + k, :], g).then_inc(done, 16)

        X_BANKS = (3, 5, 7, 2)

        def start_pe(pe):
            pe.wait_ge(consts, 1)
            pe.wait_ge(g_first_in, 16)
            nc.tensor.transpose(PS[:, 0, 0:KD], GROWS[0:KD, :], IDENT[0:KD, 0:KD]).then_inc(g_T, 1)
            pe.wait_ge(x_in, 16)
            for k in range(KD):
                last = nc.tensor.transpose(PS[:, 6, k * DEC:(k + 1) * DEC], XIN[0:DEC, TT - 1, k * P:(k + 1) * P],
                                           IDENT[0:DEC, 0:DEC])
            last.then_inc(x_T, 1)
            for k in range(KD):
                if k % 2 == 0:
                    pe.wait_ge(x_in_part[k // 2], 16)
                if k >= 4:
                    pe.wait_ge(x_cols, k - 2)
                for t in range(4):
                    last = nc.tensor.transpose(PS[:, X_BANKS[k % 4], t * P:(t + 1) * P],
                                               XIN[:, t, k * P:(k + 1) * P], IDENT[:])
                last.then_inc(x_T, 1)
            pe.wait_ge(consts, 3)

        def other_gains_pe(pe):
            pe.wait_ge(g_in, 16 * (len(GAINS) - 1))
            nc.tensor.transpose(PS[:, X_BANKS[1], 0:NG], GROWS[:], IDENT[0:NG, 0:NG]).then_inc(g_T, 1)

        def start_dve(dve):
            dve.wait_ge(g_T, 1)
            nc.vector.tensor_copy(GCOLS[:, 0:KD], PS[:, 0, 0:KD])
            dve.wait_ge(x_T, 1)
            nc.vector.tensor_copy(X[:, :, SEQ:T], PS[:, 6, :].rearrange("p (k t) -> p k t", k=KD)).then_inc(x_cols, 1)
            for k in range(KD):
                dve.wait_ge(x_T, k + 2)
                nc.vector.tensor_copy(X[:, k, 0:SEQ], PS[:, X_BANKS[k % 4], :]).then_inc(x_cols, 1)
                if k:
                    low_dve(dve, pre[0], k - 1)
                if k == 3:
                    split_lo(dve, 0)
            split_lo(dve, 1)
            low_dve(dve, pre[0], KD - 1)

        def other_gains_dve(dve):
            dve.wait_ge(g_T, 2)
            settle(dve, "dve", dve_step, nc.vector.tensor_copy(GCOLS[:, KD:NG], PS[:, X_BANKS[1], KD:NG]))
            for name in ("ff1_post_g", "ff2_post_g"):
                g = GCOLS[:, GROW[name]:GROW[name] + KD]
                nc.vector.tensor_scalar(g, g, 0.5, None, ALU.mult).then_inc(g_half, 1)

        OUT_BANKS = (0, 4, 6)

        def finish_pe(pe):
            for k in range(KD):
                x_wait(pe, post[2], k)
                b = OUT_BANKS[k % 3]
                if k >= 3:
                    pe.wait_ge(o["copied"], k - 2)
                for t in range(4):
                    nc.tensor.transpose(PS[:, b, t * P:(t + 1) * P], X[:, k, t * P:(t + 1) * P], IDENT[:])
                nc.tensor.transpose(PS[0:DEC, b + 1, 0:P], X[:, k, SEQ:T], IDENT[:]).then_inc(o["T"], 1)

        def finish_act(act):
            for k in range(KD):
                act.wait_ge(o["T"], k + 1)
                b = OUT_BANKS[k % 3]
                nc.scalar.activation(XIN[:, 0:4, k * P:(k + 1) * P],
                                     PS[:, b, :].rearrange("p (t f) -> p t f", t=4), ACT.Copy)
                nc.scalar.activation(XIN[0:DEC, 4, k * P:(k + 1) * P], PS[0:DEC, b + 1, 0:P],
                                     ACT.Copy).then_inc(o["copied"], 1)

        def finish_sp(sp):
            for q in range(KD // 2):
                sp.wait_ge(o["copied"], 2 * (q + 1))
                c = slice(2 * q * P, 2 * (q + 1) * P)
                sp.dma_start(y_prompt[0].rearrange("(t p) d -> p t d", p=P)[:, :, c], XIN[:, 0:4, c]).then_inc(out_sem, 16)
                sp.dma_start(y_sample[0][:, c], XIN[0:DEC, 4, c]).then_inc(out_sem, 16)
            sp.wait_ge(out_sem, 16 * KD)
            sp.wait_ge(st["stored"], 64)
            sp.wait_ge(m1["c_stored"], 32)
            sp.wait_ge(m2["state_out"], 64 * MH)

        o = names("out", "T", "copied")
        m1 = names("m1", "cache_T", "cache_hi", "cache_lo", "kr_c", "proj", "sq", "aq_sum", "aq_root", "aq_inv", "aq_spread",
                   "cq", "c_sum", "c_root", "c_inv", "c_spread", "c", "cq_lo", "c_lo", "lf1", "soft", "lf", "mm", "em",
                   "perm", "c_T", "c_staged", "c_stored", "kr", "kn_T", "kn_a", "kn_d", "gate_T", "gate_c", "v_T", "v_a",
                   "v_d", "q_T", "q_a", "q_d", "rs", "perm_q", "qr", "rope_in", "kr_T", "kr_staged")
        st = names("st", "stored")

        def load_mix(sp):
            w_in, w_uq, w_ukv, w_out = (a[n][0] for n in ("w_in", "w_uq", "w_ukv", "w_out"))
            wv = w_in.rearrange("(k p) f -> p k f", p=P)
            c_gate, c_aq = 4 * MW, 4 * MW + 2 * MH
            c_ckv = c_aq + QL
            c_ar = c_ckv + KVL

            def one(b, *parts):
                load_wait(sp, b)
                for dst, src in parts:
                    sp.dma_start(dst, src).then_inc(raw_in[b % NRAW], 16)

            for i in range(KQ):
                one(B_AQ + i, (raw_slot(B_AQ + i), wv[:, :, c_aq + i * P:c_aq + (i + 1) * P]))
            for i in range(KC):
                one(B_CKV + i, (raw_slot(B_CKV + i), wv[:, :, c_ckv + i * P:c_ckv + (i + 1) * P]))
            one(B_SMALL, *((raw_slot(B_SMALL)[:, :, at_:at_ + n], wv[:, :, lo:lo + n])
                           for at_, lo, n in ((0, c_ar, ROPE), (32, c_gate, MH), (64, c_gate + MH, MH))))

            def heads(b0, c0):
                with sp.Fori(0, 2) as i:
                    for t in range(4):
                        sp.wait_ge(w_lo, i * 4 + (b0 + t - NRAW + 1))
                        sp.dma_start(raw_slot(b0 + t), wv[:, :, bass.ds(i * (4 * P) + (c0 + t * P), P)]).then_inc(
                            raw_in[(b0 + t) % NRAW], 16)

            heads(B_QK, 0)
            kv = w_ukv.rearrange("(k p) (h c) -> p k h c", p=P, c=NOPE + AV)
            uq = w_uq.rearrange("(k p) (h c) -> p k h c", p=P, c=QK)

            def columns_of(b, w, nk, h0, h1, c0, c1):
                dst = raw_slot(b).rearrange("p t c -> p (t c)")
                width = (h1 - h0) * (c1 - c0)
                one(b, *((dst[:, k * width:(k + 1) * width].rearrange("p (h c) -> p h c", c=c1 - c0), w[:, k, h0:h1, c0:c1])
                         for k in range(nk)))

            columns_of(B_UKV, kv, KC, 0, AH, 0, NOPE)
            columns_of(B_UKV + 1, kv, KC, 0, AH, NOPE, NOPE + AV)
            columns_of(B_UQ, uq, KQ, 0, AH, NOPE, QK)
            columns_of(B_UQ + 1, uq, KQ, 0, 4, 0, NOPE)
            columns_of(B_UQ + 2, uq, KQ, 4, AH, 0, NOPE)
            heads(B_VO, 2 * MW)
            wo = w_out.rearrange("(k p) f -> p k f", p=P)
            for n in range(KD):
                if n == NRAW:
                    store_states(sp)
                one(B_OUT + n, (raw_slot(B_OUT + n), wo[:, :, n * P:(n + 1) * P]))

        def store_states(sp):
            for h in range(MH):
                sp.wait_ge(m2["st_c"], h + 1)
                sp.wait_ge(m2["st_v"], h + 1)
                sp.dma_start(p_C[0, 0, h], CN[:, h % 2, 0]).then_inc(m2["state_out"], 16)
                sp.dma_start(s_C[0, 0, h], CN[:, h % 2, 1]).then_inc(m2["state_out"], 16)
                sp.dma_start(p_n[0, 0, h:h + 1, :], NN[:, 0]).then_inc(m2["state_out"], 16)
                sp.dma_start(s_n[0, 0, h:h + 1, :], NN[:, 1]).then_inc(m2["state_out"], 16)

        KEY_TILES = [(i * P, P) for i in range(4)] + [(SEQ, DEC), (T, P), (T + P, P)]

        def mix1_pe(pe):
            pe.wait_ge(cache_in, 32)
            for k in range(KC):
                for t in range(2):
                    nc.tensor.transpose(PS[:, 6, (2 * k + t) * P:(2 * k + t + 1) * P], CIN[:, t, k * P:(k + 1) * P], IDENT[:])
            for t in range(2):
                last = nc.tensor.transpose(PS[0:ROPE, 7, t * P:(t + 1) * P], KIN[:, t, :], IDENT[:])
            last.then_inc(m1["cache_T"], 1)

            def tile(b, bank, m=P, first=False, at_half=None):
                weights_ready(pe, b)
                for k in range(KD):
                    if at_half is not None and k == KD // 2:
                        at_half()
                    if first:
                        h_wait(pe, pre[1], k)
                    last = product(b, k, H_HI[:, k], H_LO[:, k], bank, k == 0, k == KD - 1, m=m)
                    if first and k:
                        pre_sum_pe(pe, pre[1], k - 1)
                return last

            tile(B_AQ, 0, first=True).then_inc(w_used, 1)
            pe.wait_ge(m1["cache_lo"], 1)
            pe.wait_ge(m1["kr_c"], 1)
            pre_sum_pe(pe, pre[1], KD - 1)
            tile(B_AQ + 1, 2, at_half=lambda: pre_spread_pe(pe, pre[1])).then_inc(w_used, 1)
            tile(B_AQ + 2, 4).then_inc(w_used, 1)
            pe.wait_ge(m1["proj"], 1)
            tile(B_CKV, 6).then_inc(w_used, 1)
            tile(B_CKV + 1, 0).then_inc(w_used, 1)
            for i in range(KQ):
                pe.wait_ge(m1["sq"], i + 1)
                last = frame_sums((PAIR[:, 0], PAIR[:, 1], ACC[:])[i], 2, i == 0, i == KQ - 1)
            last.then_inc(m1["aq_sum"], 1)
            pe.wait_ge(m1["proj"], 3)
            tile(B_SMALL, 4, m=64 + MH).then_inc(w_used, 1)
            pe.wait_ge(m1["aq_inv"], 1)
            spread(2).then_inc(m1["aq_spread"], 1)
            for i in range(KC):
                pe.wait_ge(m1["sq"], KQ + i + 1)
                last = frame_sums(TF[:, i], 6, i == 0, i == KC - 1)
            last.then_inc(m1["c_sum"], 1)

            for n in range(2 * MH):
                if n == 1:
                    pe.wait_ge(m1["cq"], KQ)
                pe.wait_ge(m1["proj"], n + 5)
                tile(B_QK + n, 2 * (n % 2)).then_inc(w_used, 1)
                if n == 0:
                    pe.wait_ge(m1["c_inv"], 1)
                    spread(6).then_inc(m1["c_spread"], 1)
                if n == 1:
                    pe.wait_ge(m1["proj"], 6)
                    for s in range(2):
                        last = nc.tensor.matmul(PS[0:ROPE, 4 + s, 0:HT], PERM[0:ROPE, 0:ROPE],
                                                ARS[:, s * HT:(s + 1) * HT], start=True, stop=True)
                    last.then_inc(m1["perm"], 1)
                if n == 4:
                    pe.wait_ge(m1["c"], KC)
                    pe.wait_ge(m1["kr"], 1)
                    for t, (c, rows) in enumerate(FRAMES):
                        bank, off = ((6, 0), (6, 256), (7, 0), (7, 256), (4, 0))[t]
                        for k in range(KC):
                            last = nc.tensor.transpose(PS[0:rows, bank, off + k * P:off + (k + 1) * P],
                                                       CRAW[:, k, c:c + rows], IDENT[:])
                    last.then_inc(m1["c_T"], 1)
            pe.wait_ge(m1["c_lo"], KC)
            pe.wait_ge(m1["cache_lo"], 1)
            weights_ready(pe, B_UKV)
            NK = TK // 2
            for n in range(AH // 2):
                if n < 2:
                    pe.wait_ge(m1["proj"] if n else m1["c_staged"], 14 if n else 1)
                else:
                    pe.wait_ge(m1["kn_a"], n - 1)
                    pe.wait_ge(m1["kn_d"], n - 1)
                for k in range(KC):
                    last = product(B_UKV, k * 4 + n, C_HI[:, k], C_LO[:, k], 4 - 2 * (n % 2), k == 0, k == KC - 1, n=NK)
                last.then_inc(w_used if n == AH // 2 - 1 else m1["kn_T"], 1)
            pe.wait_ge(m1["em"], 1)
            pe.wait_ge(m1["mm"], 1)
            pe.wait_ge(m1["c_staged"], 1)
            for j, src in enumerate((GR, EM)):
                for t, (c, n) in enumerate(FRAMES):
                    last = nc.tensor.transpose(PS[0:n, 7, (j * TT + t) * MH:(j * TT + t + 1) * MH], src[:, c:c + n],
                                               IDENT[0:MH, 0:MH])
            last.then_inc(m1["gate_T"], 1)
            weights_ready(pe, B_UKV + 1)
            s_w = (B_UKV + 1) % NW
            for s, (c, n) in enumerate(KEY_TILES):
                if s == 3:
                    pe.wait_ge(m1["gate_c"], 1)
                if s >= 4:
                    pe.wait_ge(m1["v_d"] if s % 2 else m1["v_a"], s // 2 - 1)
                for k in range(KC):
                    for i, (x, w) in enumerate(passes(C_HI[:, k, c:c + n], C_LO[:, k, c:c + n],
                                                      W_HI[:, s_w, 4 * k:4 * k + 4, :].rearrange("p t c -> p (t c)"),
                                                      W_LO[:, s_w, 4 * k:4 * k + 4, :].rearrange("p t c -> p (t c)"))):
                        last = nc.tensor.matmul(PS[0:n, (0, 1, 6, 7)[s % 4], :], x, w,
                                                start=k == 0 and i == 0, stop=k == KC - 1 and i == 2)
                last.then_inc(w_used if s == 6 else m1["v_T"], 1)
            pe.wait_ge(m1["cq_lo"], KQ)
            weights_ready(pe, B_UQ)
            for r in range(2):
                pe.wait_ge(m1["kn_a"], r + 3)
                pe.wait_ge(m1["kn_d"], r + 3)
                for k in range(KQ):
                    last = product(B_UQ, 2 * k + r, CQ_HI[:, k], CQ_LO[:, k], 4 - 2 * r, k == 0, k == KQ - 1)
                last.then_inc(w_used if r else m1["q_T"], 1)
            for n in range(4):
                b = B_UQ + 1 + n // 2
                weights_ready(pe, b)
                if n < 2:
                    pe.wait_ge(m1["rs"], n + 1)
                else:
                    pe.wait_ge(m1["q_a"], n - 1)
                    pe.wait_ge(m1["q_d"], n - 1)
                for k in range(KQ):
                    last = product(b, 2 * k + n % 2, CQ_HI[:, k], CQ_LO[:, k], 4 - 2 * (n % 2), k == 0, k == KQ - 1)
                last.then_inc(w_used if n % 2 else m1["q_T"], 1)
                if n == 0:
                    pe.wait_ge(m1["v_a"], 4)
                    pe.wait_ge(m1["v_d"], 3)
                    for r in range(2):
                        pe.wait_ge(m1["rs"], r + 1)
                        for s in range(2):
                            last = nc.tensor.matmul(PS[:, (6, 0)[r] + s, 0:HT], PERM[:], TF[:, r, s * HT:(s + 1) * HT],
                                                    start=True, stop=True)
                        last.then_inc(m1["perm_q"], 1)
            pe.wait_ge(m1["qr"], 2)
            pe.wait_ge(m1["q_a"], 4)
            pe.wait_ge(m1["q_d"], 4)
            for t, (c, n) in enumerate(FRAMES):
                last = nc.tensor.transpose(PS[0:n, 4, t * ROPE:(t + 1) * ROPE], KR[:, c:c + n], IDENT[0:ROPE, 0:ROPE])
            last.then_inc(m1["kr_T"], 1)
            with pe.Fori(0, 2) as i:
                for t in range(4):
                    weights_ready(pe, i * 4 + (B_VO + t))
                    pe.wait_ge(m1["proj"], i * 4 + (13 + t))
                    for k in range(KD):
                        last = product(B_VO + t, k, H_HI[:, k], H_LO[:, k], 2 * (t % 2), k == 0, k == KD - 1)
                    last.then_inc(w_used, 1)
        def mix1_act(act):
            act.wait_ge(m1["cache_T"], 1)
            nc.scalar.activation(C_HI[:, :, T:TK], PS[:, 6, :].rearrange("p (k t) -> p k t", k=KC),
                                 ACT.Copy).then_inc(m1["cache_hi"], 1)
            nc.scalar.activation(KR[:, T:TK], PS[0:ROPE, 7, 0:PAST], ACT.Copy).then_inc(m1["kr_c"], 1)
            pre_root_act(act, pre[1])
            for i in range(KQ + KC):
                split_hi(act, B_AQ + i + 2)
                act.wait_ge(m1["proj"], i + 1)
                raw = AQRAW[:, i] if i < KQ else CRAW[:, i - KQ, 0:T]
                sq = (PAIR[:, 0], PAIR[:, 1], ACC[:], TF[:, 0], TF[:, 1])[i]
                nc.scalar.activation(sq, raw, ACT.Square).then_inc(m1["sq"], 1)
            act.wait_ge(m1["aq_sum"], 1)
            frame_roots(2, QL).then_inc(m1["aq_root"], 1)
            split_hi(act, B_SMALL + 2)
            act.wait_ge(m1["c_sum"], 1)
            act.wait_ge(m1["aq_inv"], 1)
            frame_roots(6, KVL).then_inc(m1["c_root"], 1)
            act.wait_ge(m1["lf1"], 1)
            settle(act, "act", act_step, nc.scalar.activation(GR[:], LF[:], ACT.Abs))
            settle(act, "act", act_step, nc.scalar.activation(GR[:], GR[:], ACT.Exp, scale=-1.0))
            nc.scalar.activation(GR[:], GR[:], ACT.Ln, bias=1.0).then_inc(m1["soft"], 1)
            for n in range(2 * MH):
                split_hi(act, B_QK + n + 2)
                if n == 4:
                    act.wait_ge(m1["c_T"], 1)
                    nc.scalar.activation(CSTAGE[:, 0:4], PS[:, 6:8, :].rearrange("p b (t c) -> p (b t) c", t=2), ACT.Copy)
                    nc.scalar.activation(CSTAGE[0:DEC, 4], PS[0:DEC, 4, 0:KVL], ACT.Copy).then_inc(m1["c_staged"], 1)
                if n == 6:
                    act.wait_ge(m1["mm"], 1)
                    nc.scalar.activation(EM[:], MX[:], ACT.Exp, scale=-1.0).then_inc(m1["em"], 1)
            act.wait_ge(m1["c_stored"], 32)
            for n in range(AH // 2):
                act.wait_ge(w_used if n == 3 else m1["kn_T"], B_UKV + 1 if n == 3 else n + 1)
                nc.scalar.activation(halves(KH[0:NOPE, 2 * n], TK // 2), pair(4 - 2 * (n % 2), NOPE, TK // 2),
                                     ACT.Copy).then_inc(m1["kn_a"], 1)
            split_hi(act, B_UKV + 2, 6)
            act.wait_ge(m1["gate_T"], 1)
            nc.scalar.activation(GC[:, 0:4], PS[:, 7, 0:16].rearrange("p (t h) -> p t h", h=MH), ACT.Copy)
            nc.scalar.activation(GC[0:DEC, 4], PS[0:DEC, 7, 16:20], ACT.Copy)
            nc.scalar.activation(EMC[:, 0:4], PS[:, 7, 20:36].rearrange("p (t h) -> p t h", h=MH), ACT.Copy)
            nc.scalar.activation(EMC[0:DEC, 4], PS[0:DEC, 7, 36:40], ACT.Copy).then_inc(m1["gate_c"], 1)
            for s in range(0, 7, 2):
                n = KEY_TILES[s][1]
                act.wait_ge(w_used if s == 6 else m1["v_T"], B_UKV + 2 if s == 6 else s + 1)
                nc.scalar.activation(VA[0:n, s, 0:AH * AV], PS[0:n, (0, 1, 6, 7)[s % 4], :], ACT.Copy).then_inc(m1["v_a"], 1)
            split_hi(act, B_UKV + 3, 6)
            for r in range(2):
                act.wait_ge(w_used if r else m1["q_T"], B_UQ + 1 if r else 1)
                nc.scalar.activation(halves(TF[:, r]), pair(4 - 2 * r), ACT.Copy).then_inc(m1["rs"], 1)
            split_hi(act, B_UQ + 2, 6)
            for n in range(4):
                act.wait_ge(w_used if n % 2 else m1["q_T"], B_UQ + n // 2 + 2 if n % 2 else n // 2 + 2)
                nc.scalar.activation(halves(QH[0:NOPE, 2 * n]), pair(4 - 2 * (n % 2), NOPE), ACT.Copy,
                                     scale=A_SCALE).then_inc(m1["q_a"], 1)
                if n % 2:
                    split_hi(act, B_UQ + n // 2 + 3)
            for n in range(2 * MH):
                split_hi(act, B_VO + n + 2)
                if n == 1:
                    act.wait_ge(m1["kr_T"], 1)
                    act.wait_ge(m1["qr"], 2)
                    nc.scalar.activation(KSTAGE[:, 0:4], PS[:, 4, 0:4 * ROPE].rearrange("p (t c) -> p t c", c=ROPE), ACT.Copy)
                    nc.scalar.activation(KSTAGE[0:DEC, 4], PS[0:DEC, 4, 4 * ROPE:5 * ROPE], ACT.Copy).then_inc(m1["kr_staged"], 1)
                if n >= MH:
                    act.wait_ge(m1["proj"], 15 + n)
                    nc.scalar.activation(PJ2[:, n], PJ2[:, n], ACT.Sigmoid).then_inc(m2["sig"], 1)

        def mix1_dve(dve):
            dve.wait_ge(m1["cache_hi"], 1)
            nc.vector.tensor_tensor(C_LO[:, :, T:TK], PS[:, 6, :].rearrange("p (k t) -> p k t", k=KC),
                                    C_HI[:, :, T:TK].bitcast(F32), ALU.subtract).then_inc(m1["cache_lo"], 1)
            pre_dve(dve, pre[1])

            def evacuate(dst, src, count, scale=None):
                dve.wait_ge(w_used, count)
                return scaled(dst, src, scale)

            def scaled(dst, src, scale=None, factor=RB[:]):
                if scale is None:
                    return nc.vector.tensor_tensor(halves(dst), src, halves(factor), ALU.mult)
                return nc.vector.scalar_tensor_tensor(out=halves(dst), in0=src, scalar=scale, in1=halves(factor),
                                                      op0=ALU.mult, op1=ALU.mult)

            def inverse(root, inv):
                dve.wait_ge(m1[root], 1)
                nc.vector.reciprocal(INV[:], ROOT[:]).then_inc(m1[inv], 1)

            def normed(raw, bank, gain, n, done):
                for i in range(n):
                    g = GROW[gain] + i
                    nc.vector.scalar_tensor_tensor(out=raw(i), in0=raw(i), scalar=GCOLS[:, g:g + 1], in1=spread_at(bank),
                                                   op0=ALU.mult, op1=ALU.mult).then_inc(done, 1)

            def qk(n):
                evacuate(PJ1[:, n], pair(2 * (n % 2)), B_QK + n + 1, None if n < MH else P ** -0.5).then_inc(m1["proj"], 1)
                split_lo(dve, B_QK + n + 2)

            split_lo(dve, B_AQ + 2)
            pre_factor_dve(dve, pre[1])
            for i in range(KQ + KC):
                dst = AQRAW[:, i] if i < KQ else CRAW[:, i - KQ, 0:T]
                evacuate(dst, pair((0, 2, 4, 6, 0)[i]), B_AQ + i + 1).then_inc(m1["proj"], 1)
                if i:
                    split_lo(dve, B_AQ + i + 2)
            inverse("aq_root", "aq_inv")
            dve.wait_ge(w_used, B_SMALL + 1)
            for row, dst, n in ((0, ARS, ROPE), (32, IG, MH), (64, LF, MH)):
                last = scaled(dst[:], PS[row:row + n, 4:6, 0:HT], factor=RB[row:row + n, :])
            last.then_inc(m1["proj"], 1)
            split_lo(dve, B_SMALL + 2)
            dve.wait_ge(m1["aq_spread"], 1)
            normed(lambda i: AQRAW[:, i], 2, "q_a_g", KQ, m1["cq"])
            inverse("c_root", "c_inv")
            qk(0)
            dve.wait_ge(m1["c_spread"], 1)
            normed(lambda i: CRAW[:, i, 0:T], 6, "kv_a_g", KC, m1["c"])
            qk(1)
            dve.wait_ge(m1["perm"], 1)
            dve.wait_ge(trig_in, 16)
            settle(dve, "dve", dve_step, nc.vector.tensor_tensor(PAIR[0:ROPE, 1], ARS[:], TRIG[0:ROPE, 0], ALU.mult))
            settle(dve, "dve", dve_step, nc.vector.tensor_tensor(
                halves(KR[:, 0:T]), pair(4, ROPE), halves(TRIG[0:ROPE, 1]), ALU.mult))
            nc.vector.tensor_tensor(KR[:, 0:T], KR[:, 0:T], PAIR[0:ROPE, 1], ALU.add).then_inc(m1["kr"], 1)
            qk(2)
            dve.wait_ge(m1["lf"], 1)
            dve.wait_ge(m1["cq"], KQ)
            for lo, hi in ((0, SEQ), (SEQ, T)):
                last = nc.vector.tensor_tensor_scan(out=BC[:, lo:hi], data0=ONES4[:, lo:hi], data1=LF[:, lo:hi],
                                                    initial=0.0, op0=ALU.mult, op1=ALU.add)
            settle(dve, "dve", dve_step, last)
            settle(dve, "dve", dve_step, nc.vector.tensor_tensor(GR[:], IG[:], BC[:], ALU.subtract))
            qk(3)
            nc.vector.tensor_tensor_scan(out=MX[:, 0:SEQ], data0=GR[:, 0:SEQ], data1=GR[:, 0:SEQ],
                                         initial=0.0, op0=ALU.max, op1=ALU.max)
            dve.wait_ge(bias_in, 64)
            settle(dve, "dve", dve_step, nc.vector.tensor_tensor_scan(
                out=MX[:, SEQ:T], data0=GR[:, SEQ:T], data1=GR[:, SEQ:T], initial=BIAS[:, 2:3], op0=ALU.max, op1=ALU.max))
            qk(4)
            nc.vector.tensor_scalar(NM[:], MX[:], -1.0, None, ALU.mult)
            settle(dve, "dve", dve_step, nc.vector.tensor_tensor(MX[:], MX[:], BC[:], ALU.add))
            nc.vector.tensor_copy(MEND[:, 0:1], MX[:, SEQ - 1:SEQ])
            nc.vector.tensor_copy(MEND[:, 1:2], MX[:, T - 1:T]).then_inc(m1["mm"], 1)
            for n in range(5, 2 * MH):
                qk(n)
            dve.wait_ge(m1["c_stored"], 32)
            for n in range(AH // 2):
                dve.wait_ge(w_used if n == 3 else m1["kn_T"], B_UKV + 1 if n == 3 else n + 1)
                nc.vector.tensor_copy(halves(KH[0:NOPE, 2 * n + 1], TK // 2),
                                      PS[NOPE:P, 4 - 2 * (n % 2):6 - 2 * (n % 2), 0:TK // 2]).then_inc(m1["kn_d"], 1)
            split_lo(dve, B_UKV + 2, 6)
            dve.wait_ge(m1["gate_T"], 1)
            nc.vector.memset(VA[:, :, AH * AV:VAW], 0.0)
            for s in range(1, 7, 2):
                n = KEY_TILES[s][1]
                dve.wait_ge(m1["v_T"], s + 1)
                nc.vector.tensor_copy(VA[0:n, s, 0:AH * AV], PS[0:n, (0, 1, 6, 7)[s % 4], :]).then_inc(m1["v_d"], 1)
            split_lo(dve, B_UKV + 3, 6)
            for n in range(4):
                if n == 0:
                    split_lo(dve, B_UQ + 2, 6)
                dve.wait_ge(w_used if n % 2 else m1["q_T"], B_UQ + n // 2 + 2 if n % 2 else n // 2 + 2)
                nc.vector.tensor_scalar(halves(QH[0:NOPE, 2 * n + 1]), PS[NOPE:P, 4 - 2 * (n % 2):6 - 2 * (n % 2), 0:HT],
                                        A_SCALE, None, ALU.mult).then_inc(m1["q_d"], 1)
                if n % 2:
                    split_lo(dve, B_UQ + n // 2 + 3)
                if n == 0:
                    for r in range(2):
                        dve.wait_ge(m1["rs"], r + 1)
                        settle(dve, "dve", dve_step, nc.vector.tensor_tensor(PAIR[:, r], TF[:, r], TRIG[:, 0], ALU.mult))
                        dve.wait_ge(m1["perm_q"], r + 1)
                        settle(dve, "dve", dve_step, nc.vector.tensor_tensor(
                            halves(TF[:, r]), pair((6, 0)[r]), halves(TRIG[:, 1]), ALU.mult))
                        nc.vector.tensor_tensor(PAIR[:, r], PAIR[:, r], TF[:, r], ALU.add).then_inc(m1["qr"], 1)
            with dve.Fori(0, 2) as i:
                for t in range(4):
                    dve.wait_ge(w_used, i * 4 + (B_VO + t + 1))
                    nc.vector.tensor_tensor(halves(PJ2[:, bass.ds(i * 4 + t, 1), :].rearrange("p a t -> p (a t)")),
                                            pair(2 * (t % 2)), halves(RB[:]), ALU.mult).then_inc(m1["proj"], 1)
                    split_lo(dve, B_VO + t + 2, 8, i * 4 + (B_VO + t + 2))

        def cache_pool(pool):
            pool.wait_ge(w_used, MIX0)
            pool.dma_start(CIN[:], a["cache_kv_latent"][0, 0].rearrange("(t p) c -> p t c", p=P)).then_inc(cache_in, 16)
            pool.dma_start(KIN[:], a["cache_k_rope"][0, 0].rearrange("(t p) c -> p t c", p=P)).then_inc(cache_in, 16)

        def mix1_pool(pool):
            def split(src, hi, lo, done):
                settle(pool, "pool", pool_step, nc.gpsimd.tensor_copy(hi, src))
                nc.gpsimd.tensor_tensor(lo, src, hi.bitcast(F32), ALU.subtract).then_inc(done, 1)

            pool.wait_ge(m1["proj"], 6)
            pool.wait_ge(bias_in, 64)
            settle(pool, "pool", pool_step, nc.gpsimd.tensor_scalar(IG[:], IG[:], BIAS[:, 0:1], None, ALU.add))
            nc.gpsimd.memset(ONES4[:], 1.0)
            nc.gpsimd.tensor_scalar(LF[:], LF[:], BIAS[:, 1:2], None, ALU.add).then_inc(m1["lf1"], 1)
            pool.wait_ge(m1["soft"], 1)
            settle(pool, "pool", pool_step, nc.gpsimd.tensor_scalar(LF[:], LF[:], 0.0, None, ALU.min))
            nc.gpsimd.tensor_tensor(LF[:], LF[:], GR[:], ALU.subtract).then_inc(m1["lf"], 1)
            for i in range(KQ):
                pool.wait_ge(m1["cq"], i + 1)
                split(AQRAW[:, i], CQ_HI[:, i], CQ_LO[:, i], m1["cq_lo"])
            for i in range(KC):
                pool.wait_ge(m1["c"], i + 1)
                split(CRAW[:, i, 0:T], C_HI[:, i, 0:T], C_LO[:, i, 0:T], m1["c_lo"])
            pool.wait_ge(m1["c_staged"], 1)
            pool.dma_start(p_kv[0, 0].rearrange("(t p) c -> p t c", p=P), CSTAGE[:, 0:4]).then_inc(m1["c_stored"], 16)
            pool.dma_start(s_kv[0, 0], CSTAGE[0:DEC, 4]).then_inc(m1["c_stored"], 16)
            pool.wait_ge(m1["mm"], 1)
            pool.dma_start(p_m[0].rearrange("b h -> h b"), MEND[:, 0:1]).then_inc(st["stored"], 16)
            pool.dma_start(s_m[0].rearrange("b h -> h b"), MEND[:, 1:2]).then_inc(st["stored"], 16)
            pool.wait_ge(m1["c_stored"], 32)
            pool.wait_ge(m1["kr"], 1)
            pool.wait_ge(m1["c_lo"], KC)
            for h in range(AH):
                settle(pool, "pool", pool_step, nc.gpsimd.tensor_copy(KH[NOPE:QK, h], KR[:]))
            for h in range(AH):
                if h % 4 == 0:
                    pool.wait_ge(m1["qr"], h // 4 + 1)
                settle(pool, "pool", pool_step, nc.gpsimd.tensor_scalar(
                    QH[NOPE:QK, h], PAIR[(h % 4) * ROPE:(h % 4 + 1) * ROPE, h // 4], A_SCALE, None, ALU.mult))
            pool.sem_inc(m1["rope_in"], 1)
            pool.wait_ge(m1["kr_staged"], 1)
            pool.dma_start(p_kr[0, 0].rearrange("(t p) c -> p t c", p=P), KSTAGE[:, 0:4]).then_inc(st["stored"], 16)
            pool.dma_start(s_kr[0, 0], KSTAGE[0:DEC, 4]).then_inc(st["stored"], 16)

        m2 = names("m2", "v_T", "k_T", "v_c", "k_c", "c0_T", "c0_c", "ones_v", "nb_T", "nb", "we", "s_T", "arg", "dexp",
                   "tri", "wgt", "o_T", "os", "sq", "var", "root", "hn", "h_T", "mf", "hi", "lo", "vw", "qw", "st_T",
                   "st_c", "st_v", "sig", "state_out")
        DOFF = {0: 0, 1: 512, 3: 896, 2: 1024, 4: 1280}
        DLEN = {i: SEQ - i * P for i in range(4)}
        DLEN[4] = DEC

        def carry(h):
            return PAIR[:, 1, h * DEC:(h + 1) * DEC]

        def carried_q(h):
            return PAIR[:, 1, (MH + h) * DEC:(MH + h + 1) * DEC]

        def nb_of(h):
            return (RB[:], PAIR[:, 0], PJ2[:, 2], PJ2[:, 3])[h]

        def mlstm_back(pe, h):
            pe.wait_ge(m2["hn"], h + 1)
            if h:
                pe.wait_ge(m2["mf"], h)
            else:
                pe.wait_ge(m2["nb"], MH)
            for t, (c, n) in enumerate(FRAMES):
                last = nc.tensor.transpose(PSF[:, 3 * 512 + c:3 * 512 + c + n], HN[0:n, t, :], IDENT[0:n, 0:n])
            last.then_inc(m2["h_T"], 1)

        def mix2_pe(pe):
            def values_T(t, bank):
                c, n = FRAMES[t]
                for h in range(MH):
                    last = nc.tensor.transpose(PS[0:n, bank, h * P:(h + 1) * P], PJ2[:, h, c:c + n], IDENT[:])
                last.then_inc(m2["v_T"], 1)

            def keys_T(t, bank):
                c, n = FRAMES[t]
                for h in range(MH):
                    last = nc.tensor.transpose(PS[0:n, bank, h * P:(h + 1) * P], PJ1[:, MH + h, c:c + n], IDENT[:])
                last.then_inc(m2["k_T"], 1)

            def maxima(h):
                for s in range(2):
                    last = nc.tensor.matmul(PS[:, 3 + s, 0:HT], SEL[:, h, :], NM[:, s * HT:(s + 1) * HT], start=True, stop=True)
                last.then_inc(m2["nb_T"], 1)

            def scores(h):
                if h:
                    pe.wait_ge(m2["wgt"], 2 * h)
                for i, (c, n) in enumerate(FRAMES):
                    last = nc.tensor.matmul(PSF[0:n, DOFF[i]:DOFF[i] + DLEN[i]], PJ1[:, MH + h, c:c + n],
                                            PJ1[:, h, c:(SEQ if i < 4 else T)], start=True, stop=True)
                last.then_inc(m2["s_T"], 1)

            def outputs(h):
                pe.wait_ge(m2["wgt"], 2 * h + 2)
                pe.wait_ge(m2["ones_v"], 1)
                if h:
                    pe.wait_ge(m2["os"], h)
                for j in range(4):
                    dst = PS[:, 5 + j // 3, (j % 3) * VP:(j % 3 + 1) * VP]
                    for i in range(j + 1):
                        nc.tensor.matmul(dst, DW[:, DOFF[i] + (j - i) * P:DOFF[i] + (j - i + 1) * P], VT[:, i, h, :],
                                         start=i == 0, stop=i == j)
                if h:
                    mlstm_back(pe, h - 1)
                dst = PS[0:DEC, 6, VP:2 * VP]
                nc.tensor.matmul(dst, DW[0:DEC, DOFF[4]:DOFF[4] + DEC], VT[0:DEC, 4, h, :], start=True, stop=False)
                pe.wait_ge(m2["qw"], h + 1)
                nc.tensor.matmul(dst, carried_q(h), C0T[:, h, :], start=False, stop=True).then_inc(m2["o_T"], 1)

            def states(h):
                pe.wait_ge(m2["vw"], h + 1)
                if h:
                    pe.wait_ge(m2["st_c"], h)
                    pe.wait_ge(m2["st_v"], h)
                for i in range(4):
                    nc.tensor.matmul(PS[:, 7, 0:P], VW[:, i, :], KT[:, i, h, :], start=i == 0, stop=i == 3)
                nc.tensor.matmul(PS[:, 7, P:2 * P], VW[0:DEC, 4, :], KT[0:DEC, 4, h, :], start=True, stop=True)
                for i in range(4):
                    nc.tensor.matmul(PS[0:1, 7, 2 * P:3 * P], WE[:, h, i:i + 1], KT[:, i, h, :], start=i == 0, stop=i == 3)
                nc.tensor.matmul(PS[0:1, 7, 3 * P:4 * P], WE[0:DEC, h, 4:5], KT[0:DEC, 4, h, :],
                                 start=True, stop=True).then_inc(m2["st_T"], 1)

            pe.wait_ge(m1["kr_staged"], 1)
            pe.wait_ge(m1["proj"], 22)
            maxima(0)
            scores(0)
            for t in range(3):
                values_T(t, 5 + t)
            pe.wait_ge(m2["nb"], 1)
            maxima(1)
            for t in range(3):
                pe.wait_ge(m2["v_c"], t + 1)
                keys_T(t, 5 + t)
            for t in range(3, TT):
                pe.wait_ge(m2["k_c"], t - 2)
                values_T(t, 2 + t)
            pe.wait_ge(state_in, 48)
            pe.wait_ge(m2["k_c"], 3)
            for h in range(MH):
                last = nc.tensor.transpose(PS[:, 7, h * P:(h + 1) * P], C0[:, h, :], IDENT[:])
            last.then_inc(m2["c0_T"], 1)
            for t in range(3, TT):
                pe.wait_ge(m2["v_c"], t + 1)
                keys_T(t, 2 + t)
            pe.wait_ge(m2["nb"], 2)
            nc.tensor.transpose(PS[:, 3, HT:HT + MH], N0R[:], IDENT[0:MH, 0:MH])
            maxima(2)
            pe.wait_ge(m2["c0_c"], 1)
            pe.wait_ge(m2["k_c"], TT)
            for h in range(MH):
                outputs(h)
                if h + 1 < MH:
                    scores(h + 1)
                if h == 0:
                    pe.wait_ge(m2["nb"], 3)
                    maxima(3)
                states(h)

        def mix2_act(act):
            def copy_values(t):
                act.wait_ge(m2["v_T"], t + 1)
                n = FRAMES[t][1]
                bank = 5 + t if t < 3 else 2 + t
                nc.scalar.activation(VT[0:n, t, :, 0:P], PS[0:n, bank, :].rearrange("p (h v) -> p h v", h=MH),
                                     ACT.Copy).then_inc(m2["v_c"], 1)

            def prepare(h):
                nb = nb_of(h)
                act.wait_ge(m2["nb_T"], h + 1)
                settle(act, "act", act_step, nc.scalar.activation(halves(nb), pair(3), ACT.Copy))
                if h == 0:
                    act.wait_ge(m1["rope_in"], 1)
                nc.scalar.activation(carry(h), nb[:, SEQ:T], ACT.Exp, bias=M0B[:, h:h + 1]).then_inc(m2["nb"], 1)
                nc.scalar.activation(WE[:, h, 0:4], GC[:, 0:4, h], ACT.Exp, bias=nb[:, SEQ - 1:SEQ])
                nc.scalar.activation(WE[0:DEC, h, 4:5], GC[0:DEC, 4, h:h + 1], ACT.Exp,
                                     bias=nb[0:DEC, T - 1:T]).then_inc(m2["we"], 1)

            def exponentials(h):
                act.wait_ge(m2["arg"], 2 * h + 1)
                nc.scalar.activation(DW[:, 0:SEQ], DW[:, 0:SEQ], ACT.Exp).then_inc(m2["dexp"], 1)
                act.wait_ge(m2["arg"], 2 * h + 2)
                nc.scalar.activation(DW[:, SEQ:1280], DW[:, SEQ:1280], ACT.Exp)
                nc.scalar.activation(DW[0:DEC, 1280:1344], DW[0:DEC, 1280:1344], ACT.Exp).then_inc(m2["dexp"], 1)

            nc.scalar.activation(WARM[:], EPSC[:], ACT.Exp)
            prepare(0)
            copy_values(0)
            copy_values(1)
            exponentials(0)
            copy_values(2)
            prepare(1)
            copy_values(3)
            copy_values(4)
            act.wait_ge(m2["c0_T"], 1)
            nc.scalar.activation(C0T[:, :, 0:P], PS[:, 7, :].rearrange("p (h v) -> p h v", h=MH), ACT.Copy)
            act.wait_ge(m2["nb_T"], 3)
            for i in range(2):
                last = nc.scalar.activation(C0T[:, :, P + i], PS[:, 3, HT:HT + MH], ACT.Copy)
            last.then_inc(m2["c0_c"], 1)
            prepare(2)
            for h in range(MH):
                act.wait_ge(m2["o_T"], h + 1)
                if h:
                    act.wait_ge(m2["hn"], h)
                nc.scalar.activation(OS[:, 0:3], PS[:, 5, 0:3 * VP].rearrange("p (t v) -> p t v", t=3), ACT.Copy)
                nc.scalar.activation(OS[:, 3], PS[:, 6, 0:VP], ACT.Copy)
                settle(act, "act", act_step, nc.scalar.activation(OS[0:DEC, 4], PS[0:DEC, 6, VP:2 * VP], ACT.Copy))
                act.sem_inc(m2["os"], 1)
                if h:
                    act.wait_ge(m2["h_T"], h)
                nc.scalar.activation(HN[:], OS[:, :, 0:P], ACT.Square).then_inc(m2["sq"], 1)
                if h + 1 < MH:
                    exponentials(h + 1)
                if h == 0:
                    prepare(MH - 1)
                act.wait_ge(m2["var"], h + 1)
                nc.scalar.activation(S5[:, 3], S5[:, 2], ACT.Sqrt, bias=EPSC[:], scale=1.0 / P).then_inc(m2["root"], 1)
                act.wait_ge(m2["st_T"], h + 1)
                if h >= 2:
                    act.wait_ge(m2["state_out"], 64 * (h - 1))
                nc.scalar.activation(CN[:, h % 2, 0], PS[:, 7, 0:P], ACT.Copy)
                if h:
                    act.wait_ge(m2["state_out"], 64 * h)
                nc.scalar.activation(NN[:, 0], PS[0:1, 7, 2 * P:3 * P], ACT.Copy).then_inc(m2["st_c"], 1)
                nc.scalar.activation(WARM[:], EPSC[:], ACT.Exp)
                act.wait_ge(m2["mf"], h + 1)
                nc.scalar.activation(MA_HI[:, h], TF[:, h % 2], ACT.Copy).then_inc(m2["hi"], 1)

        def mix2_dve(dve):
            def copy_keys(t):
                dve.wait_ge(m2["k_T"], t + 1)
                n = FRAMES[t][1]
                bank = 5 + t if t < 3 else 2 + t
                nc.vector.tensor_copy(KT[0:n, t], PS[0:n, bank, :].rearrange("p (h v) -> p h v", h=MH)).then_inc(m2["k_c"], 1)

            def args(h):
                nb = nb_of(h)
                dve.wait_ge(m2["nb"], h + 1)
                if h:
                    dve.wait_ge(m2["o_T"], h)
                    dve.wait_ge(m2["wgt"], 2 * h)
                nc.vector.tensor_tensor(carried_q(h), PJ1[:, h, SEQ:T], carry(h), ALU.mult).then_inc(m2["qw"], 1)
                for i, (c, n) in enumerate(FRAMES):
                    end = SEQ if i < 4 else T
                    last = nc.vector.tensor_scalar(DW[0:n, DOFF[i]:DOFF[i] + DLEN[i]], nb[0:n, c:end],
                                                   GC[0:n, i, h:h + 1], 0.0, ALU.add, ALU.min)
                    if i in (0, TT - 1):
                        last.then_inc(m2["arg"], 1)

            def weights(h):
                dve.wait_ge(m2["s_T"], h + 1)
                dve.wait_ge(m2["tri"], 2 * h + 1)
                nc.vector.tensor_tensor(DW[:, 0:SEQ], DW[:, 0:SEQ], PSF[:, 0:SEQ], ALU.mult).then_inc(m2["wgt"], 1)
                dve.wait_ge(m2["tri"], 2 * h + 2)
                nc.vector.tensor_tensor(DW[:, SEQ:1280], DW[:, SEQ:1280], PSF[:, SEQ:1280], ALU.mult)
                nc.vector.tensor_tensor(DW[0:DEC, 1280:1344], DW[0:DEC, 1280:1344], PSF[0:DEC, 1280:1344],
                                        ALU.mult).then_inc(m2["wgt"], 1)

            args(0)
            copy_keys(0)
            weights(0)
            for t in range(1, TT):
                copy_keys(t)
            dve.wait_ge(m2["ones_v"], 1)
            for h in range(MH):
                if h + 1 < MH:
                    args(h + 1)
                dve.wait_ge(m2["sq"], h + 1)
                den = OS[:, :, P:P + 1].rearrange("p t o -> p (t o)")
                settle(dve, "dve", dve_step, nc.vector.tensor_scalar(S5[:, 0], den, -1.0, None, ALU.mult))
                settle(dve, "dve", dve_step, nc.vector.tensor_tensor(S5[:, 0], S5[:, 0], den, ALU.max))
                settle(dve, "dve", dve_step, nc.vector.tensor_tensor(S5[:, 0], S5[:, 0], EMC[:, :, h], ALU.max))
                settle(dve, "dve", dve_step, nc.vector.reciprocal(S5[:, 1], S5[:, 0]))
                settle(dve, "dve", dve_step, nc.vector.tensor_reduce(S5[:, 2], HN[:], AX, ALU.add))
                settle(dve, "dve", dve_step, nc.vector.tensor_tensor(S5[:, 2], S5[:, 2], S5[:, 1], ALU.mult))
                nc.vector.tensor_tensor(S5[:, 2], S5[:, 2], S5[:, 1], ALU.mult).then_inc(m2["var"], 1)
                if h + 1 < MH:
                    weights(h + 1)
                dve.wait_ge(m2["root"], h + 1)
                settle(dve, "dve", dve_step, nc.vector.reciprocal(S5[:, 4], S5[:, 3]))
                settle(dve, "dve", dve_step, nc.vector.tensor_tensor(S5[:, 4], S5[:, 4], S5[:, 1], ALU.mult))
                nc.vector.tensor_tensor(HN[:], OS[:, :, 0:P], S5[:, 4:5, :].rearrange("p o t -> p t o").to_broadcast([P, TT, P]),
                                        ALU.mult).then_inc(m2["hn"], 1)
                dve.wait_ge(m2["st_c"], h + 1)
                if h >= 2:
                    dve.wait_ge(m2["state_out"], 64 * (h - 1))
                wst = carry(h)[:, DEC - 1:DEC]
                nc.vector.scalar_tensor_tensor(out=CN[:, h % 2, 1], in0=C0[:, h, :], scalar=wst, in1=PS[:, 7, P:2 * P],
                                               op0=ALU.mult, op1=ALU.add)
                if h:
                    dve.wait_ge(m2["state_out"], 64 * h)
                nc.vector.scalar_tensor_tensor(out=NN[:, 1], in0=N0[:, h, :], scalar=wst[0:1], in1=PS[0:1, 7, 3 * P:4 * P],
                                               op0=ALU.mult, op1=ALU.add).then_inc(m2["st_v"], 1)
                dve.wait_ge(m2["h_T"], h + 1)
                dve.wait_ge(m2["sig"], h + 1)
                if h >= 2:
                    dve.wait_ge(m2["lo"], h - 1)
                g = GROW["m_head_g"] + h
                nc.vector.scalar_tensor_tensor(out=TF[:, h % 2], in0=PSF[:, 3 * 512:3 * 512 + T], scalar=GCOLS[:, g:g + 1],
                                               in1=PJ2[:, MH + h], op0=ALU.mult, op1=ALU.mult).then_inc(m2["mf"], 1)

        def mix2_pool(pool):
            pool.wait_ge(w_used, B_OUT)
            pool.dma_start(C0[:], a["state_C"][0, 0].rearrange("h v k -> v h k")).then_inc(state_in, 16)
            pool.dma_start(N0R[:], a["state_n"][0, 0]).then_inc(state_in, 16)
            pool.wait_ge(m1["kr_T"], 1)
            pool.dma_start(N0[:], a["state_n"][0, 0:1]).then_inc(state_in, 16)
            nc.gpsimd.memset(VT[:, :, :, P:VP], 1.0)
            nc.gpsimd.memset(OS[:], 1.0).then_inc(m2["ones_v"], 1)

            def low(h):
                pool.wait_ge(m2["hi"], h + 1)
                nc.gpsimd.tensor_tensor(MA_LO[:, h], TF[:, h % 2], MA_HI[:, h].bitcast(F32), ALU.subtract).then_inc(m2["lo"], 1)

            for h in range(MH):
                for i in range(TT):
                    if i < 2:
                        pool.wait_ge(m2["dexp"], 2 * h + i + 1)
                    n = FRAMES[i][1]
                    blk = DW[0:n, DOFF[i]:DOFF[i] + n]
                    last = nc.gpsimd.affine_select(out=blk, in_=blk, compare_op=ALU.is_ge, fill=0.0, base=0,
                                                   pattern=[[1, n]], channel_multiplier=-1)
                    if i in (0, TT - 1):
                        last.then_inc(m2["tri"], 1)
                pool.wait_ge(m2["we"], h + 1)
                pool.wait_ge(m2["v_c"], TT)
                if h:
                    pool.wait_ge(m2["st_T"], h)
                for i, (c, n) in enumerate(FRAMES):
                    last = nc.gpsimd.tensor_scalar(VW[0:n, i], VT[0:n, i, h, 0:P], WE[0:n, h, i:i + 1], None, ALU.mult)
                last.then_inc(m2["vw"], 1)
                if h:
                    low(h - 1)
            low(MH - 1)

        m3 = names("m3", "s", "max", "p", "p_T", "pt_a", "pt_d", "o", "at", "a_T", "hi", "lo")
        SOFF = {3: 0, 2: 512, 0: 896, 1: 1024, 4: 1536}
        UNITS = ((3,), (2, 0), (1,), (4,))
        POFF = {3: 0, 2: 512, 0: 896, 1: 1024, 4: 1280}
        SLEN = {0: P, 1: 2 * P, 2: 3 * P, 3: 4 * P, 4: DEC + PAST}
        GROUP_A = [(3, i * P, P, i) for i in range(4)]
        GROUP_B = [(2, i * P, P, i) for i in range(3)] + [(0, 0, P, 0)]
        GROUP_C = [(1, 0, P, 0), (1, P, P, 1), (4, DEC, P, 5), (4, DEC + P, P, 6), (4, 0, DEC, 4)]

        def rows_of(j):
            return DEC if j == 4 else P

        def columns(group, base):
            out, at_ = [], base
            for blk in group:
                out.append((*blk, at_))
                at_ += rows_of(blk[0])
            return out

        BLOCKS = [columns(GROUP_A, 0), columns(GROUP_B, 512), columns(GROUP_C, 1024)]

        def mix3_pe(pe):
            pe.wait_ge(m2["wgt"], 2 * MH)
            pe.wait_ge(m1["rope_in"], 1)

            def scores(h):
                for u, tiles in enumerate(UNITS):
                    if h == 0 and u == 3:
                        mlstm_back(pe, MH - 1)
                        pe.wait_ge(m2["mf"], MH)
                    if h:
                        pe.wait_ge(m3["p"], 4 * (h - 1) + u + 1)
                    for j in tiles:
                        n = rows_of(j)
                        k0 = SEQ if j == 4 else 0
                        last = nc.tensor.matmul(PSF[0:n, SOFF[j]:SOFF[j] + SLEN[j]], QH[:, h, j * P:j * P + n],
                                                KH[:, h, k0:k0 + SLEN[j]], start=True, stop=True)
                    last.then_inc(m3["s"], 1)

            def turn(h):
                for g, bank in enumerate((4, 5, 7)):
                    pe.wait_ge(m3["p"], 4 * h + (1, 2, 4)[g])
                    if h:
                        pe.wait_ge(*((m3["pt_d"], 2 * h - 1), (m3["pt_a"], h), (m3["pt_d"], 2 * h))[g])
                    if g == 0 and h >= 3 and h % 2:
                        pe.wait_ge(m3["lo"], h // 2)
                    at_ = 0
                    for j, k0, kn, _, _ in BLOCKS[g]:
                        n = rows_of(j)
                        last = nc.tensor.transpose(PS[0:kn, bank, at_:at_ + n], PR[0:n, h % 2, POFF[j] + k0:POFF[j] + k0 + kn],
                                                   IDENT[0:n, 0:n])
                        at_ += n
                    last.then_inc(m3["p_T"], 1)

            def values(h):
                pe.wait_ge(m3["pt_d"], 2 * h + 2)
                pe.wait_ge(m3["pt_a"], h + 1)
                if h:
                    pe.wait_ge(m3["at"], h)
                for j in range(TT):
                    blks = [b for g in BLOCKS for b in g if b[0] == j]
                    n = rows_of(j)
                    for i, (_, _, kn, kt, col) in enumerate(blks):
                        last = nc.tensor.matmul(PS[0:n, 6, 96 * j:96 * (j + 1)], PT[0:kn, h % 2, col:col + n],
                                                VA[0:kn, kt, AV * h:AV * h + 96], start=i == 0, stop=i == len(blks) - 1)
                last.then_inc(m3["o"], 1)

            def merge(c):
                pe.wait_ge(m3["at"], 2 * c + 2)
                for t, (f, n) in enumerate(FRAMES):
                    if t == 0:
                        pe.wait_ge(m3["pt_d"], 2 * min(2 * c + 2, AH - 1) + 2)
                        pe.wait_ge(m3["pt_a"], min(2 * c + 2, AH - 1) + 1)
                    last = nc.tensor.transpose(PSF[:, 4 * 512 + f:4 * 512 + f + n], AT[0:n, t, :], IDENT[0:n, 0:n])
                last.then_inc(m3["a_T"], 1)

            scores(0)
            for h in range(AH):
                turn(h)
                if h + 1 < AH:
                    scores(h + 1)
                if h and h % 2 == 0:
                    merge(h // 2 - 1)
                values(h)
            merge(AH // 2 - 1)

        def mix3_dve(dve):
            def softmax_max(h):
                for u, tiles in enumerate(UNITS):
                    dve.wait_ge(m3["s"], 4 * h + u + 1)
                    if u < 3:
                        for j in tiles:
                            c = SOFF[j] + SLEN[j]
                            last = nc.vector.memset(PSF[0:DEC, c - DEC:c], MASKED)
                        settle(dve, "dve", dve_step, last)
                    for j in tiles:
                        n = rows_of(j)
                        last = nc.vector.tensor_reduce(S5[0:n, h % 2, j:j + 1], PSF[0:n, SOFF[j]:SOFF[j] + SLEN[j]], AX,
                                                       ALU.max, negate=True)
                    last.then_inc(m3["max"], 1)

            def turned(h, first):
                if h >= 2:
                    dve.wait_ge(m3["o"], h - 1)
                if first:
                    dve.wait_ge(m3["p_T"], 3 * h + 1)
                    nc.vector.tensor_copy(PT[:, h % 2, 0:512], PS[:, 4, :]).then_inc(m3["pt_d"], 1)
                else:
                    dve.wait_ge(m3["p_T"], 3 * h + 3)
                    nc.vector.tensor_copy(PT[:, h % 2, 1024:1408], PS[:, 7, 0:384])
                    nc.vector.tensor_copy(PT[0:DEC, h % 2, 1408:1472], PS[0:DEC, 7, 384:448]).then_inc(m3["pt_d"], 1)

            softmax_max(0)
            for h in range(AH):
                turned(h, True)
                turned(h, False)
                if h + 1 < AH:
                    softmax_max(h + 1)
                if h and h % 2 == 0:
                    low(dve, h // 2 - 1)
                dve.wait_ge(m3["o"], h + 1)
                settle(dve, "dve", dve_step, nc.vector.reciprocal(S5[:, 4], S5[:, 2 + h % 2]))
                if h >= 2 and h % 2 == 0:
                    dve.wait_ge(m3["a_T"], h // 2)
                o_ = PS[:, 6, 0:480].rearrange("p (t v) -> p t v", v=96)[:, :, 0:AV]
                r_ = S5[:, 4:5, :].rearrange("p o t -> p t o")
                c = AV * (h % 2)
                nc.vector.tensor_tensor(AT[:, 0:4, c:c + AV], o_[:, 0:4], r_[:, 0:4].to_broadcast([P, 4, AV]), ALU.mult)
                nc.vector.tensor_tensor(AT[0:DEC, 4:5, c:c + AV], o_[0:DEC, 4:5], r_[0:DEC, 4:5].to_broadcast([DEC, 1, AV]),
                                        ALU.mult).then_inc(m3["at"], 1)
            low(dve, AH // 2 - 1)

        def low(dve, c):
            dve.wait_ge(m3["hi"], c + 1)
            nc.vector.tensor_tensor(MB_LO[:, c], PSF[:, 4 * 512:4 * 512 + T], MB_HI[:, c].bitcast(F32),
                                    ALU.subtract).then_inc(m3["lo"], 1)

        def mix3_act(act):
            act.wait_ge(m2["h_T"], MH)
            act.wait_ge(m2["st_T"], MH)
            act.wait_ge(m2["st_v"], MH)

            def exps(h):
                if h >= 2:
                    act.wait_ge(m3["p_T"], 3 * (h - 1))
                    act.wait_ge(m3["at"], h - 1)
                for u, tiles in enumerate(UNITS):
                    act.wait_ge(m3["max"], 4 * h + u + 1)
                    for j in tiles:
                        n = rows_of(j)
                        last = nc.scalar.activation(PR[0:n, h % 2, POFF[j]:POFF[j] + SLEN[j]],
                                                    PSF[0:n, SOFF[j]:SOFF[j] + SLEN[j]], ACT.Exp,
                                                    bias=S5[0:n, h % 2, j:j + 1], accum_out=S5[0:n, 2 + h % 2, j:j + 1])
                    last.then_inc(m3["p"], 1)

            exps(0)
            for h in range(AH):
                act.wait_ge(m3["p_T"], 3 * h + 2)
                if h >= 2:
                    act.wait_ge(m3["o"], h - 1)
                nc.scalar.activation(PT[:, h % 2, 512:1024], PS[:, 5, :], ACT.Copy).then_inc(m3["pt_a"], 1)
                if h and h % 2 == 0:
                    high(act, h // 2 - 1)
                if h + 1 < AH:
                    exps(h + 1)
            high(act, AH // 2 - 1)

        def high(act, c):
            act.wait_ge(m3["a_T"], c + 1)
            nc.scalar.activation(MB_HI[:, c], PSF[:, 4 * 512:4 * 512 + T], ACT.Copy).then_inc(m3["hi"], 1)

        def out_pe(pe, p):
            pe.wait_ge(m2["lo"], MH)

            def tiles(i, first=False):
                for t in range(4):
                    weights_ready(pe, i * 4 + (B_OUT + t))
                    if not (first and t < 2):
                        pe.wait_ge(p["y_copy"].sem, i * 4 + (t - 1) + p["y_copy"].base)
                    for k in range(KD):
                        if first and t == 0 and k == MH:
                            pe.wait_ge(m3["lo"], AH // 2)
                        hi, lo = (MA_HI[:, k], MA_LO[:, k]) if k < MH else (MB_HI[:, k - MH], MB_LO[:, k - MH])
                        last = product(B_OUT + t, k, hi, lo, 6 - 2 * (t % 2), k == 0, k == KD - 1)
                    last.then_inc(w_used, 1)

            tiles(0, first=True)
            tiles(1)

        def out_act(act, p):
            nc.scalar.activation(WARM[:], EPSC[:], ACT.Sqrt)
            for m in range(KD):
                act.wait_ge(w_used, B_OUT + m + 1)
                y_out(act, p, m, m % 2, 6 - 2 * (m % 2), "mix_post_g", m < 2)
                split_hi(act, B_OUT + m + 2)

        def out_dve(dve):
            for m in range(KD):
                split_lo(dve, B_OUT + m + 2)

        block = ctx.enter_context(nc.Block())

        @block.sync
        def _(sp):
            start_sp(sp)
            load_ffn(sp, 0, a["ff1_w_gate"][0], a["ff1_w_up"][0], a["ff1_w_down"][0], after_first=lambda q: load_x(sp, q + 1))
            load_mix(sp)
            load_ffn(sp, FF2_0, a["ff2_w_gate"][0], a["ff2_w_up"][0], a["ff2_w_down"][0])
            finish_sp(sp)

        @block.gpsimd
        def _(pool):
            start_pool(pool)
            acc_pool(pool, post[0])
            cache_pool(pool)
            post_pool(pool, post[0])
            mix1_pool(pool)
            mix2_pool(pool)
            acc_pool(pool, post[1])
            post_pool(pool, post[1])
            acc_pool(pool, post[2])
            post_pool(pool, post[2])

        @block.scalar
        def _(act):
            load_gains(act, GAINS[:1], g_first_in)
            pre_act(act, pre[0], None, PRE_GAINS[0], split=True)
            pre_root_act(act, pre[0])
            ffn_act(act, ff[0], post[0], 0, "ff1_post_g")
            post_act(act, post[0])
            pre_act(act, pre[1], post[0], PRE_GAINS[1])
            mix1_act(act)
            mix2_act(act)
            mix3_act(act)
            out_act(act, post[1])
            post_act(act, post[1])
            pre_act(act, pre[2], post[1], PRE_GAINS[2])
            pre_root_act(act, pre[2])
            ffn_act(act, ff[1], post[2], FF2_0, "ff2_post_g")
            post_act(act, post[2])
            finish_act(act)

        @block.vector
        def _(dve):
            start_dve(dve)
            pre_dve(dve, pre[0])
            other_gains_dve(dve)
            ffn_dve(dve, ff[0], pre[0], 0)
            post_dve(dve, post[0], pre[1])
            mix1_dve(dve)
            mix2_dve(dve)
            mix3_dve(dve)
            out_dve(dve)
            post_dve(dve, post[1], pre[2])
            pre_dve(dve, pre[2])
            ffn_dve(dve, ff[1], pre[2], FF2_0)
            post_dve(dve, post[2])

        @block.tensor
        def _(pe):
            start_pe(pe)
            ffn_pe(pe, ff[0], pre[0], post[0], 0)
            post_pe(pe, post[0])
            mix1_pe(pe)
            mix2_pe(pe)
            mix3_pe(pe)
            out_pe(pe, post[1])
            post_pe(pe, post[1])
            ffn_pe(pe, ff[1], pre[2], post[2], FF2_0)
            post_pe(pe, post[2])
            finish_pe(pe)


INPUTS = ["x_prompt", "x_sample", "cache_kv_latent", "cache_k_rope", "state_C", "state_n", "state_m",
          "ff1_pre_g", "ff1_w_gate", "ff1_w_up", "ff1_w_down", "ff1_post_g",
          "mix_pre_g", "w_in", "b_igate", "b_fgate", "q_a_g", "w_uq", "kv_a_g", "w_ukv", "m_head_g", "w_out",
          "mix_post_g", "ff2_pre_g", "ff2_w_gate", "ff2_w_up", "ff2_w_down", "ff2_post_g"]
OUTPUTS = [(1, SEQ, D), (1, DEC, D),
           (1, 1, SEQ, KVL), (1, 1, SEQ, ROPE), (1, 1, MH, P, P), (1, 1, MH, P), (1, 1, MH),
           (1, 1, DEC, KVL), (1, 1, DEC, ROPE), (1, 1, MH, P, P), (1, 1, MH, P), (1, 1, MH)]


def kernel(**inputs):
    import numpy as np
    import concourse.bacc as bacc
    from concourse.bass_utils import run_bass_kernel_spmd

    half = ROPE // 2
    pos = np.concatenate([np.arange(SEQ), PAST + np.arange(DEC)]).astype(np.float32)
    freq = (np.float32(10000.0) ** (-np.arange(half, dtype=np.float32) / np.float32(half))).astype(np.float32)
    ang = (freq[:, None] * pos[None, :]).astype(np.float32)
    cos, sin = np.cos(ang), np.sin(ang)
    rope = np.stack([np.concatenate([cos, cos]), np.concatenate([-sin, sin])], axis=1)
    rope = np.ascontiguousarray(np.concatenate([rope] * (P // ROPE)), dtype=np.float32)

    nc = bacc.Bacc("TRN2", target_bir_lowering=False, num_devices=1)
    arrays, aps = {}, {}
    for name in INPUTS:
        x = np.ascontiguousarray(inputs[name])
        arrays[f"in_{name}"] = x
        aps[name] = nc.dram_tensor(f"in_{name}", x.shape, mybir.dt.from_np(x.dtype), kind="ExternalInput").ap()
    arrays["rope_table"] = rope
    table = nc.dram_tensor("rope_table", rope.shape, F32, kind="ExternalInput").ap()
    outs = [nc.dram_tensor(f"out_{i}", s, F32, kind="ExternalOutput").ap() for i, s in enumerate(OUTPUTS)]
    build(nc, aps, table, outs)
    r = run_bass_kernel_spmd(nc, [arrays], core_ids=[0])
    return tuple(r.results[0][f"out_{i}"] for i in range(len(OUTPUTS)))
```
